# Optimizing a Trainium2 kernel written in Bass

```python
import math
import jax, jax.numpy as jnp
from jax import lax
import numpy as np

D_MODEL = 1024
BATCH = 1
SEQ = 1024
DEPTH = 1
DEC_BATCH = 1
DEC_SEQ = 64
PAST_LEN = 512

CHUNK = 64
EPS = 1e-6
GLA_HEADS = 4
GLA_DK = 64
GLA_DV = 128
GLA_RANK = 16
GLA_TAU = 16.0
FOX_HEADS = 8
FOX_DH = 64
MEM_HEADS = 4
MEM_DH = 128
N_MEM = 256
N_BRANCH = 3
BRANCH_W = 512
Q_BLOCK = 128
PEER_HEADS = 8
N_KEYS = 128
N_EXPERTS = N_KEYS * N_KEYS
PEER_TOPK = 16
PEER_DKEY = 256
PEER_DHALF = PEER_DKEY // 2
PEER_TOK_BLOCK = 128

IN_SIZES = (GLA_HEADS * GLA_DK, GLA_HEADS * GLA_DK, GLA_HEADS * GLA_DV, GLA_HEADS * GLA_DV, GLA_RANK,
            FOX_HEADS * FOX_DH, FOX_HEADS * FOX_DH, FOX_HEADS * FOX_DH, FOX_HEADS,
            MEM_HEADS * MEM_DH, N_BRANCH * D_MODEL)
IN_TOTAL = sum(IN_SIZES)

kernel_name = "hybrid_gla_fox_mem_peer_stream_step"

def rmsnorm(x, g):
    xf = x.astype(jnp.float32)
    y = xf * lax.rsqrt(jnp.mean(xf * xf, axis=-1, keepdims=True) + EPS)
    return (y * g.astype(jnp.float32)).astype(x.dtype)

def split_cols(p):
    idx = np.cumsum(IN_SIZES)[:-1].tolist()
    return jnp.split(p, idx, axis=-1)

def gla_recurrence(q, k, v, log_a, s0):
    B, T, H, DK = q.shape
    DV = v.shape[-1]
    L = min(CHUNK, T)
    n = T // L

    def blocks(a):
        return a.reshape(B, n, L, H, a.shape[-1]).transpose(1, 0, 3, 2, 4)

    qc = blocks(q.astype(jnp.float32)) * (DK ** -0.5)
    kc = blocks(k.astype(jnp.float32))
    vc = blocks(v.astype(jnp.float32))
    b = jnp.cumsum(blocks(log_a.astype(jnp.float32)), axis=3)
    b_last = b[:, :, :, -1:, :]
    q_dec = qc * jnp.exp(b)
    k_dec = kc * jnp.exp(-b)
    k_out = kc * jnp.exp(b_last - b)
    causal = jnp.tril(jnp.ones((L, L), dtype=bool))
    att = jnp.where(causal, jnp.einsum('nbhld,nbhmd->nbhlm', q_dec, k_dec), 0.0)
    o_intra = jnp.einsum('nbhlm,nbhme->nbhle', att, vc)

    def step(S, inp):
        qd, ko, vv, dl = inp
        o = jnp.einsum('bhld,bhde->bhle', qd, S)
        S = S * dl[..., 0, :, None] + jnp.einsum('bhld,bhle->bhde', ko, vv)
        return S, o

    s_fin, o_inter = lax.scan(step, s0.astype(jnp.float32), (q_dec, k_out, vc, jnp.exp(b_last)))
    o = (o_intra + o_inter).transpose(1, 0, 3, 2, 4).reshape(B, T, H, DV)
    return o.astype(q.dtype), s_fin

def fox_attention(q, k, v, c_q, c_k):
    B, Tq, H, d = q.shape
    Tk = k.shape[1]
    blk = min(Q_BLOCK, Tq)
    nb = Tq // blk
    q_pos = (Tk - Tq) + jnp.arange(Tq)
    k_pos = jnp.arange(Tk)
    c_kT = c_k.astype(jnp.float32).transpose(0, 2, 1)[:, :, None, :]
    qb = q.reshape(B, nb, blk, H, d).transpose(1, 0, 2, 3, 4)
    cqb = c_q.astype(jnp.float32).reshape(B, nb, blk, H).transpose(1, 0, 3, 2)
    pb = q_pos.reshape(nb, blk)
    scale = d ** -0.5

    def one_block(args):
        qq, cq, pp = args
        s = jnp.einsum('bqhd,bkhd->bhqk', qq, k, preferred_element_type=jnp.float32) * scale
        s = s + cq[..., None] - c_kT
        s = jnp.where(k_pos[None, :] <= pp[:, None], s, -jnp.inf)
        p = jax.nn.softmax(s, axis=-1)
        return jnp.einsum('bhqk,bkhd->bqhd', p.astype(v.dtype), v)

    o = lax.map(one_block, (qb, cqb, pb))
    return o.transpose(1, 0, 2, 3, 4).reshape(B, Tq, H, d)

def mem_attention(q, k, v):
    s = jnp.einsum('bqhd,bkhd->bhqk', q, k, preferred_element_type=jnp.float32) * (MEM_DH ** -0.5)
    p = jax.nn.softmax(s, axis=-1)
    return jnp.einsum('bhqk,bkhd->bqhd', p.astype(v.dtype), v)

def mem_keys_values(mem, g_in, w_kv, g_k):
    B = mem.shape[0]
    kv = rmsnorm(mem, g_in) @ w_kv
    k, v = jnp.split(kv, 2, axis=-1)
    k = rmsnorm(k.reshape(B, N_MEM, MEM_HEADS, MEM_DH), g_k)
    v = v.reshape(B, N_MEM, MEM_HEADS, MEM_DH)
    return k, v

def peer_ffn(h, w_q, sub_keys, u_tab, v_tab):
    B, T, D = h.shape
    n = B * T
    blk = min(PEER_TOK_BLOCK, n)
    pad = (-n) % blk
    hb = jnp.pad(h.reshape(n, D), ((0, pad), (0, 0))).reshape(-1, blk, D)

    def one_block(xb):
        q = (xb @ w_q).reshape(blk, PEER_HEADS, 2, PEER_DHALF)
        s = jnp.einsum('thpc,hpkc->thpk', q, sub_keys, preferred_element_type=jnp.float32)
        s1, i1 = lax.top_k(s[:, :, 0], PEER_TOPK)
        s2, i2 = lax.top_k(s[:, :, 1], PEER_TOPK)
        cand = (s1[..., :, None] + s2[..., None, :]).reshape(blk, PEER_HEADS, PEER_TOPK * PEER_TOPK)
        cidx = (i1[..., :, None] * N_KEYS + i2[..., None, :]).reshape(blk, PEER_HEADS, PEER_TOPK * PEER_TOPK)
        top, pos = lax.top_k(cand, PEER_TOPK)
        idx = jnp.take_along_axis(cidx, pos, axis=-1)
        g = jax.nn.softmax(top, axis=-1)
        u = jnp.take(u_tab, idx, axis=0)
        a = jax.nn.gelu(jnp.einsum('thkd,td->thk', u, xb, preferred_element_type=jnp.float32), approximate=False)
        w = (g * a).astype(xb.dtype)
        return jnp.einsum('thk,thkd->td', w, jnp.take(v_tab, idx, axis=0))

    out = lax.map(one_block, hb)
    return out.reshape(-1, D)[:n].reshape(B, T, D)

def trunk_layer(x, mem_k, mem_v, fox_past, gla_s0, g_attn, w_in, gla_w_a2, gla_b_a, gla_g_out, fox_b_f,
                fox_g_q, fox_g_k, mem_g_q, w_branch, w_out, g_ffn, peer_w_q, peer_sub_keys, peer_u, peer_v):
    B, T, _ = x.shape
    h = rmsnorm(x, g_attn)
    gq, gk, gv, gg, ga, fq, fk, fv, ff, mq, gates = split_cols(h @ w_in)
    log_a = jax.nn.log_sigmoid((ga @ gla_w_a2 + gla_b_a).astype(jnp.float32)) / GLA_TAU
    o_gla, s_new = gla_recurrence(gq.reshape(B, T, GLA_HEADS, GLA_DK), gk.reshape(B, T, GLA_HEADS, GLA_DK),
                                  gv.reshape(B, T, GLA_HEADS, GLA_DV), log_a.reshape(B, T, GLA_HEADS, GLA_DK), gla_s0)
    o_gla = (rmsnorm(o_gla, gla_g_out) * jax.nn.silu(gg.reshape(B, T, GLA_HEADS, GLA_DV))).reshape(B, T, BRANCH_W)
    fq = rmsnorm(fq.reshape(B, T, FOX_HEADS, FOX_DH), fox_g_q)
    fk = rmsnorm(fk.reshape(B, T, FOX_HEADS, FOX_DH), fox_g_k)
    fv = fv.reshape(B, T, FOX_HEADS, FOX_DH)
    logf = jax.nn.log_sigmoid((ff + fox_b_f).astype(jnp.float32))
    if fox_past is None:
        k_all, v_all, logf_all = fk, fv, logf
    else:
        k_all = jnp.concatenate([fox_past[0], fk], axis=1)
        v_all = jnp.concatenate([fox_past[1], fv], axis=1)
        logf_all = jnp.concatenate([fox_past[2].astype(jnp.float32), logf], axis=1)
    c_all = jnp.cumsum(logf_all, axis=1)
    o_fox = fox_attention(fq, k_all, v_all, c_all[:, -T:], c_all).reshape(B, T, BRANCH_W)
    mq = rmsnorm(mq.reshape(B, T, MEM_HEADS, MEM_DH), mem_g_q)
    o_mem = mem_attention(mq, mem_k, mem_v).reshape(B, T, BRANCH_W)
    proj = jnp.einsum('nbtc,ncd->nbtd', jnp.stack([o_gla, o_fox, o_mem], axis=0), w_branch)
    gate = jax.nn.sigmoid(gates.reshape(B, T, N_BRANCH, D_MODEL))
    x = x + jnp.einsum('btnd,nbtd->btd', gate, proj) @ w_out
    x = x + peer_ffn(rmsnorm(x, g_ffn), peer_w_q, peer_sub_keys, peer_u, peer_v)
    return x, fk, fv, logf, s_new

def setup_inputs(seed: int = 0) -> dict:
    key = jax.random.key(seed)
    ks = list(jax.random.split(key, 40))

    def nrm(i, shape, scale):
        return jax.random.normal(ks[i], shape, jnp.float32) * scale

    D = D_MODEL
    return {
        "x_prompt": nrm(0, (BATCH, SEQ, D), 1.0),
        "x_sample": nrm(1, (DEC_BATCH, DEC_SEQ, D), 1.0),
        "mem_prompt": nrm(2, (BATCH, N_MEM, D), 1.0),
        "cache_fox_k": nrm(3, (DEPTH, DEC_BATCH, PAST_LEN, FOX_HEADS, FOX_DH), 1.0),
        "cache_fox_v": nrm(4, (DEPTH, DEC_BATCH, PAST_LEN, FOX_HEADS, FOX_DH), 1.0),
        "cache_fox_logf": jax.nn.log_sigmoid(2.0 + nrm(5, (DEPTH, DEC_BATCH, PAST_LEN, FOX_HEADS), 1.0)),
        "state_gla": nrm(6, (DEPTH, DEC_BATCH, GLA_HEADS, GLA_DK, GLA_DV), 0.5),
        "cache_mem_k": nrm(7, (DEPTH, DEC_BATCH, N_MEM, MEM_HEADS, MEM_DH), 1.0),
        "cache_mem_v": nrm(8, (DEPTH, DEC_BATCH, N_MEM, MEM_HEADS, MEM_DH), 1.0),
        "g_attn": 1.0 + nrm(9, (DEPTH, D), 0.02),
        "w_in": nrm(10, (DEPTH, D, IN_TOTAL), D ** -0.5),
        "gla_w_a2": nrm(11, (DEPTH, GLA_RANK, GLA_HEADS * GLA_DK), GLA_RANK ** -0.5),
        "gla_b_a": nrm(12, (DEPTH, GLA_HEADS * GLA_DK), 0.1),
        "gla_g_out": 1.0 + nrm(13, (DEPTH, GLA_DV), 0.02),
        "fox_b_f": 2.0 + nrm(14, (DEPTH, FOX_HEADS), 0.1),
        "fox_g_q": 1.0 + nrm(15, (DEPTH, FOX_DH), 0.02),
        "fox_g_k": 1.0 + nrm(16, (DEPTH, FOX_DH), 0.02),
        "mem_g_q": 1.0 + nrm(17, (DEPTH, MEM_DH), 0.02),
        "mem_g_in": 1.0 + nrm(18, (DEPTH, D), 0.02),
        "mem_w_kv": nrm(19, (DEPTH, D, 2 * MEM_HEADS * MEM_DH), D ** -0.5),
        "mem_g_k": 1.0 + nrm(20, (DEPTH, MEM_DH), 0.02),
        "w_branch": nrm(21, (DEPTH, N_BRANCH, BRANCH_W, D), BRANCH_W ** -0.5),
        "w_out": nrm(22, (DEPTH, D, D), D ** -0.5),
        "g_ffn": 1.0 + nrm(23, (DEPTH, D), 0.02),
        "peer_w_q": nrm(24, (DEPTH, D, PEER_HEADS * PEER_DKEY), D ** -0.5),
        "peer_sub_keys": nrm(25, (DEPTH, PEER_HEADS, 2, N_KEYS, PEER_DHALF), PEER_DHALF ** -0.5),
        "peer_u": nrm(26, (DEPTH, N_EXPERTS, D), D ** -0.5),
        "peer_v": nrm(27, (DEPTH, N_EXPERTS, D), PEER_HEADS ** -0.5),
    }

def reference(x_prompt, x_sample, mem_prompt, cache_fox_k, cache_fox_v, cache_fox_logf, state_gla,
              cache_mem_k, cache_mem_v, g_attn, w_in, gla_w_a2, gla_b_a, gla_g_out, fox_b_f, fox_g_q, fox_g_k,
              mem_g_q, mem_g_in, mem_w_kv, mem_g_k, w_branch, w_out, g_ffn, peer_w_q, peer_sub_keys, peer_u, peer_v):
    yp, ys = x_prompt, x_sample
    fkp, fvp, flp, sgp, mkp, mvp = [], [], [], [], [], []
    fks, fvs, fls, sgs = [], [], [], []
    for l in range(DEPTH):
        lw = dict(g_attn=g_attn[l], w_in=w_in[l], gla_w_a2=gla_w_a2[l], gla_b_a=gla_b_a[l], gla_g_out=gla_g_out[l],
                  fox_b_f=fox_b_f[l], fox_g_q=fox_g_q[l], fox_g_k=fox_g_k[l], mem_g_q=mem_g_q[l],
                  w_branch=w_branch[l], w_out=w_out[l], g_ffn=g_ffn[l], peer_w_q=peer_w_q[l],
                  peer_sub_keys=peer_sub_keys[l], peer_u=peer_u[l], peer_v=peer_v[l])
        mk, mv = mem_keys_values(mem_prompt, mem_g_in[l], mem_w_kv[l], mem_g_k[l])
        s0 = jnp.zeros((yp.shape[0], GLA_HEADS, GLA_DK, GLA_DV), jnp.float32)
        yp, k1, v1, lf1, s1 = trunk_layer(yp, mk, mv, None, s0, **lw)
        fkp.append(k1); fvp.append(v1); flp.append(lf1); sgp.append(s1); mkp.append(mk); mvp.append(mv)
        ys, k2, v2, lf2, s2 = trunk_layer(ys, cache_mem_k[l], cache_mem_v[l],
                                          (cache_fox_k[l], cache_fox_v[l], cache_fox_logf[l]), state_gla[l], **lw)
        fks.append(k2); fvs.append(v2); fls.append(lf2); sgs.append(s2)
    return (yp, ys, jnp.stack(fkp), jnp.stack(fvp), jnp.stack(flp), jnp.stack(sgp), jnp.stack(mkp), jnp.stack(mvp),
            jnp.stack(fks), jnp.stack(fvs), jnp.stack(fls), jnp.stack(sgs))


_drawn_inputs = setup_inputs


def setup_inputs(seed=0):
    import zlib

    import numpy as np

    out = dict(_drawn_inputs(seed))
    spreads = {}
    factors = {'cache_fox_logf': 3.293,
     'gla_g_out': 9.77,
     'fox_g_q': 80.11,
     'mem_g_q': 8.0,
     'mem_g_in': 2.873,
     'mem_g_k': 2.946,
     'g_ffn': 3.663}
    for name, (base, spread) in spreads.items():
        noise = np.random.default_rng([zlib.crc32(name.encode()), seed]).standard_normal(out[name].shape)
        drawn = base * np.exp(spread * noise) if base else spread * noise
        out[name] = __import__('jax').numpy.asarray(drawn.astype(out[name].dtype))
    for name, factor in factors.items():
        out[name] = (out[name] * factor).astype(out[name].dtype)
    return out
```

```python
import concourse.bass as bass
from concourse import mybir
from contextlib import ExitStack

F32 = mybir.dt.float32
U32 = mybir.dt.uint32
I32 = mybir.dt.int32
ALU = mybir.AluOpType
ACT = mybir.ActivationFunctionType
AX = mybir.AxisListType

D = 1024
DT = D // 128
SEQ, SAMPLE_T, PAST = 1024, 64, 512
TOKENS = SEQ + SAMPLE_T
TILES = SEQ // 128
PAST_TILES = PAST // 128
EPS = 1e-6
CHUNK = 64
GH, GDK, GDV, GRANK = 4, 64, 128, 16
GLA_TAU = 16.0
FH, FD = 8, 64
MH, MD, NMEM = 4, 128, 256
MT = NMEM // 128
BW = 512
BRANCHES = 3
GQ, GK, GV, GG, GA, FQ, FK, FV, FF, MQ = 0, 256, 512, 1024, 1536, 1552, 2064, 2576, 3088, 3096
P_COLS = 3608
P_CHUNKS = 8
PW = P_COLS // P_CHUNKS
MASKED = -1.0e30


def rows(tile, T):
    if isinstance(tile, int):
        return slice(tile * 128, tile * 128 + T)
    return bass.ds(tile * 128, T)


def tokens(t0):
    return t0 * 128


class Scope:

    def __init__(self, nc, ctx, tag):
        self.nc, self.ctx, self.tag, self.sems = nc, ctx, tag, []

    def sb(self, name, shape, dt=F32):
        return self.ctx.enter_context(self.nc.sbuf_tensor(f"{self.tag}_{name}", shape, dt))

    def pb(self, name, shape, dt=F32):
        return self.ctx.enter_context(self.nc.psum_tensor(f"{self.tag}_{name}", shape, dt))

    def sem(self, name):
        self.sems.append(self.ctx.enter_context(self.nc.semaphore(f"{self.tag}_{name}")))
        return self.sems[-1]

    def retire(self):
        ids = sorted(x.num for x in self.sems)
        assert ids == list(range(ids[0], ids[-1] + 1))
        with self.nc.Block() as block:
            @block.gpsimd
            def _(pool):
                pool.sem_clear(range(ids[0], ids[-1] + 1))


def constants(nc, c):
    with nc.Block() as block:
        s = c.sem("const")

        @block.gpsimd
        def _(pool):
            n = [0]

            def step(ins):
                n[0] += 1
                ins.then_inc(s, 1)
                pool.wait_ge(s, n[0])

            step(nc.gpsimd.memset(c.ident[:, :], 0.0))
            step(nc.gpsimd.affine_select(out=c.ident[:, :], in_=c.ident[:, :], compare_op=ALU.not_equal, fill=1.0,
                                         base=0, pattern=[[-1, 128]], channel_multiplier=1))
            step(nc.gpsimd.memset(c.ones[:, :], 1.0))
            step(nc.gpsimd.affine_select(out=c.upto[:, :], in_=c.ones[:, :], compare_op=ALU.is_ge, fill=0.0,
                                         base=0, pattern=[[1, 128]], channel_multiplier=-1))
            step(nc.gpsimd.tensor_copy(c.upto_chunk[:, :], c.upto[:, :]))
            step(nc.gpsimd.memset(c.upto_chunk[0:CHUNK, CHUNK:128], 0.0))
            step(nc.gpsimd.affine_select(out=c.after_chunk[:, :], in_=c.ones[:, :], compare_op=ALU.is_gt, fill=0.0,
                                         base=0, pattern=[[-1, 128]], channel_multiplier=1))
            step(nc.gpsimd.memset(c.after_chunk[CHUNK:128, 0:CHUNK], 0.0))
            step(nc.gpsimd.memset(c.chunk_of[:, :], 0.0))
            step(nc.gpsimd.memset(c.chunk_of[0:CHUNK, 0:1], 1.0))
            step(nc.gpsimd.memset(c.chunk_of[CHUNK:128, 1:2], 1.0))
            step(nc.gpsimd.memset(c.future[:, :], 0.0))
            step(nc.gpsimd.affine_select(out=c.future[:, :], in_=c.future[:, :], compare_op=ALU.is_ge, fill=MASKED,
                                         base=0, pattern=[[-1, 128]], channel_multiplier=1))
            step(nc.gpsimd.memset(c.eps[:, :], EPS))
            step(nc.gpsimd.memset(c.one[:, :], 1.0))
            step(nc.gpsimd.memset(c.zero_row[:, :], 0.0))
            step(nc.gpsimd.iota(c.iota16[:, :], pattern=[[1, 16]], base=0, channel_multiplier=0,
                                allow_small_or_imprecise_dtypes=True))


def input_projection(nc, c, x_all, g_attn, w_in1, proj, hT_spill):
    UN = 18
    RING = 6
    with ExitStack() as ctx:
        m = Scope(nc, ctx, "in")
        g_bc = m.sb("g_bc", [128, D])
        x_tile = [m.sb(f"x_tile{k}", [128, D]) for k in range(2)]
        h_tile = m.sb("h_tile", [128, D])
        squares = m.sb("squares", [128, D])
        stat = m.sb("stat", [128, 4])
        hT = m.sb("hT", [128, DT, TOKENS])
        w = [m.sb(f"w{k}", [128, DT, PW]) for k in range(2)]
        out = m.sb("out", [128, RING, PW])
        p_tr = m.pb("p_tr", [128, D])
        p_mm = [m.pb(f"p_mm{k}", [128, 512]) for k in range(RING)]

        s_g, s_spill = m.sem("s_g"), m.sem("s_spill")
        s_x = m.sem("s_x")
        s_w = [m.sem(f"s_w{k}") for k in range(2)]
        s_sq, s_std, s_rstd, s_h, s_tr, s_hT = (m.sem(n) for n in ("s_sq", "s_std", "s_rstd", "s_h", "s_tr", "s_hT"))
        s_mm = m.sem("s_mm")
        s_ev = [m.sem(f"s_ev{k}") for k in range(2)]
        s_put = [m.sem(f"s_put{k}") for k in range(RING)]
        s_step = {e: m.sem(f"s_step_{k}") for k, e in (("pe", nc.tensor),)}

        with nc.Block() as block:
            @block.sync
            def _(sp):
                sp.dma_start(g_bc[:, :], g_attn[0:1, :].broadcast_to([128, D])).then_inc(s_g, 16)

                def load(tile, T):
                    sp.dma_start(x_tile[0][:T, :], x_all[rows(tile, T), :]).then_inc(s_x, 16)

                load(0, 128)
                for k in range(2):
                    sp.dma_start(w[k][:, :, :], w_in1[k].rearrange("p (a b) -> p a b", a=DT)).then_inc(s_w[k], 16)
                with sp.Fori(1, TILES) as t:
                    sp.wait_ge(s_h, t)
                    load(t, 128)
                sp.wait_ge(s_h, TILES)
                load(TILES, SAMPLE_T)
                sp.wait_ge(s_hT, TILES + 1)
                sp.dma_start(hT_spill.rearrange("p (a b) -> p a b", a=DT), hT[:, :, :]).then_inc(s_spill, 16)
                def store_chunks(b, load_more):
                    for u in range(UN):
                        chunk, tile = b * 2 + u // 9, u % 9
                        T = 128 if tile < TILES else SAMPLE_T
                        sp.wait_ge(s_ev[u % 2], b * 9 + u // 2 + 1 + 3)
                        sp.dma_start(proj[tile * 128:tile * 128 + T, bass.ds(chunk * PW, PW)],
                                     out[:T, u % RING, :]).then_inc(s_put[u % RING], 16)
                        if load_more and tile == TILES:
                            sp.wait_ge(s_mm, b * UN + u + 1)
                            sp.dma_start(w[u // 9][:, :, :], w_in1[bass.ds(chunk + 2, 1), :, :].squeeze(0)
                                         .rearrange("p (a b) -> p a b", a=DT)).then_inc(s_w[u // 9], 16)

                with sp.Fori(0, P_CHUNKS // 2 - 1) as b:
                    store_chunks(b, True)
                store_chunks(P_CHUNKS // 2 - 1, False)
                for k in range(RING):
                    sp.wait_ge(s_put[k], 16 * (P_CHUNKS // 2 * 3 + 1))
                sp.wait_ge(s_spill, 16)

            @block.tensor
            def _(pe):
                def transposes(tile, T):
                    pe.wait_ge(s_h, tile + 1)
                    if not (isinstance(tile, int) and tile == 0):
                        pe.wait_ge(s_hT, tile)
                        pe.sem_inc(s_step[pe], 1)
                    for dt in range(DT):
                        mm = nc.tensor.transpose(p_tr[:, dt * 128:dt * 128 + T], h_tile[:T, dt * 128:(dt + 1) * 128],
                                                 c.ident[:T, :T])
                    mm.then_inc(s_tr, 1)

                transposes(0, 128)
                with pe.Fori(1, TILES) as t:
                    transposes(t, 128)
                transposes(TILES, SAMPLE_T)
                pe.wait_ge(s_hT, TILES + 1)
                with pe.Fori(0, P_CHUNKS // 2) as b:
                    for u in range(UN):
                        tile = u % 9
                        T = 128 if tile < TILES else SAMPLE_T
                        if tile == 0:
                            pe.wait_ge(s_w[u // 9], (b + 1) * 16)
                        pe.wait_ge(s_ev[u % 2], b * 9 + u // 2 + 1)
                        pe.sem_inc(s_step[pe], 1)
                        for dt in range(DT):
                            mm = nc.tensor.matmul(p_mm[u % RING][:T, :PW], hT[:, dt, tile * 128:tile * 128 + T],
                                                  w[u // 9][:, dt, :], start=dt == 0, stop=dt == DT - 1)
                        mm.then_inc(s_mm, 1)

            def evacuate(eng, parity, copy):
                eng.sem_inc(s_ev[parity], 3)
                with eng.Fori(0, P_CHUNKS // 2) as b:
                    for u in range(parity, UN, 2):
                        T = 128 if u % 9 < TILES else SAMPLE_T
                        eng.wait_ge(s_mm, b * UN + u + 1)
                        eng.wait_ge(s_put[u % RING], 16 * (b * 3 + u // RING + 1))
                        copy(out[:T, u % RING, :], p_mm[u % RING][:T, :PW]).then_inc(s_ev[parity], 1)

            @block.scalar
            def _(act):
                def stats(tile, T):
                    act.wait_ge(s_x, 16 * (tile + 1))
                    nc.scalar.activation(squares[:T, :], x_tile[0][:T, :], ACT.Square,
                                         accum_out=stat[:T, 0:1]).then_inc(s_sq, 1)
                    act.wait_ge(s_sq, tile + 1)
                    nc.scalar.activation(stat[:T, 1:2], stat[:T, 0:1], ACT.Sqrt, bias=c.eps[:T, :],
                                         scale=1.0 / D).then_inc(s_std, 1)
                    act.wait_ge(s_tr, tile + 1)
                    nc.scalar.copy(hT[:, :, bass.ds(tile * 128, T)],
                                   p_tr[:, :].rearrange("p (a b) -> p a b", b=128)[:, :, :T]).then_inc(s_hT, 1)

                for k in range(0, RING, 2):
                    act.sem_inc(s_put[k], 16)
                with act.Fori(0, TILES) as t:
                    stats(t, 128)
                stats(TILES, SAMPLE_T)
                evacuate(act, 0, nc.scalar.copy)

            @block.vector
            def _(dve):
                dve.wait_ge(s_g, 16)

                def norm(tile, T):
                    dve.wait_ge(s_std, tile + 1)
                    nc.vector.reciprocal(stat[:T, 2:3], stat[:T, 1:2]).then_inc(s_rstd, 1)
                    if not (isinstance(tile, int) and tile == 0):
                        dve.wait_ge(s_tr, tile)
                    dve.wait_ge(s_rstd, tile + 1)
                    nc.vector.scalar_tensor_tensor(out=h_tile[:T, :], in0=x_tile[0][:T, :], scalar=stat[:T, 2:3],
                                                   in1=g_bc[:T, :], op0=ALU.mult, op1=ALU.mult).then_inc(s_h, 1)

                for k in range(1, RING, 2):
                    dve.sem_inc(s_put[k], 16)
                norm(0, 128)
                with dve.Fori(1, TILES) as t:
                    norm(t, 128)
                norm(TILES, SAMPLE_T)
                evacuate(dve, 1, nc.vector.tensor_copy)
        m.retire()


def memory_projection(nc, c, mem, g_in, w_kv, g_k, mem_k, mem_v):
    with ExitStack() as ctx:
        m = Scope(nc, ctx, "mem")
        g_bc = m.sb("g_bc", [128, D])
        gk_bc = m.sb("gk_bc", [128, MD])
        w = m.sb("w", [128, DT, D])
        x = m.sb("x", [128, MT, D])
        h = m.sb("h", [128, MT, D])
        hT = m.sb("hT", [128, DT, NMEM])
        squares = m.sb("squares", [128, D])
        stat = m.sb("stat", [128, MT, 4])
        ksq = m.sb("ksq", [128, MT, BW])
        kst = m.sb("kst", [128, MT, 3 * MH])
        kn = m.sb("kn", [128, MT, BW])
        v = m.sb("v", [128, MT, BW])
        p_tr = m.pb("p_tr", [128, D])
        p_kv = m.pb("p_kv", [128, MT, 2, BW])
        s_g, s_w, s_x, s_sq, s_std, s_h, s_tr, s_hT = (m.sem(n) for n in (
            "s_g", "s_w", "s_x", "s_sq", "s_std", "s_h", "s_tr", "s_hT"))
        s_kv, s_ksq, s_kss, s_kstd, s_kn, s_v, s_put, s_d = (m.sem(n) for n in (
            "s_kv", "s_ksq", "s_kss", "s_kstd", "s_kn", "s_v", "s_put", "s_d"))

        with nc.Block() as block:
            @block.sync
            def _(sp):
                sp.dma_start(x[:, :, :], mem.rearrange("(a p) d -> p a d", p=128)).then_inc(s_x, 16)
                sp.dma_start(g_bc[:, :], g_in[0:1, :].broadcast_to([128, D])).then_inc(s_g, 16)
                sp.dma_start(gk_bc[:, :], g_k[0:1, :].broadcast_to([128, MD])).then_inc(s_g, 16)
                sp.dma_start(w[:, :, :], w_kv.rearrange("(a p) n -> p a n", p=128)).then_inc(s_w, 16)
                sp.wait_ge(s_kn, MT)
                sp.dma_start(mem_k.rearrange("(a p) n -> p a n", p=128), kn[:, :, :]).then_inc(s_put, 16)
                sp.wait_ge(s_v, MT)
                sp.dma_start(mem_v.rearrange("(a p) n -> p a n", p=128), v[:, :, :]).then_inc(s_put, 16)
                sp.wait_ge(s_put, 32)

            @block.tensor
            def _(pe):
                for a in range(MT):
                    pe.wait_ge(s_h, a + 1)
                    if a:
                        pe.wait_ge(s_hT, a)
                    for dt in range(DT):
                        mm = nc.tensor.transpose(p_tr[:, dt * 128:(dt + 1) * 128], h[:, a, dt * 128:(dt + 1) * 128],
                                                 c.ident[:, :])
                    mm.then_inc(s_tr, 1)
                pe.wait_ge(s_w, 16)
                for a in range(MT):
                    pe.wait_ge(s_hT, a + 1)
                    for n in range(2):
                        for dt in range(DT):
                            mm = nc.tensor.matmul(p_kv[:, a, n, :], hT[:, dt, a * 128:(a + 1) * 128],
                                                  w[:, dt, n * BW:(n + 1) * BW], start=dt == 0, stop=dt == DT - 1)
                    mm.then_inc(s_kv, 1)

            @block.scalar
            def _(act):
                act.wait_ge(s_x, 16)
                for a in range(MT):
                    if a:
                        act.wait_ge(s_sq, a)
                    nc.scalar.activation(squares[:, :], x[:, a, :], ACT.Square,
                                         accum_out=stat[:, a, 0:1]).then_inc(s_sq, 1)
                for a in range(MT):
                    act.wait_ge(s_sq, a + 1)
                    nc.scalar.activation(stat[:, a, 1:2], stat[:, a, 0:1], ACT.Sqrt, bias=c.eps[:, :],
                                         scale=1.0 / D).then_inc(s_std, 1)
                for a in range(MT):
                    act.wait_ge(s_tr, a + 1)
                    nc.scalar.copy(hT[:, :, a * 128:(a + 1) * 128],
                                   p_tr[:, :].rearrange("p (a b) -> p a b", b=128)).then_inc(s_hT, 1)
                for a in range(MT):
                    act.wait_ge(s_kv, a + 1)
                    nc.scalar.activation(ksq[:, a, :], p_kv[:, a, 0, :], ACT.Square).then_inc(s_ksq, 1)
                    nc.scalar.copy(v[:, a, :], p_kv[:, a, 1, :]).then_inc(s_v, 1)
                    act.wait_ge(s_kss, a + 1)
                    nc.scalar.activation(kst[:, a, MH:2 * MH], kst[:, a, 0:MH], ACT.Sqrt, bias=c.eps[:, :],
                                         scale=1.0 / MD).then_inc(s_kstd, 1)

            @block.vector
            def _(dve):
                n = [0]

                def link(ins):
                    n[0] += 1
                    ins.then_inc(s_d, 1)
                    dve.wait_ge(s_d, n[0])

                dve.wait_ge(s_g, 32)
                for a in range(MT):
                    dve.wait_ge(s_std, a + 1)
                    link(nc.vector.reciprocal(stat[:, a, 2:3], stat[:, a, 1:2]))
                    nc.vector.scalar_tensor_tensor(out=h[:, a, :], in0=x[:, a, :], scalar=stat[:, a, 2:3],
                                                   in1=g_bc[:, :], op0=ALU.mult, op1=ALU.mult).then_inc(s_h, 1)
                for a in range(MT):
                    dve.wait_ge(s_ksq, a + 1)
                    nc.vector.tensor_reduce(out=kst[:, a, 0:MH], in_=ksq[:, a, :].rearrange("p (h d) -> p h d", h=MH),
                                            axis=AX.X, op=ALU.add).then_inc(s_kss, 1)
                    dve.wait_ge(s_kstd, a + 1)
                    link(nc.vector.reciprocal(kst[:, a, 2 * MH:3 * MH], kst[:, a, MH:2 * MH]))
                    k3 = kn[:, a, :].rearrange("p (h d) -> p h d", h=MH)
                    link(nc.vector.tensor_tensor(
                        out=k3, in0=p_kv[:, a, 0, :].rearrange("p (h d) -> p h d", h=MH),
                        in1=kst[:, a, 2 * MH:3 * MH].unsqueeze(2).broadcast_to([128, MH, MD]), op=ALU.mult))
                    nc.vector.tensor_tensor(out=k3, in0=k3, in1=gk_bc[:, :].unsqueeze(1).broadcast_to([128, MH, MD]),
                                            op=ALU.mult).then_inc(s_kn, 1)
        m.retire()


def mixers(nc, c, proj, small, caches, mem_k, mem_v, outs, oT_spill):
    w_a2, b_a, g_out, b_f, g_q, g_k, g_mq = small
    ck, cv, clf, state0, cmk, cmv = caches
    k_p, v_p, lf_p, st_p, k_s, v_s, lf_s, st_s = outs
    HH = FH // 2
    AD = FD + 2

    with ExitStack() as ctx:
        m = Scope(nc, ctx, "mix")
        wa2 = m.sb("wa2", [GRANK, GH * GDK])
        ba_bc = m.sb("ba_bc", [128, GH * GDK])
        go_bc = m.sb("go_bc", [128, GDV])
        bf_bc = m.sb("bf_bc", [128, FH])
        gq_bc = m.sb("gq_bc", [128, FD])
        gk_bc = m.sb("gk_bc", [128, FD])
        gm_bc = m.sb("gm_bc", [128, MD])
        P = m.sb("P", [128, P_COLS])
        sq = m.sb("sq", [128, 1024])
        sqm = m.sb("sqm", [128, BW])
        tmp = m.sb("tmp", [128, BW])
        st = m.sb("st", [128, 64])
        q_aug = m.sb("q_aug", [128, FH, AD])
        k_aug = m.sb("k_aug", [128, FH, AD])
        mq = m.sb("mq", [128, BW])
        z = m.sb("z", [128, 264])
        za = m.sb("za", [128, 264])
        ze = m.sb("ze", [128, 264])
        zl = m.sb("zl", [128, 264])
        ls = m.sb("ls", [128, 264])
        la = m.sb("la", [128, 256])
        gaT = m.sb("gaT", [GRANK, 128])
        carry = m.sb("carry", [128, FH])
        cs = m.sb("cs", [128, FH])
        eb = m.sb("eb", [128, 3, 256])
        ebl = m.sb("ebl", [GDK, 2 * GH])
        qkd = m.sb("qkd", [128, 2 * GH, GDK])
        ko = m.sb("ko", [128, GH, GDK])
        qkdT = m.sb("qkdT", [GDK, 2 * GH, 128])
        attT = m.sb("attT", [128, GH, 128])
        S = [m.sb(f"S{k}", [GDK, GH, GDV]) for k in range(2)]
        sig = m.sb("sig", [128, BW])
        qT = m.sb("qT", [AD, FH, 128])
        kT = m.sb("kT", [AD, FH, SEQ])
        V = m.sb("V", [128, TILES, BW])
        mkT = m.sb("mkT", [128, MH, NMEM])
        mv = m.sb("mv", [128, MT, BW])
        mk = m.sb("mk", [128, MT, BW])
        mqT = m.sb("mqT", [128, MH, 128])
        pm = m.sb("pm", [128, MH, NMEM])
        pmT = m.sb("pmT", [128, MH * MT, 128])
        mstat = m.sb("mstat", [128, 4 * MH])
        diag = m.sb("diag", [128, FH, 128])
        fmax = m.sb("fmax", [128, 3, FH])
        lsum = m.sb("lsum", [128, FH])
        rsum = m.sb("rsum", [128, FH])
        rl = m.sb("rl", [128, FH])
        PP = m.sb("PP", [128, FH, 128])
        PT = m.sb("PT", [128, FH, 128])
        o_all = m.sb("o_all", [128, BRANCHES * BW])
        oT = [m.sb(f"oT{k}", [128, 4, 128]) for k in range(3)]

        p_tr = m.pb("p_tr", [128, 1024])
        p_h = [m.pb(f"p_h{k}", [128, HH, 128]) for k in range(2)]
        p_of = m.pb("p_of", [128, BW])
        p_g = m.pb("p_g", [128, BW])
        p_x = m.pb("p_x", [128, BW])
        p_y = m.pb("p_y", [128, BW])

        names = ("par", "P", "sq", "ss", "std", "kn", "qn", "mq", "gaT_mm", "gaT", "za", "z", "ln", "la", "cum",
                 "aug", "eb", "qd", "trq", "qT", "trk", "kT", "trg", "gT", "trm", "mqT", "att_mm", "att", "dS",
                 "S1", "S2", "og_mm", "gsq", "gss", "gstd", "og", "sig", "ogl", "ms_mm", "mmax", "pm", "trpm",
                 "pmT", "om_mm", "omem", "fmaxd", "neg", "z0", "ofox", "tro", "oT", "kout", "lfout", "V", "vout",
                 "mem", "mkT_mm", "mkT", "S0", "sout", "ck", "ot", "carry",
                 "d", "a", "e", "dg", "ls0", "astep", "spstep", "dstep", "pestep", "gq")
        s = {n: m.sem(f"s_{n}") for n in names}
        s_oput = [m.sem(f"s_oput{k}") for k in range(3)]
        s_qk = [m.sem(f"s_qk{k}") for k in range(2)]
        s_free = [m.sem(f"s_free{k}") for k in range(2)]
        s_p = [m.sem(f"s_p{k}") for k in range(2)]
        s_l = [m.sem(f"s_l{k}") for k in range(2)]
        s_pt = [m.sem(f"s_pt{k}") for k in range(2)]
        s_pts = [m.sem(f"s_pts{k}") for k in range(2)]
        s_pv = [m.sem(f"s_pv{k}") for k in range(2)]

        def at0(t):
            return isinstance(t, int) and t == 0

        def key_step(t):
            return t if not (isinstance(t, int) and t == TILES) else TILES + PAST_TILES

        def qk_base(t):
            return t * t

        def pv_base(t):
            return t * (t + 1) // 2

        def h3(ap, h):
            return ap.rearrange("p (h d) -> p h d", h=h)

        with nc.Block() as block:
            @block.sync
            def _(sp):
                for dst, src, n in ((wa2[:, :], w_a2[0], None), (ba_bc[:, :], b_a, 256), (go_bc[:, :], g_out, GDV),
                                    (bf_bc[:, :], b_f, FH), (gq_bc[:, :], g_q, FD), (gk_bc[:, :], g_k, FD),
                                    (gm_bc[:, :], g_mq, MD)):
                    sp.dma_start(dst, src if n is None else src[0:1, :].broadcast_to([128, n])).then_inc(s["par"], 16)

                def load_P(t, T):
                    if not at0(t):
                        sp.wait_ge(s["ogl"], t)
                    sp.dma_start(P[:T, :], proj[rows(t, T), :]).then_inc(s["P"], 16)

                def load_mem(k_src, v_src, again):
                    if again:
                        sp.wait_ge(s["om_mm"], TILES)
                    sp.dma_start(mk[:, :, :], k_src.rearrange("(a p) n -> p a n", p=128)).then_inc(s["mem"], 16)
                    sp.dma_start(mv[:, :, :], v_src.rearrange("(a p) n -> p a n", p=128)).then_inc(s["mem"], 16)

                def store_tile(t, T, k_dst, lf_dst, r):
                    sp.wait_ge(s["kn"], t + 1)
                    sp.dma_start(h3(k_dst[r, :], FH), k_aug[:T, :, 0:FD]).then_inc(s["kout"], 16)
                    sp.wait_ge(s["la"], t + 1)
                    sp.dma_start(lf_dst[r, :], ls[:T, 256:264]).then_inc(s["lfout"], 16)

                def store_o(t, T):
                    for k in range(3):
                        sp.wait_ge(s["oT"], 3 * t + k + 1)
                        sp.sem_inc(s["spstep"], 1)
                        sp.dma_start(oT_spill[k, :, :, bass.ds(t * 128, T)] if not isinstance(t, int) else
                                     oT_spill[k, :, :, t * 128:t * 128 + T], oT[k][:, :, :T]).then_inc(s_oput[k], 16)

                load_P(0, 128)
                load_mem(mem_k, mem_v, False)
                sp.dma_start(V[:, :, :], proj[0:SEQ, FV:FV + BW].rearrange("(a p) n -> p a n", p=128))\
                    .then_inc(s["V"], 16)
                sp.wait_ge(s["V"], 16)
                sp.dma_start(v_p.rearrange("(a p) n -> p a n", p=128), V[:, :, :]).then_inc(s["vout"], 16)
                store_tile(0, 128, k_p, lf_p, rows(0, 128))
                load_P(1, 128)
                store_o(0, 128)
                with sp.Fori(1, TILES - 1) as t:
                    store_tile(t, 128, k_p, lf_p, rows(t, 128))
                    load_P(t + 1, 128)
                    store_o(t, 128)
                t = TILES - 1
                store_tile(t, 128, k_p, lf_p, rows(t, 128))
                load_P(TILES, SAMPLE_T)
                load_mem(cmk, cmv, True)
                store_o(t, 128)
                sp.wait_ge(s["S2"], TILES)
                sp.dma_start(st_p.rearrange("h d e -> d h e"), S[0][:, :, :]).then_inc(s["sout"], 16)
                sp.wait_ge(s["sout"], 16)
                sp.dma_start(S[0][:, :, :], state0.rearrange("h d e -> d h e")).then_inc(s["S0"], 16)
                sp.wait_ge(s["vout"], 16)
                sp.wait_ge(s_pv[0], pv_base(TILES) + 1)
                sp.wait_ge(s_pv[1], pv_base(TILES) + 1)
                sp.dma_start(V[:, 0:PAST_TILES, :], cv.rearrange("(a p) n -> p a n", p=128)).then_inc(s["V"], 16)
                sp.dma_start(V[:SAMPLE_T, PAST_TILES, :], proj[SEQ:TOKENS, FV:FV + BW]).then_inc(s["V"], 16)
                for u in range(PAST_TILES):
                    sp.wait_ge(s["trk"], TILES + u)
                    sp.wait_ge(s["cum"], TILES + u)
                    if u == 0:
                        sp.wait_ge(s["kout"], 16 * TILES)
                        sp.wait_ge(s["lfout"], 16 * TILES)
                    sp.dma_start(k_aug[:, :, 0:FD], h3(ck[rows(u, 128), :], FH)).then_inc(s["ck"], 16)
                    sp.dma_start(ls[:, 256:264], clf[rows(u, 128), :]).then_inc(s["ck"], 16)
                sp.wait_ge(s["V"], 48)
                sp.dma_start(v_s, V[:SAMPLE_T, PAST_TILES, :]).then_inc(s["vout"], 16)
                store_tile(TILES, SAMPLE_T, k_s, lf_s, slice(0, SAMPLE_T))
                sp.wait_ge(s["S1"], TILES + 1)
                sp.dma_start(st_s.rearrange("h d e -> d h e"), S[1][:, :, :]).then_inc(s["sout"], 16)
                store_o(TILES, SAMPLE_T)
                for k in range(3):
                    sp.wait_ge(s_oput[k], 16 * (TILES + 2))
                sp.wait_ge(s["sout"], 32)
                sp.wait_ge(s["kout"], 16 * (TILES + 1))
                sp.wait_ge(s["lfout"], 16 * (TILES + 1))
                sp.wait_ge(s["vout"], 32)

            @block.gpsimd
            def _(pool):
                pool.memset(q_aug[:, :, FD:FD + 1], 1.0).then_inc(s["z0"], 1)
                pool.memset(k_aug[:, :, FD + 1:FD + 2], 1.0).then_inc(s["z0"], 1)
                pool.memset(attT[:, :, :], 0.0).then_inc(s["z0"], 1)
                pool.memset(carry[:, :], 0.0).then_inc(s["z0"], 1)
                pool.memset(S[0][:, :, :], 0.0).then_inc(s["z0"], 1)

            @block.tensor
            def _(pe):
                def alone():
                    pe.sem_inc(s["pestep"], 1)

                def forget_sums(u, T, with_gla):
                    pe.matmul(p_y[:T, 0:FH], c.upto[:T, :T], ls[:T, 256:264], start=True, stop=True)
                    mm = nc.tensor.matmul(p_y[:, FH:2 * FH], c.ones[:T, :], ls[:T, 256:264], start=True, stop=True)
                    if with_gla:
                        nc.tensor.matmul(p_x[:T, 0:256], c.upto_chunk[:T, :T], la[:T, :], start=True, stop=True)
                        nc.tensor.matmul(p_x[:T, 256:512], c.after_chunk[:T, :T], la[:T, :], start=True, stop=True)
                        for h in range(GH):
                            mm = nc.tensor.matmul(p_y[:GDK, 16 + 2 * h:18 + 2 * h], la[:T, h * GDK:(h + 1) * GDK],
                                                  c.chunk_of[:T, :], start=True, stop=True)
                    mm.then_inc(s["cum"], 1)

                def keys_transposed(u, T):
                    for h in range(FH):
                        mm = nc.tensor.transpose(p_tr[:AD, h * 128:h * 128 + T], k_aug[:T, h, :], c.ident[:T, :T])
                    mm.then_inc(s["trk"], 1)

                def memory_keys(n):
                    pe.wait_ge(s["mem"], 32 * n + 32)
                    if n:
                        pe.wait_ge(s["oT"], 3 * TILES)
                    for h in range(MH):
                        for a in range(MT):
                            mm = nc.tensor.transpose(p_tr[:, (h * MT + a) * 128:(h * MT + a + 1) * 128],
                                                     mk[:, a, h * MD:(h + 1) * MD], c.ident[:, :])
                    mm.then_inc(s["mkT_mm"], 1)
                    pe.wait_ge(s["mkT"], n + 1)

                def softmax_values(t, n, half, slot, T, Tk):
                    b = pv_base(t)
                    pe.wait_ge(s_p[half], b + n + 1)
                    pe.wait_ge(s_pts[half], b + n + 1)
                    alone()
                    for h in range(HH):
                        hh = half * HH + h
                        mm = nc.tensor.transpose(p_tr[:Tk, hh * 128:hh * 128 + T], PP[:T, hh, :Tk], c.ident[:T, :T])
                    mm.then_inc(s_pt[half], 1)

                def values(t, n, half, slot, T, Tk):
                    b = pv_base(t)
                    pe.wait_ge(s_pts[half], b + n + 2)
                    alone()
                    for h in range(HH):
                        hh = half * HH + h
                        if isinstance(slot, int):
                            v = V[:Tk, slot, hh * FD:(hh + 1) * FD]
                        else:
                            v = V[:Tk, bass.ds(slot, 1), hh * FD:(hh + 1) * FD].squeeze(1)
                        mm = nc.tensor.matmul(p_of[:T, hh * FD:(hh + 1) * FD], PT[:Tk, hh, :T], v,
                                              start=False, stop=True, skip_group_check=True)
                    mm.then_inc(s_pv[half], 1)

                def scores(t, n, half, k0, T, Tk):
                    pe.wait_ge(s_free[half], qk_base(t) + n + 1)
                    alone()
                    for h in range(HH):
                        hh = half * HH + h
                        mm = nc.tensor.matmul(p_h[half][:T, h, :Tk], qT[:, hh, :T], kT[:, hh, bass.ds(k0, Tk)],
                                              start=True, stop=True)
                    mm.then_inc(s_qk[half], 1)

                def tile(t, T, prior, gla_chunks):
                    u = key_step(t)
                    pe.wait_ge(s["P"], 16 * (t + 1))
                    alone()
                    nc.tensor.transpose(p_y[:GRANK, :T], P[:T, GA:GA + GRANK], c.ident[:T, :T])\
                        .then_inc(s["gaT_mm"], 1)
                    pe.wait_ge(s["gaT"], t + 1)
                    alone()
                    nc.tensor.matmul(p_x[:T, 0:256], gaT[:, :T], wa2[:, :], start=True, stop=True)\
                        .then_inc(s["za"], 1)
                    pe.wait_ge(s["la"], t + 1)
                    alone()
                    forget_sums(u, T, True)
                    pe.wait_ge(s["aug"], u + 1)
                    alone()
                    for h in range(FH):
                        mm = nc.tensor.transpose(p_tr[:AD, h * 128:h * 128 + T], q_aug[:T, h, :], c.ident[:T, :T])
                    mm.then_inc(s["trq"], 1)
                    pe.wait_ge(s["qT"], t + 1)
                    alone()
                    keys_transposed(u, T)
                    pe.wait_ge(s["kT"], u + 1)
                    pe.wait_ge(s["qd"], t + 1)
                    alone()
                    for h in range(2 * GH):
                        mm = nc.tensor.transpose(p_tr[:GDK, h * 128:h * 128 + T], qkd[:T, h, :], c.ident[:T, :T])
                    mm.then_inc(s["trg"], 1)
                    pe.wait_ge(s["gT"], t + 1)
                    pe.wait_ge(s["mq"], t + 1)
                    alone()
                    for h in range(MH):
                        mm = nc.tensor.transpose(p_tr[:, h * 128:h * 128 + T], mq[:T, h * MD:(h + 1) * MD],
                                                 c.ident[:T, :T])
                    mm.then_inc(s["trm"], 1)
                    for h in range(GH):
                        mm = nc.tensor.matmul(p_g[:T, h * 128:h * 128 + T], qkdT[:, GH + h, :T], qkdT[:, h, :T],
                                              start=True, stop=True)
                    mm.then_inc(s["att_mm"], 1)
                    for ch in range(gla_chunks):
                        r = slice(ch * CHUNK, (ch + 1) * CHUNK)
                        for h in range(GH):
                            mm = nc.tensor.matmul((p_x, p_y)[ch][:GDK, h * GDV:(h + 1) * GDV], ko[r, h, :],
                                                  P[r, GV + h * GDV:GV + (h + 1) * GDV], start=True, stop=True)
                        mm.then_inc(s["dS"], 1)
                    pe.wait_ge(s["att"], t + 1)
                    if gla_chunks == 2:
                        pe.wait_ge(s["S1"], t + 1)
                    alone()
                    for h in range(GH):
                        o = p_g[:, h * GDV:(h + 1) * GDV]
                        nc.tensor.matmul(o[:T, :], attT[:T, h, :T], P[:T, GV + h * GDV:GV + (h + 1) * GDV],
                                         start=True, stop=False, skip_group_check=True)
                        for ch in range(gla_chunks):
                            r = slice(ch * CHUNK, (ch + 1) * CHUNK)
                            mm = nc.tensor.matmul(o[r, :], qkdT[:, h, r], S[ch][:, h, :], start=False, stop=True,
                                                  skip_group_check=True)
                    mm.then_inc(s["og_mm"], 1)
                    pe.wait_ge(s["mqT"], t + 1)
                    alone()
                    for h in range(MH):
                        mm = nc.tensor.matmul(p_tr[:T, h * NMEM:(h + 1) * NMEM], mqT[:, h, :T], mkT[:, h, :],
                                              start=True, stop=True)
                    mm.then_inc(s["ms_mm"], 1)
                    pe.wait_ge(s["pm"], t + 1)
                    alone()
                    for h in range(MH):
                        for a in range(MT):
                            b = h * MT + a
                            mm = nc.tensor.transpose(p_tr[:, b * 128:b * 128 + T], pm[:T, h, a * 128:(a + 1) * 128],
                                                     c.ident[:T, :T])
                    mm.then_inc(s["trpm"], 1)
                    pe.wait_ge(s["pmT"], t + 1)
                    pe.wait_ge(s["og"], t + 1)
                    alone()
                    for h in range(MH):
                        for a in range(MT):
                            mm = nc.tensor.matmul(p_g[:T, h * MD:(h + 1) * MD], pmT[:, h * MT + a, :T],
                                                  mv[:, a, h * MD:(h + 1) * MD], start=a == 0, stop=a == MT - 1)
                    mm.then_inc(s["om_mm"], 1)
                    for half in range(2):
                        scores(t, 0, half, prior * 128, T, T)
                    if not (isinstance(prior, int) and prior == 0):
                        with pe.Fori(0, prior) as j:
                            for half in range(2):
                                scores(t, j + 1, half, j * 128, T, 128)
                    if not at0(t):
                        pe.wait_ge(s["ofox"], t)
                        alone()
                    nc.tensor.matmul(p_of[:T, :], c.zero_row[:, :T], c.zero_row[:, :], start=True, stop=True)
                    for half in range(2):
                        softmax_values(t, 0, half, prior, T, T)
                    for half in range(2):
                        values(t, 0, half, prior, T, T)
                    if not (isinstance(prior, int) and prior == 0):
                        with pe.Fori(0, prior) as j:
                            for half in range(2):
                                scores(t, prior + j + 1, half, j * 128, T, 128)
                            for half in range(2):
                                softmax_values(t, j + 1, half, j, T, 128)
                            for half in range(2):
                                values(t, j + 1, half, j, T, 128)
                    pe.wait_ge(s["ogl"], t + 1)
                    pe.wait_ge(s["omem"], t + 1)
                    pe.wait_ge(s["ofox"], t + 1)
                    alone()
                    for k in range(3):
                        if k == 2:
                            pe.wait_ge(s["oT"], 3 * t + 1)
                            alone()
                        for b in range(4):
                            col = (k * 4 + b) * 128
                            mm = nc.tensor.transpose(p_tr[:, (k % 2) * 512 + b * 128:(k % 2) * 512 + b * 128 + T],
                                                     o_all[:T, col:col + 128], c.ident[:T, :T])
                        mm.then_inc(s["tro"], 1)
                    pe.wait_ge(s["oT"], 3 * t + 3)
                    alone()

                pe.wait_ge(s["par"], 7 * 16)
                pe.wait_ge(s["V"], 16)
                pe.wait_ge(s["z0"], 5)
                memory_keys(0)
                tile(0, 128, 0, 2)
                with pe.Fori(1, TILES) as t:
                    tile(t, 128, t, 2)
                memory_keys(1)
                for u in range(PAST_TILES):
                    pe.wait_ge(s["ck"], 32 * (u + 1))
                    if u:
                        pe.wait_ge(s["aug"], TILES + u)
                    forget_sums(TILES + u, 128, False)
                    pe.wait_ge(s["aug"], TILES + u + 1)
                    if u:
                        pe.wait_ge(s["kT"], TILES + u)
                    keys_transposed(TILES + u, 128)
                pe.wait_ge(s["kT"], TILES + PAST_TILES)
                pe.wait_ge(s["V"], 48)
                pe.wait_ge(s["S0"], 16)
                tile(TILES, SAMPLE_T, PAST_TILES, 1)

            @block.scalar
            def _(act):
                def tile(t, T, prior, gla_chunks):
                    u = key_step(t)
                    n = [0]

                    def link(ins):
                        n[0] += 1
                        ins.then_inc(s["a"], 1)
                        act.wait_ge(s["a"], n[0])

                    act.wait_ge(s["P"], 16 * (t + 1))
                    act.sem_inc(s["astep"], 1)
                    act.sem_clear(s["a"])
                    nc.scalar.activation(sq[:T, :], P[:T, FQ:FQ + 2 * BW], ACT.Square).then_inc(s["sq"], 1)
                    nc.scalar.activation(sqm[:T, :], P[:T, MQ:MQ + BW], ACT.Square).then_inc(s["sq"], 1)
                    act.wait_ge(s["gaT_mm"], t + 1)
                    nc.scalar.copy(gaT[:, :T], p_y[:GRANK, :T]).then_inc(s["gaT"], 1)
                    act.wait_ge(s["ss"], t + 1)
                    nc.scalar.activation(st[:T, 20:36], st[:T, 0:16], ACT.Sqrt, bias=c.eps[:T, :], scale=1.0 / FD)
                    nc.scalar.activation(st[:T, 36:40], st[:T, 16:20], ACT.Sqrt, bias=c.eps[:T, :], scale=1.0 / MD)\
                        .then_inc(s["std"], 1)
                    act.wait_ge(s["z"], t + 1)
                    link(nc.scalar.activation(za[:T, :], z[:T, :], ACT.Abs))
                    link(nc.scalar.activation(ze[:T, :], za[:T, :], ACT.Exp, scale=-1.0))
                    nc.scalar.activation(zl[:T, :], ze[:T, :], ACT.Ln, bias=c.one[:T, :]).then_inc(s["ln"], 1)
                    nc.scalar.activation(sig[:T, :], P[:T, GG:GG + BW], ACT.Exp, scale=-1.0).then_inc(s["sig"], 1)
                    act.wait_ge(s["cum"], u + 1)
                    nc.scalar.activation(eb[:T, 0, :], p_x[:T, 0:256], ACT.Exp)
                    nc.scalar.activation(eb[:T, 1, :], p_x[:T, 0:256], ACT.Exp, scale=-1.0)
                    nc.scalar.activation(eb[:T, 2, :], p_x[:T, 256:512], ACT.Exp)
                    act.wait_ge(s["aug"], u + 1)
                    nc.scalar.activation(ebl[:, :], p_y[:GDK, 16:24], ACT.Exp).then_inc(s["eb"], 1)
                    act.wait_ge(s["trq"], t + 1)
                    nc.scalar.copy(qT[:, :, :T], p_tr[:AD, :].rearrange("p (h t) -> p h t", h=FH)[:, :, :T])\
                        .then_inc(s["qT"], 1)
                    act.wait_ge(s["trg"], t + 1)
                    nc.scalar.copy(qkdT[:, :, :T], p_tr[:GDK, :].rearrange("p (h t) -> p h t", h=2 * GH)[:, :, :T])\
                        .then_inc(s["gT"], 1)
                    act.wait_ge(s["trm"], t + 1)
                    nc.scalar.copy(mqT[:, :, :T], p_tr[:, 0:512].rearrange("p (h t) -> p h t", h=MH)[:, :, :T])\
                        .then_inc(s["mqT"], 1)
                    act.wait_ge(s["og_mm"], t + 1)
                    nc.scalar.activation(sqm[:T, :], p_g[:T, :], ACT.Square).then_inc(s["gsq"], 1)
                    act.wait_ge(s["gss"], t + 1)
                    nc.scalar.activation(st[:T, 44:48], st[:T, 40:44], ACT.Sqrt, bias=c.eps[:T, :], scale=1.0 / GDV)\
                        .then_inc(s["gstd"], 1)
                    act.wait_ge(s["mmax"], t + 1)
                    for h in range(MH):
                        last = nc.scalar.activation(pm[:T, h, :], p_tr[:T, h * NMEM:(h + 1) * NMEM], ACT.Exp,
                                                    bias=mstat[:T, h:h + 1], accum_out=mstat[:T, MH + h:MH + h + 1])
                    last.then_inc(s["pm"], 1)
                    act.wait_ge(s["trpm"], t + 1)
                    nc.scalar.copy(pmT[:, :, :T], p_tr[:, :].rearrange("p (h t) -> p h t", h=MH * MT)[:, :, :T])\
                        .then_inc(s["pmT"], 1)

                    def exps(n, k, half, src, Tk):
                        b = pv_base(t)
                        act.wait_ge(s_pt[half], b + n + 1)
                        act.wait_ge(s_l[half], b + n + 1)
                        for h in range(HH):
                            hh = half * HH + h
                            last = nc.scalar.activation(PP[:T, hh, :Tk], src[h], ACT.Exp, bias=fmax[:T, 2, hh:hh + 1],
                                                        accum_out=rsum[:T, hh:hh + 1])
                        last.then_inc(s_p[half], 1)

                    act.wait_ge(s["neg"], t + 1)
                    for half in range(2):
                        exps(0, None, half, [diag[:T, half * HH + h, :T] for h in range(HH)], T)
                    if not (isinstance(prior, int) and prior == 0):
                        with act.Fori(0, prior) as j:
                            for half in range(2):
                                act.wait_ge(s_qk[half], qk_base(t) + prior + j + 2)
                                exps(j + 1, None, half, [p_h[half][:T, h, :] for h in range(HH)], 128)
                                act.wait_ge(s_p[half], pv_base(t) + j + 2)
                                act.sem_inc(s_free[half], 1)
                    for k in range(3):
                        act.wait_ge(s["tro"], 3 * t + k + 1)
                        act.wait_ge(s_oput[k], 16 * (t + 1))
                        nc.scalar.copy(oT[k][:, :, :T],
                                       p_tr[:, (k % 2) * 512:(k % 2) * 512 + 512]
                                       .rearrange("p (h t) -> p h t", h=4)[:, :, :T]).then_inc(s["oT"], 1)

                def memory_keys(n):
                    act.wait_ge(s["mkT_mm"], n + 1)
                    nc.scalar.copy(mkT[:, :, :].rearrange("p h k -> p (h k)"), p_tr[:, :]).then_inc(s["mkT"], 1)

                for half in range(2):
                    act.sem_inc(s_l[half], 1)
                    act.sem_inc(s_pt[half], 1)
                for k in range(3):
                    act.sem_inc(s_oput[k], 16)
                memory_keys(0)
                tile(0, 128, 0, 2)
                with act.Fori(1, TILES) as t:
                    tile(t, 128, t, 2)
                memory_keys(1)
                tile(TILES, SAMPLE_T, PAST_TILES, 1)

            @block.vector
            def _(dve):
                def sums_added(u, T, link):
                    link(nc.vector.tensor_tensor(out=cs[:T, :], in0=p_y[:T, 0:FH], in1=carry[:T, :], op=ALU.add))
                    nc.vector.tensor_copy(q_aug[:T, :, FD + 1], cs[:T, :])
                    nc.vector.tensor_scalar(out=k_aug[:T, :, FD], in0=cs[:T, :], scalar1=-1.0, scalar2=None,
                                            op0=ALU.mult)
                    link(nc.vector.tensor_tensor(out=carry[:, :], in0=p_y[:, FH:2 * FH], in1=carry[:, :],
                                                 op=ALU.add))

                def tile(t, T, prior, gla_chunks):
                    u = key_step(t)
                    n = [0]

                    def link(ins):
                        n[0] += 1
                        ins.then_inc(s["d"], 1)
                        dve.wait_ge(s["d"], n[0])

                    def bc(col, h, d):
                        return st[:T, col:col + h].unsqueeze(2).broadcast_to([T, h, d])

                    dve.wait_ge(s["sq"], 2 * (t + 1))
                    dve.sem_inc(s["dstep"], 1)
                    dve.sem_clear(s["d"])
                    nc.vector.tensor_reduce(out=st[:T, 0:16], in_=h3(sq[:T, :], 2 * FH), axis=AX.X, op=ALU.add)
                    nc.vector.tensor_reduce(out=st[:T, 16:20], in_=h3(sqm[:T, :], MH), axis=AX.X, op=ALU.add)\
                        .then_inc(s["ss"], 1)
                    nc.vector.tensor_tensor(out=z[:T, 256:264], in0=P[:T, FF:FF + FH], in1=bf_bc[:T, :], op=ALU.add)
                    dve.wait_ge(s["za"], t + 1)
                    nc.vector.tensor_tensor(out=z[:T, 0:256], in0=p_x[:T, 0:256], in1=ba_bc[:T, :], op=ALU.add)\
                        .then_inc(s["z"], 1)
                    dve.wait_ge(s["std"], t + 1)
                    link(nc.vector.reciprocal(st[:T, 20:40], st[:T, 20:40]))
                    link(nc.vector.tensor_tensor(out=h3(tmp[:T, :], FH), in0=h3(P[:T, FK:FK + BW], FH),
                                                 in1=bc(28, FH, FD), op=ALU.mult))
                    if not at0(t):
                        dve.wait_ge(s["trk"], u)
                        dve.wait_ge(s["kout"], 16 * t)
                    nc.vector.tensor_tensor(out=k_aug[:T, :, 0:FD], in0=h3(tmp[:T, :], FH),
                                            in1=gk_bc[:T, :].unsqueeze(1).broadcast_to([T, FH, FD]), op=ALU.mult)\
                        .then_inc(s["kn"], 1)
                    dve.wait_ge(s["kn"], t + 1)
                    link(nc.vector.tensor_tensor(out=h3(tmp[:T, :], FH), in0=h3(P[:T, FQ:FQ + BW], FH),
                                                 in1=bc(20, FH, FD), op=ALU.mult))
                    link(nc.vector.tensor_tensor(out=q_aug[:T, :, 0:FD], in0=h3(tmp[:T, :], FH),
                                                 in1=gq_bc[:T, :].unsqueeze(1).broadcast_to([T, FH, FD]),
                                                 op=ALU.mult))
                    link(nc.vector.tensor_tensor(out=h3(tmp[:T, :], MH), in0=h3(P[:T, MQ:MQ + BW], MH),
                                                 in1=bc(36, MH, MD), op=ALU.mult))
                    nc.vector.tensor_tensor(out=h3(mq[:T, :], MH), in0=h3(tmp[:T, :], MH),
                                            in1=gm_bc[:T, :].unsqueeze(1).broadcast_to([T, MH, MD]), op=ALU.mult)\
                        .then_inc(s["mq"], 1)
                    dve.wait_ge(s["ln"], t + 1)
                    if not at0(t):
                        dve.wait_ge(s["lfout"], 16 * t)
                        dve.sem_inc(s["dstep"], 1)
                    link(nc.vector.scalar_tensor_tensor(out=ls[:T, :], in0=z[:T, :], scalar=0.0, in1=zl[:T, :],
                                                        op0=ALU.min, op1=ALU.subtract))
                    nc.vector.tensor_scalar(out=la[:T, :], in0=ls[:T, 0:256], scalar1=1.0 / GLA_TAU, scalar2=None,
                                            op0=ALU.mult).then_inc(s["la"], 1)
                    dve.wait_ge(s["cum"], u + 1)
                    sums_added(u, T, link)
                    dve.sem_inc(s["aug"], 1)
                    dve.wait_ge(s["eb"], t + 1)
                    nc.vector.scalar_tensor_tensor(out=qkd[:T, 0:GH, :].rearrange("p h d -> p (h d)"),
                                                   in0=P[:T, GQ:GQ + 256], scalar=GDK ** -0.5, in1=eb[:T, 0, :],
                                                   op0=ALU.mult, op1=ALU.mult)
                    nc.vector.tensor_tensor(out=qkd[:T, GH:2 * GH, :].rearrange("p h d -> p (h d)"),
                                            in0=P[:T, GK:GK + 256], in1=eb[:T, 1, :], op=ALU.mult)
                    nc.vector.tensor_tensor(out=ko[:T, :, :].rearrange("p h d -> p (h d)"),
                                            in0=P[:T, GK:GK + 256], in1=eb[:T, 2, :], op=ALU.mult)\
                        .then_inc(s["qd"], 1)
                    dve.wait_ge(s["trk"], u + 1)
                    nc.vector.tensor_copy(kT[:, :, bass.ds(prior * 128, T)],
                                          p_tr[:AD, :].rearrange("p (h t) -> p h t", h=FH)[:, :, :T])\
                        .then_inc(s["kT"], 1)
                    dve.wait_ge(s["att_mm"], t + 1)
                    dve.sem_inc(s["dstep"], 1)
                    for h in range(GH):
                        last = nc.vector.copy_predicated(attT[:T, h, :T], c.upto_chunk[:T, :T].bitcast(I32),
                                                         p_g[:T, h * 128:h * 128 + T])
                    last.then_inc(s["att"], 1)
                    if gla_chunks == 2:
                        dve.wait_ge(s["dS"], 2 * t + 1)
                    else:
                        dve.wait_ge(s["dS"], 2 * TILES + 1)
                        dve.wait_ge(s["S0"], 16)
                    if not at0(t):
                        dve.wait_ge(s["og_mm"], t)
                    for h in range(GH):
                        last = nc.vector.scalar_tensor_tensor(
                            out=S[1][:, h, :], in0=S[0][:, h, :], scalar=ebl[:, 2 * h:2 * h + 1],
                            in1=p_x[:GDK, h * GDV:(h + 1) * GDV], op0=ALU.mult, op1=ALU.add)
                    last.then_inc(s["S1"], 1)
                    dve.wait_ge(s["gsq"], t + 1)
                    nc.vector.tensor_reduce(out=st[:T, 40:44], in_=h3(sqm[:T, :], GH), axis=AX.X, op=ALU.add)\
                        .then_inc(s["gss"], 1)
                    if gla_chunks == 2:
                        dve.wait_ge(s["dS"], 2 * t + 2)
                        dve.wait_ge(s["S1"], t + 1)
                        dve.wait_ge(s["og_mm"], t + 1)
                        for h in range(GH):
                            last = nc.vector.scalar_tensor_tensor(
                                out=S[0][:, h, :], in0=S[1][:, h, :], scalar=ebl[:, 2 * h + 1:2 * h + 2],
                                in1=p_y[:GDK, h * GDV:(h + 1) * GDV], op0=ALU.mult, op1=ALU.add)
                        last.then_inc(s["S2"], 1)
                        dve.wait_ge(s["S2"], t + 1)
                    dve.wait_ge(s["gstd"], t + 1)
                    link(nc.vector.reciprocal(st[:T, 48:52], st[:T, 44:48]))
                    nc.vector.tensor_tensor(out=h3(tmp[:T, :], GH), in0=h3(p_g[:T, :], GH), in1=bc(48, GH, GDV),
                                            op=ALU.mult).then_inc(s["og"], 1)
                    dve.wait_ge(s["og"], t + 1)
                    link(nc.vector.tensor_tensor(out=h3(tmp[:T, :], GH), in0=h3(tmp[:T, :], GH),
                                                 in1=go_bc[:T, :].unsqueeze(1).broadcast_to([T, GH, GDV]),
                                                 op=ALU.mult))
                    dve.wait_ge(s["sig"], t + 1)
                    dve.sem_inc(s["dstep"], 1)
                    link(nc.vector.tensor_scalar(out=sig[:T, :], in0=sig[:T, :], scalar1=1.0, scalar2=None,
                                                 op0=ALU.add))
                    link(nc.vector.reciprocal(sig[:T, :], sig[:T, :]))
                    link(nc.vector.tensor_tensor(out=sig[:T, :], in0=sig[:T, :], in1=P[:T, GG:GG + BW],
                                                 op=ALU.mult))
                    nc.vector.tensor_tensor(out=o_all[:T, 0:BW], in0=tmp[:T, :], in1=sig[:T, :], op=ALU.mult)\
                        .then_inc(s["ogl"], 1)
                    dve.wait_ge(s["ms_mm"], t + 1)
                    nc.vector.tensor_reduce(out=mstat[:T, 0:MH], in_=h3(p_tr[:T, :], MH), axis=AX.X, op=ALU.max,
                                            negate=True).then_inc(s["mmax"], 1)
                    dve.wait_ge(s["pm"], t + 1)
                    link(nc.vector.reciprocal(mstat[:T, 2 * MH:3 * MH], mstat[:T, MH:2 * MH]))
                    dve.wait_ge(s["om_mm"], t + 1)
                    nc.vector.tensor_tensor(out=h3(o_all[:T, 2 * BW:3 * BW], MH), in0=h3(p_g[:T, :], MH),
                                            in1=mstat[:T, 2 * MH:3 * MH].unsqueeze(2).broadcast_to([T, MH, MD]),
                                            op=ALU.mult).then_inc(s["omem"], 1)
                    for half in range(2):
                        hs = slice(half * HH, half * HH + HH)
                        dve.wait_ge(s_qk[half], qk_base(t) + 1)
                        nc.vector.tensor_tensor(out=diag[:T, hs, :T], in0=p_h[half][:T, :, :T],
                                                in1=c.future[:T, :T].unsqueeze(1).broadcast_to([T, HH, T]),
                                                op=ALU.add).then_inc(s["dg"], 1)
                        dve.wait_ge(s["dg"], 2 * t + half + 1)
                        dve.sem_inc(s_free[half], 1)
                        link(nc.vector.tensor_reduce(out=fmax[:T, 0, hs], in_=diag[:T, hs, :T], axis=AX.X,
                                                     op=ALU.max))
                    if not (isinstance(prior, int) and prior == 0):
                        with dve.Fori(0, prior) as j:
                            dve.sem_clear(s["e"])
                            for half in range(2):
                                hs = slice(half * HH, half * HH + HH)
                                dve.wait_ge(s_qk[half], qk_base(t) + j + 2)
                                nc.vector.tensor_reduce(out=fmax[:T, 1, hs], in_=p_h[half][:T, :, :], axis=AX.X,
                                                        op=ALU.max).then_inc(s["e"], 1)
                                dve.wait_ge(s["e"], 2 * half + 1)
                                dve.sem_inc(s_free[half], 1)
                                nc.vector.tensor_tensor(out=fmax[:T, 0, hs], in0=fmax[:T, 0, hs],
                                                        in1=fmax[:T, 1, hs], op=ALU.max).then_inc(s["e"], 1)
                                dve.wait_ge(s["e"], 2 * half + 2)
                    nc.vector.memset(lsum[:T, :], 0.0).then_inc(s["ls0"], 1)
                    nc.vector.tensor_scalar(out=fmax[:T, 2, :], in0=fmax[:T, 0, :], scalar1=-1.0, scalar2=None,
                                            op0=ALU.mult).then_inc(s["neg"], 1)
                    dve.wait_ge(s["ls0"], t + 1)

                    def evacuate(n, half, Tk):
                        b = pv_base(t)
                        hs = slice(half * HH, half * HH + HH)
                        dve.wait_ge(s_p[half], b + n + 1)
                        nc.vector.tensor_tensor(out=lsum[:T, hs], in0=lsum[:T, hs], in1=rsum[:T, hs], op=ALU.add)\
                            .then_inc(s_l[half], 1)
                        dve.wait_ge(s_pt[half], b + n + 2)
                        dve.wait_ge(s_pv[half], b + n + 1)
                        dve.wait_ge(s_l[half], b + n + 2)
                        nc.vector.tensor_copy(
                            PT[:Tk, hs, :T],
                            p_tr[:Tk, half * 512:half * 512 + 512].rearrange("p (h t) -> p h t", h=HH)[:, :, :T])\
                            .then_inc(s_pts[half], 1)

                    for half in range(2):
                        evacuate(0, half, T)
                    if not (isinstance(prior, int) and prior == 0):
                        with dve.Fori(0, prior) as j:
                            for half in range(2):
                                evacuate(j + 1, half, 128)
                    dve.wait_ge(s_l[1], pv_base(t) + prior + 2)
                    link(nc.vector.reciprocal(rl[:T, :], lsum[:T, :]))
                    dve.wait_ge(s_pv[0], pv_base(t) + prior + 2)
                    dve.wait_ge(s_pv[1], pv_base(t) + prior + 2)
                    nc.vector.tensor_tensor(out=h3(o_all[:T, BW:2 * BW], FH), in0=h3(p_of[:T, :], FH),
                                            in1=rl[:T, :].unsqueeze(2).broadcast_to([T, FH, FD]), op=ALU.mult)\
                        .then_inc(s["ofox"], 1)
                    dve.wait_ge(s["oT"], 3 * t + 3)
                    dve.sem_inc(s["dstep"], 1)

                for half in range(2):
                    dve.sem_inc(s_free[half], 1)
                    dve.sem_inc(s_pts[half], 1)
                    dve.sem_inc(s_pv[half], 1)
                dve.wait_ge(s["par"], 7 * 16)
                dve.wait_ge(s["z0"], 5)
                nc.vector.tensor_scalar(out=gq_bc[:, :], in0=gq_bc[:, :], scalar1=FD ** -0.5, scalar2=None,
                                        op0=ALU.mult).then_inc(s["gq"], 1)
                nc.vector.tensor_scalar(out=gm_bc[:, :], in0=gm_bc[:, :], scalar1=MD ** -0.5, scalar2=None,
                                        op0=ALU.mult).then_inc(s["gq"], 1)
                dve.wait_ge(s["gq"], 2)
                tile(0, 128, 0, 2)
                with dve.Fori(1, TILES) as t:
                    tile(t, 128, t, 2)
                nc.vector.memset(carry[:, :], 0.0).then_inc(s["carry"], 1)
                dve.wait_ge(s["carry"], 1)
                dve.sem_clear(s["d"])
                n = [0]

                def link(ins):
                    n[0] += 1
                    ins.then_inc(s["d"], 1)
                    dve.wait_ge(s["d"], n[0])

                for u in range(PAST_TILES):
                    dve.wait_ge(s["cum"], TILES + u + 1)
                    dve.wait_ge(s["ck"], 32 * (u + 1))
                    sums_added(TILES + u, 128, link)
                    dve.sem_inc(s["aug"], 1)
                    dve.wait_ge(s["trk"], TILES + u + 1)
                    nc.vector.tensor_copy(kT[:, :, u * 128:(u + 1) * 128],
                                          p_tr[:AD, :].rearrange("p (h t) -> p h t", h=FH)).then_inc(s["kT"], 1)
                tile(TILES, SAMPLE_T, PAST_TILES, 1)
        m.retire()


def gated_mix(nc, c, hT_spill, oT_spill, w_gate, w_br, mixT):
    SPANS = [(0, 364), (364, 364), (728, 360)]
    assert sum(n for _, n in SPANS) == TOKENS
    UN = 2 * BRANCHES * len(SPANS)
    GW, BRW = DT * 128, 4 * 128
    with ExitStack() as ctx:
        m = Scope(nc, ctx, "gate")
        hT = m.sb("hT", [128, DT, TOKENS])
        oT = m.sb("oT", [128, BRANCHES * 4, TOKENS])
        wg = [m.sb(f"wg{k}", [128, BRANCHES, DT, 128]) for k in range(2)]
        wb = [m.sb(f"wb{k}", [128, BRANCHES, 4, 128]) for k in range(2)]
        sg = [m.sb(f"sg{k}", [128, 364]) for k in range(3)]
        part = [m.sb(f"part{k}", [128, 364]) for k in range(3)]
        acc = [m.sb(f"acc{k}", [128, 364]) for k in range(3)]
        p_g = [m.pb(f"p_g{k}", [128, 512]) for k in range(3)]
        p_b = [m.pb(f"p_b{k}", [128, 512]) for k in range(3)]
        s_h, s_o, s_mm, s_sg, s_pr, s_part, s_step = (m.sem(n) for n in (
            "s_h", "s_o", "s_mm", "s_sg", "s_pr", "s_part", "s_step"))
        s_w = [m.sem(f"s_w{k}") for k in range(2)]

        def units():
            for v in range(UN):
                yield v, v // 9, (v // 3) % 3, v % 3

        with nc.Block() as block:
            @block.sync
            def _(sp):
                def load(k, dd):
                    if isinstance(dd, int):
                        g, b = w_gate[dd], w_br[dd]
                    else:
                        g, b = w_gate[bass.ds(dd, 1)].squeeze(0), w_br[bass.ds(dd, 1)].squeeze(0)
                    sp.dma_start(wg[k][:, :, :, :].rearrange("p n k m -> p (n k m)"), g).then_inc(s_w[k], 16)
                    sp.dma_start(wb[k][:, :, :, :].rearrange("p n k m -> p (n k m)"), b).then_inc(s_w[k], 16)

                load(0, 0)
                sp.dma_start(hT[:, :, :], hT_spill.rearrange("p (a b) -> p a b", a=DT)).then_inc(s_h, 16)
                for k in range(BRANCHES):
                    sp.dma_start(oT[:, 4 * k:4 * k + 4, :], oT_spill[k]).then_inc(s_o, 16)
                load(1, 1)
                with sp.Fori(1, DT // 2) as b:
                    for k in range(2):
                        sp.wait_ge(s_mm, b * UN - UN + 9 * (k + 1))
                        load(k, b * 2 + k)

            @block.tensor
            def _(pe):
                pe.wait_ge(s_h, 16)
                pe.wait_ge(s_o, 48)
                with pe.Fori(0, DT // 2) as b:
                    for v, e, n, tc in units():
                        t0, N = SPANS[tc]
                        if n == 0 and tc == 0:
                            pe.wait_ge(s_w[e], 32 * (b + 1))
                        pe.wait_ge(s_sg, b * UN + v + 1)
                        pe.wait_ge(s_pr, b * UN + v + 1)
                        pe.sem_inc(s_step, 1)
                        for k in range(DT):
                            nc.tensor.matmul(p_g[tc][:, :N], wg[e][:, n, k, :], hT[:, k, t0:t0 + N],
                                             start=k == 0, stop=k == DT - 1)
                        for k in range(4):
                            mm = nc.tensor.matmul(p_b[tc][:, :N], wb[e][:, n, k, :], oT[:, 4 * n + k, t0:t0 + N],
                                                  start=k == 0, stop=k == 3)
                        mm.then_inc(s_mm, 1)

            @block.scalar
            def _(act):
                act.sem_inc(s_sg, 3)
                with act.Fori(0, DT // 2) as b:
                    for v, e, n, tc in units():
                        N = SPANS[tc][1]
                        act.wait_ge(s_mm, b * UN + v + 1)
                        act.wait_ge(s_pr, b * UN + v + 1)
                        nc.scalar.activation(sg[tc][:, :N], p_g[tc][:, :N], ACT.Sigmoid).then_inc(s_sg, 1)

            @block.vector
            def _(dve):
                dve.sem_inc(s_pr, 3)
                with dve.Fori(0, DT // 2) as b:
                    for v, e, n, tc in units():
                        t0, N = SPANS[tc]
                        dve.wait_ge(s_sg, b * UN + v + 4)
                        to = acc if n == 0 else part
                        nc.vector.tensor_tensor(out=to[tc][:, :N], in0=sg[tc][:, :N], in1=p_b[tc][:, :N],
                                                op=ALU.mult).then_inc(s_pr, 1)
                        dve.wait_ge(s_pr, b * UN + v + 4)
                        if n:
                            out = acc[tc][:, :N]
                            if n == BRANCHES - 1:
                                out = mixT[:, bass.ds(b * 2 + e, 1), t0:t0 + N].squeeze(1)
                            nc.vector.tensor_tensor(out=out, in0=acc[tc][:, :N], in1=part[tc][:, :N], op=ALU.add)\
                                .then_inc(s_part, 1)
                            dve.wait_ge(s_part, (b * 2 + e) * 6 + (n - 1) * 3 + tc + 1)
        m.retire()


def output_projection(nc, c, x_all, w_out, mixT, x1):
    with ExitStack() as ctx:
        m = Scope(nc, ctx, "out")
        w = m.sb("w", [128, DT, D])
        mt = [m.sb(f"mt{k}", [128, DT, 128]) for k in range(2)]
        x = [m.sb(f"x{k}", [128, D]) for k in range(2)]
        y = [m.sb(f"y{k}", [128, D]) for k in range(2)]
        p_o = [m.pb(f"p_o{k}", [128, D]) for k in range(2)]
        s_w, s_mt, s_mm, s_y, s_yfree, s_step = (m.sem(n) for n in (
            "s_w", "s_mt", "s_mm", "s_y", "s_yfree", "s_step"))
        s_x = [m.sem(f"s_x{k}") for k in range(2)]
        s_put = [m.sem(f"s_put{k}") for k in range(2)]

        with nc.Block() as block:
            @block.sync
            def _(sp):
                def load(k, t, T):
                    sp.dma_start(x[k][:T, :], x_all[rows(t, T), :]).then_inc(s_x[k], 16)

                def store(k, t, T):
                    sp.wait_ge(s_y, t + 1)
                    sp.dma_start(x1[rows(t, T), :], y[k][:T, :]).then_inc(s_put[k], 16)

                for k in range(2):
                    load(k, k, 128)
                for half in range(2):
                    sp.dma_start(w[:, half * 4:half * 4 + 4, :],
                                 w_out[half * 512:(half + 1) * 512, :].rearrange("(a p) n -> p a n", p=128))\
                        .then_inc(s_w, 16)
                with sp.Fori(0, TILES // 2 - 1) as b:
                    for k in range(2):
                        store(k, b * 2 + k, 128)
                        load(k, b * 2 + k + 2, 128)
                store(0, TILES - 2, 128)
                load(0, TILES, SAMPLE_T)
                store(1, TILES - 1, 128)
                store(0, TILES, SAMPLE_T)
                sp.wait_ge(s_put[0], 16 * (TILES // 2 + 1) + 16)
                sp.wait_ge(s_put[1], 16 * (TILES // 2) + 16)

            @block.scalar
            def _(act):
                for k in range(2):
                    act.sem_inc(s_put[k], 16)
                act.sem_inc(s_mm, 2)

                def take(k, t, T):
                    act.wait_ge(s_mm, t + 1)
                    nc.scalar.copy(mt[k][:, :, :T], mixT[:, :, bass.ds(t * 128, T)]).then_inc(s_mt, 1)

                with act.Fori(0, TILES // 2) as b:
                    for k in range(2):
                        take(k, b * 2 + k, 128)
                take(0, TILES, SAMPLE_T)

            @block.tensor
            def _(pe):
                pe.wait_ge(s_w, 32)

                def product(k, t, T):
                    pe.wait_ge(s_mt, t + 1)
                    pe.wait_ge(s_yfree, t + 1)
                    pe.sem_inc(s_step, 1)
                    for n in range(2):
                        for dt in range(DT):
                            mm = nc.tensor.matmul(p_o[k][:T, n * 512:(n + 1) * 512], mt[k][:, dt, :T],
                                                  w[:, dt, n * 512:(n + 1) * 512], start=dt == 0, stop=dt == DT - 1)
                    mm.then_inc(s_mm, 1)

                with pe.Fori(0, TILES // 2) as b:
                    for k in range(2):
                        product(k, b * 2 + k, 128)
                product(0, TILES, SAMPLE_T)

            @block.vector
            def _(dve):
                dve.sem_inc(s_yfree, 2)

                def add(k, t, T):
                    dve.wait_ge(s_mm, t + 3)
                    dve.wait_ge(s_x[k], (t - k) * 8 + 16)
                    dve.wait_ge(s_put[k], (t - k) * 8 + 16)
                    nc.vector.tensor_tensor(out=y[k][:T, :], in0=p_o[k][:T, :], in1=x[k][:T, :], op=ALU.add)\
                        .then_inc(s_y, 1)
                    dve.wait_ge(s_y, t + 1)
                    dve.sem_inc(s_yfree, 1)

                with dve.Fori(0, TILES // 2) as b:
                    for k in range(2):
                        add(k, b * 2 + k, 128)
                add(0, TILES, SAMPLE_T)
        m.retire()


def peer(nc, c, x1, g_ffn, w_qT, sub_kT, uv, y):
    HEADS, TOPK, NK = 8, 16, 128
    SLOTS = 16
    RING = 8
    GROUP = 2
    NG = SLOTS // GROUP
    NEG = -3.0e38

    ctx = ExitStack()
    with ctx:
        m = Scope(nc, ctx, "peer")
        sb, pb, sem = m.sb, m.pb, m.sem
        ident, iota16, eps_col = c.ident, c.iota16, c.eps

        gf_bc = sb("gf_bc", [128, D])
        skT = sb("skT", [128, 16, NK])
        wq_buf = [sb(f"wq_buf{j}", [128, D]) for j in range(2)]
        route_w = sb("route_w", [128, DT, 16 * NK])
        x_tile = sb("x_tile", [128, D])
        x_res = sb("x_res", [128, D])
        h_next = sb("h_next", [128, D])
        h_cur = sb("h_cur", [128, D])
        hT = sb("hT", [128, DT, 128])
        junk_a = sb("junk_a", [128, D])
        stat = sb("stat", [128, 4])
        sc = sb("sc", [128, 256])
        sc_rep = sb("sc_rep", [128, 256])
        v16 = sb("v16", [128, 2, TOPK])
        i16 = sb("i16", [128, 2, TOPK], U32)
        i16f = sb("i16f", [128, 2, TOPK])
        cand = sb("cand", [128, TOPK * TOPK])
        cand_rep = sb("cand_rep", [128, TOPK * TOPK])
        top = sb("top", [128, TOPK])
        pos = sb("pos", [128, TOPK], U32)
        posab = sb("posab", [128, 2, TOPK], U32)
        posabf = sb("posabf", [128, 2, TOPK])
        onehot = sb("onehot", [128, 2, TOPK, TOPK])
        isel = sb("isel", [128, 2, TOPK])
        smx = sb("smx", [128, 4])
        ex = sb("ex", [128, TOPK])
        idx_all = sb("idx_all", [128, HEADS * TOPK], U32)
        g_all = sb("g_all", [128, HEADS * TOPK])
        idx_now = sb("idx_now", [128, SLOTS], U32)
        g_now = sb("g_now", [128, SLOTS])
        dots = sb("dots", [128, SLOTS])
        gel = sb("gel", [128, SLOTS])
        wgt = sb("wgt", [128, SLOTS])
        diag = sb("diag", [128, RING, 128])
        ring = sb("ring", [128, RING, 2 * D])
        ysb = sb("ysb", [128, D])

        p_y = pb("p_y", [128, D])
        p_s = pb("p_s", [128, 512])
        p_t = pb("p_t", [128, D])

        s_gf = sem("s_gf")
        s_sk = sem("s_sk")
        s_wq = [sem(f"s_wq{j}") for j in range(2)]
        s_rw_mm = sem("s_rw_mm")
        s_rw = sem("s_rw")
        s_x = sem("s_x")
        s_xres = sem("s_xres")
        s_sq = sem("s_sq")
        s_std = sem("s_std")
        s_h = sem("s_h")
        s_rstd = sem("s_rstd")
        s_hcur = sem("s_hcur")
        s_tr = sem("s_tr")
        s_hT = sem("s_hT")
        s_res = sem("s_res")
        s_scores = sem("s_scores")
        s_sc = sem("s_sc")
        s_sfree = sem("s_sfree")
        s_top = sem("s_top")
        s_ex = sem("s_ex")
        s_idx = sem("s_idx")
        s_idxcp = sem("s_idxcp")
        s_gcp = sem("s_gcp")
        s_slot = [sem(f"s_slot{j}") for j in range(RING)]
        s_dot = sem("s_dot")
        s_diag = sem("s_diag")
        s_vdone = sem("s_vdone")
        s_yev = sem("s_yev")
        s_out = sem("s_out")
        s_dch = sem("s_dch")
        s_ach = sem("s_ach")
        s_step = {e: sem(f"s_step_{k}") for k, e in (("dve", nc.vector), ("pe", nc.tensor), ("pool", nc.gpsimd))}

        block = ctx.enter_context(nc.Block())

        def apart(eng):
            eng.sem_inc(s_step[eng], 1)

        @block.sync
        def _(sp):
            sp.dma_start(gf_bc[:, :], g_ffn[0:1, :].broadcast_to([128, D])).then_inc(s_gf, 16)
            sp.dma_start(skT[:, :, :], sub_kT.rearrange("h c k -> c h k")).then_inc(s_sk, 16)
            for j in range(2):
                sp.dma_start(wq_buf[j][:, :], w_qT[j * 128:(j + 1) * 128, :]).then_inc(s_wq[j], 16)
            with sp.Fori(1, 8) as pair:
                for j in range(2):
                    sp.wait_ge(s_rw_mm, pair * 2 + j - 1)
                    sp.dma_start(wq_buf[j][:, :], w_qT[bass.ds((pair * 2 + j) * 128, 128), :]).then_inc(s_wq[j], 16)

            def load_x(tile, T):
                if not (isinstance(tile, int) and tile == 0):
                    sp.wait_ge(s_h, tile)
                sp.dma_start(x_tile[:T, :], x1[rows(tile, T), :]).then_inc(s_x, 16)

            def load_res(tile, T):
                if not (isinstance(tile, int) and tile == 0):
                    sp.wait_ge(s_res, tile)
                sp.dma_start(x_res[:T, :], x1[rows(tile, T), :]).then_inc(s_xres, 16)

            def store_y(tile, T):
                sp.wait_ge(s_yev, 2 * (tile + 2))
                sp.dma_start(y[rows(tile, T), :], ysb[:T, :]).then_inc(s_out, 16)

            load_x(0, 128)
            load_res(0, 128)
            load_x(1, 128)
            load_res(1, 128)
            with sp.Fori(0, TILES - 2) as i:
                load_x(i + 2, 128)
                store_y(i, 128)
                load_res(i + 2, 128)
            load_x(TILES, SAMPLE_T)
            store_y(TILES - 2, 128)
            load_res(TILES, SAMPLE_T)
            store_y(TILES - 1, 128)
            store_y(TILES, SAMPLE_T)
            sp.wait_ge(s_out, 16 * (TILES + 2))

        @block.gpsimd
        def _(pool):
            def gather_head(tile, r, T):
                n = tile * HEADS + r
                pool.wait_ge(s_idx, n + 1)
                for half in range(2):
                    c = half * RING
                    pool.tensor_copy(idx_now[:T, c:c + RING],
                                     idx_all[:T, bass.ds(r * TOPK + c, RING)]).then_inc(s_idxcp, 1)
                    pool.wait_ge(s_idxcp, 2 * n + half + 1)
                    for j in range(RING):
                        if j % GROUP == 0:
                            k = n * NG + half * (RING // GROUP) + j // GROUP - RING // GROUP + 1
                            first = isinstance(n, int) and k <= 0
                            if not first:
                                pool.wait_ge(s_vdone, k)
                                apart(pool)
                        nc.gpsimd.indirect_dma_start(
                            out=ring[:T, j, :], out_offset=None, in_=uv[:, :],
                            in_offset=bass.IndirectOffsetOnAxis(ap=idx_now[:T, c + j:c + j + 1], axis=0)
                        ).then_inc(s_slot[j], 16)

            gather_head(0, 0, 128)
            with pool.Fori(1, HEADS) as r:
                gather_head(0, r, 128)
            with pool.Fori(1, TILES) as i:
                with pool.Fori(0, HEADS) as r:
                    gather_head(i, r, 128)
            with pool.Fori(0, HEADS) as r:
                gather_head(TILES, r, SAMPLE_T)

        @block.tensor
        def _(pe):
            pe.wait_ge(s_sk, 16)
            with pe.Fori(0, 8) as pair:
                for j in range(2):
                    hp = pair * 2 + j
                    pe.wait_ge(s_wq[j], (pair + 1) * 16)
                    pe.wait_ge(s_rw, hp + 1)
                    for dt in range(DT):
                        mm = nc.tensor.matmul(p_t[:, dt * 128:(dt + 1) * 128], wq_buf[j][:, dt * 128:(dt + 1) * 128],
                                              skT[:, bass.ds(hp, 1), :].squeeze(1), start=True, stop=True)
                    mm.then_inc(s_rw_mm, 1)
            pe.wait_ge(s_rw, 17)

            def prep(tile, T):
                pe.wait_ge(s_h, tile + 1)
                if not (isinstance(tile, int) and tile == 0):
                    pe.wait_ge(s_hT, tile)
                    apart(pe)
                for dt in range(DT):
                    mm = nc.tensor.transpose(p_t[:, dt * 128:dt * 128 + T], h_next[:T, dt * 128:(dt + 1) * 128],
                                             ident[:T, :T])
                mm.then_inc(s_tr, 1)
                pe.wait_ge(s_hT, tile + 1)
                apart(pe)

            def scores(tile, r, T):
                n = tile * HEADS + r
                pe.wait_ge(s_sc, n + 1)
                apart(pe)
                for dt in range(DT):
                    mm = nc.tensor.matmul(p_s[:T, 0:256], hT[:, dt, :T], route_w[:, dt, bass.ds(r * 256, 256)],
                                          start=dt == 0, stop=dt == DT - 1)
                mm.then_inc(s_scores, 1)

            def residual(tile, T):
                pe.wait_ge(s_yev, 2 * tile + 2)
                pe.wait_ge(s_xres, 16 * (tile + 1))
                apart(pe)
                for c in range(2):
                    mm = nc.tensor.matmul(p_y[:T, c * 512:(c + 1) * 512], ident[:T, :T],
                                          x_res[:T, c * 512:(c + 1) * 512], start=True, stop=True)
                mm.then_inc(s_res, 1)

            def values(tile, r, T, q):
                n = tile * HEADS + r
                pe.wait_ge(s_diag, n * NG + q + 1)
                apart(pe)
                for k in range(GROUP):
                    j = (q * GROUP + k) % RING
                    for c in range(2):
                        mm = nc.tensor.matmul(p_y[:T, c * 512:(c + 1) * 512], diag[:T, j, :T],
                                              ring[:T, j, D + c * 512:D + (c + 1) * 512],
                                              start=False, stop=True, skip_group_check=True)
                mm.then_inc(s_vdone, 1)

            def values_and_scores(tile, r, T, T_next):
                values(tile, r, T, 0)
                scores(tile + 1, r, T_next)
                for q in range(1, NG):
                    values(tile, r, T, q)

            prep(0, 128)
            with pe.Fori(0, HEADS) as r:
                scores(0, r, 128)
            residual(0, 128)
            prep(1, 128)
            with pe.Fori(0, TILES - 2) as i:
                with pe.Fori(0, HEADS) as r:
                    values_and_scores(i, r, 128, 128)
                residual(i + 1, 128)
                prep(i + 2, 128)
            with pe.Fori(0, HEADS) as r:
                values_and_scores(TILES - 2, r, 128, 128)
            residual(TILES - 1, 128)
            prep(TILES, SAMPLE_T)
            with pe.Fori(0, HEADS) as r:
                values_and_scores(TILES - 1, r, 128, SAMPLE_T)
            residual(TILES, SAMPLE_T)
            with pe.Fori(0, HEADS) as r:
                for q in range(NG):
                    values(TILES, r, SAMPLE_T, q)

        @block.scalar
        def _(act):
            act.sem_inc(s_rw, 1)
            act.sem_inc(s_sc, 1)
            act.sem_inc(s_out, 16)
            with act.Fori(0, 16) as hp:
                act.wait_ge(s_rw_mm, hp + 1)
                nc.scalar.copy(route_w[:, :, bass.ds(hp * NK, NK)],
                               p_t[:, :].rearrange("p (a b) -> p a b", b=NK)).then_inc(s_rw, 1)

            def stats(tile, T):
                act.wait_ge(s_x, 16 * (tile + 1))
                nc.scalar.activation(junk_a[:T, :], x_tile[:T, :], ACT.Square,
                                     accum_out=stat[:T, 0:1]).then_inc(s_sq, 1)
                act.wait_ge(s_sq, tile + 1)
                nc.scalar.activation(stat[:T, 1:2], stat[:T, 0:1], ACT.Sqrt, bias=eps_col[:T, :],
                                     scale=1.0 / D).then_inc(s_std, 1)

            def take_hT(tile, T):
                act.wait_ge(s_tr, tile + 1)
                nc.scalar.copy(hT[:, :, :T],
                               p_t[:, :].rearrange("p (a b) -> p a b", b=128)[:, :, :T]).then_inc(s_hT, 1)

            def route(tile, r, T):
                n = tile * HEADS + r
                act.wait_ge(s_scores, n + 1)
                act.wait_ge(s_sfree, n + 1)
                nc.scalar.copy(sc[:T, :], p_s[:T, 0:256]).then_inc(s_sc, 1)

            def soften(tile, r, T):
                n = tile * HEADS + r
                act.wait_ge(s_top, n + 1)
                nc.scalar.activation(ex[:T, :], top[:T, :], ACT.Exp, bias=smx[:T, 0:1],
                                     accum_out=smx[:T, 1:2]).then_inc(s_ex, 1)

            def weigh(tile, r, T, q):
                n = tile * HEADS + r
                c = q * GROUP
                act.wait_ge(s_dot, n * NG + q + 1)
                nc.scalar.activation(gel[:T, c:c + GROUP], dots[:T, c:c + GROUP], ACT.Gelu).then_inc(s_ach, 1)
                act.wait_ge(s_ach, (n * NG + q) * 2 + 1)
                for k in range(GROUP):
                    last = nc.scalar.mul(wgt[:T, c + k:c + k + 1], gel[:T, c + k:c + k + 1],
                                         g_now[:T, c + k:c + k + 1])
                last.then_inc(s_ach, 1)
                act.wait_ge(s_ach, (n * NG + q) * 2 + 2)
                for k in range(GROUP):
                    last = nc.scalar.mul(diag[:T, (c + k) % RING, :T], ident[:T, :T], wgt[:T, c + k:c + k + 1])
                last.then_inc(s_diag, 1)

            def take_g(tile, r, T):
                n = tile * HEADS + r
                act.wait_ge(s_idx, n + 1)
                nc.scalar.copy(g_now[:T, :], g_all[:T, bass.ds(r * TOPK, TOPK)]).then_inc(s_gcp, 1)
                act.wait_ge(s_gcp, n + 1)

            def finish(tile, T):
                act.wait_ge(s_vdone, (tile + 1) * HEADS * NG)
                act.wait_ge(s_out, 16 * tile + 16)
                nc.scalar.copy(ysb[:T, 512:1024], p_y[:T, 512:1024]).then_inc(s_yev, 1)

            def weigh_and_route(tile, r, T, T_next):
                take_g(tile, r, T)
                weigh(tile, r, T, 0)
                route(tile + 1, r, T_next)
                for q in range(1, 5):
                    weigh(tile, r, T, q)
                soften(tile + 1, r, T_next)
                for q in range(5, NG):
                    weigh(tile, r, T, q)

            stats(0, 128)
            take_hT(0, 128)
            with act.Fori(0, HEADS) as r:
                route(0, r, 128)
                soften(0, r, 128)
            stats(1, 128)
            take_hT(1, 128)
            with act.Fori(0, TILES - 2) as i:
                with act.Fori(0, HEADS) as r:
                    weigh_and_route(i, r, 128, 128)
                stats(i + 2, 128)
                finish(i, 128)
                take_hT(i + 2, 128)
            with act.Fori(0, HEADS) as r:
                weigh_and_route(TILES - 2, r, 128, 128)
            stats(TILES, SAMPLE_T)
            finish(TILES - 2, 128)
            take_hT(TILES, SAMPLE_T)
            with act.Fori(0, HEADS) as r:
                weigh_and_route(TILES - 1, r, 128, SAMPLE_T)
            finish(TILES - 1, 128)
            with act.Fori(0, HEADS) as r:
                take_g(TILES, r, SAMPLE_T)
                for q in range(NG):
                    weigh(TILES, r, SAMPLE_T, q)
            finish(TILES, SAMPLE_T)

        @block.vector
        def _(dve):
            dve.sem_inc(s_sfree, 1)
            dve.sem_inc(s_yev, 2)
            dve.wait_ge(s_gf, 16)

            def prep(tile, T):
                dve.wait_ge(s_std, tile + 1)
                if not (isinstance(tile, int) and tile == 0):
                    dve.wait_ge(s_tr, tile)
                nc.vector.reciprocal(stat[:T, 2:3], stat[:T, 1:2]).then_inc(s_rstd, 1)
                dve.wait_ge(s_rstd, tile + 1)
                nc.vector.scalar_tensor_tensor(out=h_next[:T, :], in0=x_tile[:T, :], scalar=stat[:T, 2:3],
                                               in1=gf_bc[:T, :], op0=ALU.mult, op1=ALU.mult).then_inc(s_h, 1)

            def linked(ins, k):
                ins.then_inc(s_dch, 1)
                dve.wait_ge(s_dch, k)

            def best_of_side(tile, r, T, p):
                n = tile * HEADS + r
                if p == 0:
                    dve.wait_ge(s_sc, n + 2)
                    apart(dve)
                    dve.sem_clear(s_dch)
                s, rep = sc[:T, p * NK:(p + 1) * NK], sc_rep[:T, p * NK:(p + 1) * NK]
                lo, hi = v16[:T, p, 0:8], v16[:T, p, 8:16]
                linked(nc.vector.max(lo, s), 4 * p + 1)
                nc.vector.max_index(i16[:T, p, 0:8], lo, s)
                linked(nc.vector.match_replace(rep, lo, s, NEG), 4 * p + 2)
                linked(nc.vector.max(hi, rep), 4 * p + 3)
                linked(nc.vector.max_index(i16[:T, p, 8:16], hi, rep), 4 * p + 4)

            def best_sums_first(tile, r, T):
                n = tile * HEADS + r
                nc.vector.tensor_copy(i16f[:T, :, :], i16[:T, :, :])
                nc.vector.tensor_tensor(
                    out=cand[:T, :].rearrange("p (a b) -> p a b", b=TOPK),
                    in0=v16[:T, 0, :].unsqueeze(2).broadcast_to([T, TOPK, TOPK]),
                    in1=v16[:T, 1, :].unsqueeze(1).broadcast_to([T, TOPK, TOPK]), op=ALU.add).then_inc(s_sfree, 1)
                dve.wait_ge(s_sfree, n + 2)
                apart(dve)
                linked(nc.vector.max(top[:T, 0:8], cand[:T, :]), 9)
                nc.vector.tensor_scalar(out=smx[:T, 0:1], in0=top[:T, 0:1], scalar1=-1.0, scalar2=None, op0=ALU.mult)
                nc.vector.max_index(pos[:T, 0:8], top[:T, 0:8], cand[:T, :])
                linked(nc.vector.match_replace(cand_rep[:T, :], top[:T, 0:8], cand[:T, :], NEG), 10)

            def best_sums_second(tile, r, T):
                n = tile * HEADS + r
                nc.vector.max(top[:T, 8:16], cand_rep[:T, :]).then_inc(s_top, 1)
                dve.wait_ge(s_top, n + 1)
                apart(dve)
                linked(nc.vector.max_index(pos[:T, 8:16], top[:T, 8:16], cand_rep[:T, :]), 11)
                nc.vector.tensor_single_scalar(posab[:T, 0, :], pos[:T, :], 4, ALU.logical_shift_right)
                linked(nc.vector.tensor_single_scalar(posab[:T, 1, :], pos[:T, :], 15, ALU.bitwise_and), 12)
                linked(nc.vector.tensor_copy(posabf[:T, :, :], posab[:T, :, :]), 13)

            def expert_numbers(tile, r, T, gathering):
                n = tile * HEADS + r
                oh = onehot[:T, :, :, :].rearrange("p s k a -> p (s k) a")
                linked(nc.vector.tensor_tensor(
                    out=oh, in0=iota16[:T, :].unsqueeze(1).broadcast_to([T, 32, 16]),
                    in1=posabf[:T, :, :].rearrange("p s k -> p (s k)").unsqueeze(2).broadcast_to([T, 32, 16]),
                    op=ALU.is_equal), 14)
                linked(nc.vector.tensor_tensor(
                    out=onehot[:T, :, :, :], in0=onehot[:T, :, :, :],
                    in1=i16f[:T, :, :].unsqueeze(2).broadcast_to([T, 2, TOPK, TOPK]), op=ALU.mult), 15)
                linked(nc.vector.tensor_reduce(out=isel[:T, :, :].rearrange("p s k -> p (s k)"), in_=oh,
                                               axis=AX.X, op=ALU.add), 16)

            def softmax_weights(tile, r, T, gathering):
                n = tile * HEADS + r
                if gathering:
                    dve.wait_ge(s_idxcp, 2 * (n - HEADS + 1))
                    dve.wait_ge(s_gcp, n - HEADS + 1)
                nc.vector.scalar_tensor_tensor(out=idx_all[:T, bass.ds(r * TOPK, TOPK)], in0=isel[:T, 0, :],
                                               scalar=float(NK), in1=isel[:T, 1, :], op0=ALU.mult, op1=ALU.add)
                dve.wait_ge(s_ex, n + 1)
                linked(nc.vector.reciprocal(smx[:T, 2:3], smx[:T, 1:2]), 17)
                nc.vector.tensor_scalar(out=g_all[:T, bass.ds(r * TOPK, TOPK)], in0=ex[:T, :],
                                        scalar1=smx[:T, 2:3], scalar2=None, op0=ALU.mult).then_inc(s_idx, 1)

            def dot(tile, r, T, q):
                n = tile * HEADS + r
                for k in range(GROUP):
                    c = q * GROUP + k
                    dve.wait_ge(s_slot[c % RING], 32 * n + 16 * (c // RING + 1))
                    last = nc.vector.tensor_tensor_reduce(
                        out=ring[:T, c % RING, 0:D], in0=ring[:T, c % RING, 0:D], in1=h_cur[:T, :], scale=1.0,
                        scalar=0.0, op0=ALU.mult, op1=ALU.add, accum_out=dots[:T, c:c + 1])
                last.then_inc(s_dot, 1)

            def pick(tile, r, T):
                best_of_side(tile, r, T, 0)
                best_of_side(tile, r, T, 1)
                best_sums_first(tile, r, T)
                best_sums_second(tile, r, T)
                expert_numbers(tile, r, T, False)
                softmax_weights(tile, r, T, False)

            def dot_and_pick(tile, r, T, T_next):
                dot(tile, r, T, 0)
                dot(tile, r, T, 1)
                best_of_side(tile + 1, r, T_next, 0)
                dot(tile, r, T, 2)
                best_of_side(tile + 1, r, T_next, 1)
                dot(tile, r, T, 3)
                best_sums_first(tile + 1, r, T_next)
                dot(tile, r, T, 4)
                best_sums_second(tile + 1, r, T_next)
                dot(tile, r, T, 5)
                expert_numbers(tile + 1, r, T_next, True)
                dot(tile, r, T, 6)
                softmax_weights(tile + 1, r, T_next, True)
                dot(tile, r, T, 7)

            def keep_h(tile, T):
                if not (isinstance(tile, int) and tile == 0):
                    dve.wait_ge(s_dot, tile * HEADS * NG)
                dve.wait_ge(s_h, tile + 1)
                nc.vector.tensor_copy(h_cur[:T, :], h_next[:T, :]).then_inc(s_hcur, 1)
                dve.wait_ge(s_hcur, tile + 1)

            def finish(tile, T):
                dve.wait_ge(s_vdone, (tile + 1) * HEADS * NG)
                dve.wait_ge(s_out, 16 * tile + 16)
                nc.vector.tensor_copy(ysb[:T, 0:512], p_y[:T, 0:512]).then_inc(s_yev, 1)

            prep(0, 128)
            with dve.Fori(0, HEADS) as r:
                pick(0, r, 128)
            keep_h(0, 128)
            prep(1, 128)
            with dve.Fori(0, TILES - 2) as i:
                with dve.Fori(0, HEADS) as r:
                    dot_and_pick(i, r, 128, 128)
                keep_h(i + 1, 128)
                prep(i + 2, 128)
                finish(i, 128)
            with dve.Fori(0, HEADS) as r:
                dot_and_pick(TILES - 2, r, 128, 128)
            keep_h(TILES - 1, 128)
            prep(TILES, SAMPLE_T)
            finish(TILES - 2, 128)
            with dve.Fori(0, HEADS) as r:
                dot_and_pick(TILES - 1, r, 128, SAMPLE_T)
            keep_h(TILES, SAMPLE_T)
            finish(TILES - 1, 128)
            with dve.Fori(0, HEADS) as r:
                for q in range(NG):
                    dot(TILES, r, SAMPLE_T, q)
            finish(TILES, SAMPLE_T)


def program(nc, t, out):
    with ExitStack() as ctx:
        c = Scope(nc, ctx, "c")
        c.ident, c.ones, c.upto, c.upto_chunk, c.after_chunk, c.future = (
            c.sb(n, [128, 128]) for n in ("ident", "ones", "upto", "upto_chunk", "after_chunk", "future"))
        c.chunk_of = c.sb("chunk_of", [128, 2])
        c.eps, c.one = c.sb("eps", [128, 1]), c.sb("one", [128, 1])
        c.zero_row = c.sb("zero_row", [1, BW])
        c.iota16 = c.sb("iota16", [128, 16])
        proj = nc.dram_tensor("proj", (TOKENS, P_COLS), F32, kind="Internal").ap()
        hT_spill = nc.dram_tensor("hT_spill", (128, DT * TOKENS), F32, kind="Internal").ap()
        oT_spill = nc.dram_tensor("oT_spill", (BRANCHES, 128, 4, TOKENS), F32, kind="Internal").ap()
        x1 = nc.dram_tensor("x1", (TOKENS, D), F32, kind="Internal").ap()

        constants(nc, c)
        input_projection(nc, c, t["x_all"], t["g_attn"], t["w_in1"], proj, hT_spill)
        memory_projection(nc, c, t["mem"], t["mem_g_in"], t["w_kv"], t["mem_g_k"], out["mem_k"], out["mem_v"])
        mixers(nc, c, proj,
               [t[k] for k in ("gla_w_a2", "gla_b_a", "gla_g_out", "fox_b_f", "fox_g_q", "fox_g_k", "mem_g_q")],
               [t[k] for k in ("fox_k", "fox_v", "fox_logf", "state_gla", "cache_mem_k", "cache_mem_v")],
               out["mem_k"], out["mem_v"],
               [out[k] for k in ("k_p", "v_p", "lf_p", "st_p", "k_s", "v_s", "lf_s", "st_s")], oT_spill)
        with ExitStack() as inner:
            mixT = inner.enter_context(nc.sbuf_tensor("mixT", [128, DT, TOKENS], F32))
            gated_mix(nc, c, hT_spill, oT_spill, t["w_gate"], t["w_br"], mixT)
            output_projection(nc, c, t["x_all"], t["w_out"], mixT, x1)
        peer(nc, c, x1, t["g_ffn"], t["w_qT"], t["sub_kT"], t["uv"], out["y"])


def kernel(x_prompt, x_sample, mem_prompt, cache_fox_k, cache_fox_v, cache_fox_logf, state_gla,
           cache_mem_k, cache_mem_v, g_attn, w_in, gla_w_a2, gla_b_a, gla_g_out, fox_b_f, fox_g_q, fox_g_k,
           mem_g_q, mem_g_in, mem_w_kv, mem_g_k, w_branch, w_out, g_ffn, peer_w_q, peer_sub_keys, peer_u, peer_v):
    import numpy as np
    import concourse.bacc as bacc
    from concourse.bass_utils import run_bass_kernel_spmd

    a = np.asarray
    w = a(w_in)[0]
    laid = {
        "x_all": np.concatenate([a(x_prompt)[0], a(x_sample)[0]], axis=0),
        "mem": a(mem_prompt)[0],
        "fox_k": a(cache_fox_k)[0, 0].reshape(PAST, BW),
        "fox_v": a(cache_fox_v)[0, 0].reshape(PAST, BW),
        "fox_logf": a(cache_fox_logf)[0, 0],
        "state_gla": a(state_gla)[0, 0],
        "cache_mem_k": a(cache_mem_k)[0, 0].reshape(NMEM, BW),
        "cache_mem_v": a(cache_mem_v)[0, 0].reshape(NMEM, BW),
        "g_attn": a(g_attn), "gla_w_a2": a(gla_w_a2), "gla_b_a": a(gla_b_a), "gla_g_out": a(gla_g_out),
        "fox_b_f": a(fox_b_f), "fox_g_q": a(fox_g_q), "fox_g_k": a(fox_g_k), "mem_g_q": a(mem_g_q),
        "mem_g_in": a(mem_g_in), "w_kv": a(mem_w_kv)[0], "mem_g_k": a(mem_g_k),
        "w_in1": w[:, :P_COLS].reshape(DT, 128, P_CHUNKS, PW).transpose(2, 1, 0, 3).reshape(P_CHUNKS, 128, DT * PW),
        "w_gate": w[:, P_COLS:].reshape(DT, 128, BRANCHES, DT, 128).transpose(3, 1, 2, 0, 4)
                   .reshape(DT, 128, BRANCHES * DT * 128),
        "w_br": a(w_branch)[0].reshape(BRANCHES, 4, 128, DT, 128).transpose(3, 2, 0, 1, 4)
                 .reshape(DT, 128, BRANCHES * 4 * 128),
        "w_out": a(w_out)[0], "g_ffn": a(g_ffn),
        "w_qT": a(peer_w_q)[0].T,
        "sub_kT": a(peer_sub_keys)[0].reshape(16, 128, 128).transpose(0, 2, 1),
        "uv": np.concatenate([a(peer_u)[0], a(peer_v)[0]], axis=1),
    }
    shapes = {"y": (TOKENS, D), "k_p": (SEQ, BW), "v_p": (SEQ, BW), "lf_p": (SEQ, FH), "st_p": (GH, GDK, GDV),
              "mem_k": (NMEM, BW), "mem_v": (NMEM, BW), "k_s": (SAMPLE_T, BW), "v_s": (SAMPLE_T, BW),
              "lf_s": (SAMPLE_T, FH), "st_s": (GH, GDK, GDV)}
    nc = bacc.Bacc("TRN2", target_bir_lowering=False, num_devices=1)
    laid = {k: np.ascontiguousarray(v) for k, v in laid.items()}
    t = {k: nc.dram_tensor(f"in_{k}", v.shape, F32, kind="ExternalInput").ap() for k, v in laid.items()}
    out = {k: nc.dram_tensor(f"out_{k}", v, F32, kind="ExternalOutput").ap() for k, v in shapes.items()}
    program(nc, t, out)
    r = run_bass_kernel_spmd(nc, [{f"in_{k}": v for k, v in laid.items()}], core_ids=[0]).results[0]
    o = {k: a(r[f"out_{k}"]) for k in shapes}
    return (o["y"][:SEQ].reshape(1, SEQ, D), o["y"][SEQ:].reshape(1, SAMPLE_T, D),
            o["k_p"].reshape(1, 1, SEQ, FH, FD), o["v_p"].reshape(1, 1, SEQ, FH, FD), o["lf_p"].reshape(1, 1, SEQ, FH),
            o["st_p"].reshape(1, 1, GH, GDK, GDV), o["mem_k"].reshape(1, 1, NMEM, MH, MD),
            o["mem_v"].reshape(1, 1, NMEM, MH, MD), o["k_s"].reshape(1, 1, SAMPLE_T, FH, FD),
            o["v_s"].reshape(1, 1, SAMPLE_T, FH, FD), o["lf_s"].reshape(1, 1, SAMPLE_T, FH),
            o["st_s"].reshape(1, 1, GH, GDK, GDV))
```

```python
import concourse.bass as bass
from concourse import mybir
from contextlib import ExitStack

F32 = mybir.dt.float32
U32 = mybir.dt.uint32
I32 = mybir.dt.int32
ALU = mybir.AluOpType
ACT = mybir.ActivationFunctionType
AX = mybir.AxisListType

D = 1024
DT = D // 128
SEQ, SAMPLE_T, PAST = 1024, 64, 512
TOKENS = SEQ + SAMPLE_T
TILES = SEQ // 128
PAST_TILES = PAST // 128
EPS = 1e-6
CHUNK = 64
GH, GDK, GDV, GRANK = 4, 64, 128, 16
GLA_TAU = 16.0
FH, FD = 8, 64
MH, MD, NMEM = 4, 128, 256
MT = NMEM // 128
BW = 512
BRANCHES = 3
GQ, GK, GV, GG, GA, FQ, FK, FV, FF, MQ = 0, 256, 512, 1024, 1536, 1552, 2064, 2576, 3088, 3096
P_COLS = 3608
P_CHUNKS = 8
PW = P_COLS // P_CHUNKS
MASKED = -1.0e30


def rows(tile, T):
    if isinstance(tile, int):
        return slice(tile * 128, tile * 128 + T)
    return bass.ds(tile * 128, T)


def tokens(t0):
    return t0 * 128


class Scope:

    def __init__(self, nc, ctx, tag):
        self.nc, self.ctx, self.tag, self.sems = nc, ctx, tag, []

    def sb(self, name, shape, dt=F32):
        return self.ctx.enter_context(self.nc.sbuf_tensor(f"{self.tag}_{name}", shape, dt))

    def pb(self, name, shape, dt=F32):
        return self.ctx.enter_context(self.nc.psum_tensor(f"{self.tag}_{name}", shape, dt))

    def sem(self, name):
        self.sems.append(self.ctx.enter_context(self.nc.semaphore(f"{self.tag}_{name}")))
        return self.sems[-1]

    def retire(self):
        ids = sorted(x.num for x in self.sems)
        assert ids == list(range(ids[0], ids[-1] + 1))
        with self.nc.Block() as block:
            @block.gpsimd
            def _(pool):
                pool.sem_clear(range(ids[0], ids[-1] + 1))


def constants(nc, c):
    with nc.Block() as block:
        s = c.sem("const")

        @block.gpsimd
        def _(pool):
            n = [0]

            def step(ins):
                n[0] += 1
                ins.then_inc(s, 1)
                pool.wait_ge(s, n[0])

            step(nc.gpsimd.memset(c.ident[:, :], 0.0))
            step(nc.gpsimd.affine_select(out=c.ident[:, :], in_=c.ident[:, :], compare_op=ALU.not_equal, fill=1.0,
                                         base=0, pattern=[[-1, 128]], channel_multiplier=1))
            step(nc.gpsimd.memset(c.ones[:, :], 1.0))
            step(nc.gpsimd.affine_select(out=c.upto[:, :], in_=c.ones[:, :], compare_op=ALU.is_ge, fill=0.0,
                                         base=0, pattern=[[1, 128]], channel_multiplier=-1))
            step(nc.gpsimd.tensor_copy(c.upto_chunk[:, :], c.upto[:, :]))
            step(nc.gpsimd.memset(c.upto_chunk[0:CHUNK, CHUNK:128], 0.0))
            step(nc.gpsimd.affine_select(out=c.after_chunk[:, :], in_=c.ones[:, :], compare_op=ALU.is_gt, fill=0.0,
                                         base=0, pattern=[[-1, 128]], channel_multiplier=1))
            step(nc.gpsimd.memset(c.after_chunk[CHUNK:128, 0:CHUNK], 0.0))
            step(nc.gpsimd.memset(c.chunk_of[:, :], 0.0))
            step(nc.gpsimd.memset(c.chunk_of[0:CHUNK, 0:1], 1.0))
            step(nc.gpsimd.memset(c.chunk_of[CHUNK:128, 1:2], 1.0))
            step(nc.gpsimd.memset(c.eps[:, :], EPS))
            step(nc.gpsimd.memset(c.one[:, :], 1.0))
            step(nc.gpsimd.iota(c.iota16[:, :], pattern=[[1, 16]], base=0, channel_multiplier=0,
                                allow_small_or_imprecise_dtypes=True))


def input_projection(nc, c, x_all, g_attn, w_in1, proj, hT_spill):
    UN = 18
    RING = 6
    with ExitStack() as ctx:
        m = Scope(nc, ctx, "in")
        g_bc = m.sb("g_bc", [128, D])
        x_tile = [m.sb(f"x_tile{k}", [128, D]) for k in range(2)]
        h_tile = m.sb("h_tile", [128, D])
        squares = m.sb("squares", [128, D])
        stat = m.sb("stat", [128, 4])
        hT = m.sb("hT", [128, DT, TOKENS])
        w = [m.sb(f"w{k}", [128, DT, PW]) for k in range(2)]
        out = m.sb("out", [128, RING, PW])
        p_tr = m.pb("p_tr", [128, D])
        p_mm = [m.pb(f"p_mm{k}", [128, 512]) for k in range(RING)]

        s_g, s_spill = m.sem("s_g"), m.sem("s_spill")
        s_x = m.sem("s_x")
        s_w = [m.sem(f"s_w{k}") for k in range(2)]
        s_sq, s_std, s_rstd, s_h, s_tr, s_hT = (m.sem(n) for n in ("s_sq", "s_std", "s_rstd", "s_h", "s_tr", "s_hT"))
        s_mm = m.sem("s_mm")
        s_ev = [m.sem(f"s_ev{k}") for k in range(2)]
        s_put = [m.sem(f"s_put{k}") for k in range(RING)]
        s_step = {e: m.sem(f"s_step_{k}") for k, e in (("pe", nc.tensor),)}

        with nc.Block() as block:
            @block.sync
            def _(sp):
                sp.dma_start(g_bc[:, :], g_attn[0:1, :].broadcast_to([128, D])).then_inc(s_g, 16)

                def load(tile, T):
                    sp.dma_start(x_tile[0][:T, :], x_all[rows(tile, T), :]).then_inc(s_x, 16)

                load(0, 128)
                for k in range(2):
                    sp.dma_start(w[k][:, :, :], w_in1[k].rearrange("p (a b) -> p a b", a=DT)).then_inc(s_w[k], 16)
                with sp.Fori(1, TILES) as t:
                    sp.wait_ge(s_h, t)
                    load(t, 128)
                sp.wait_ge(s_h, TILES)
                load(TILES, SAMPLE_T)
                sp.wait_ge(s_hT, TILES + 1)
                sp.dma_start(hT_spill.rearrange("p (a b) -> p a b", a=DT), hT[:, :, :]).then_inc(s_spill, 16)
                def store_chunks(b, load_more):
                    for u in range(UN):
                        chunk, tile = b * 2 + u // 9, u % 9
                        T = 128 if tile < TILES else SAMPLE_T
                        sp.wait_ge(s_ev[u % 2], b * 9 + u // 2 + 1 + 3)
                        sp.dma_start(proj[tile * 128:tile * 128 + T, bass.ds(chunk * PW, PW)],
                                     out[:T, u % RING, :]).then_inc(s_put[u % RING], 16)
                        if load_more and tile == TILES:
                            sp.wait_ge(s_mm, b * UN + u + 1)
                            sp.dma_start(w[u // 9][:, :, :], w_in1[bass.ds(chunk + 2, 1), :, :].squeeze(0)
                                         .rearrange("p (a b) -> p a b", a=DT)).then_inc(s_w[u // 9], 16)

                with sp.Fori(0, P_CHUNKS // 2 - 1) as b:
                    store_chunks(b, True)
                store_chunks(P_CHUNKS // 2 - 1, False)
                for k in range(RING):
                    sp.wait_ge(s_put[k], 16 * (P_CHUNKS // 2 * 3 + 1))
                sp.wait_ge(s_spill, 16)

            @block.tensor
            def _(pe):
                def transposes(tile, T):
                    pe.wait_ge(s_h, tile + 1)
                    if not (isinstance(tile, int) and tile == 0):
                        pe.wait_ge(s_hT, tile)
                        pe.sem_inc(s_step[pe], 1)
                    for dt in range(DT):
                        mm = nc.tensor.transpose(p_tr[:, dt * 128:dt * 128 + T], h_tile[:T, dt * 128:(dt + 1) * 128],
                                                 c.ident[:T, :T])
                    mm.then_inc(s_tr, 1)

                transposes(0, 128)
                with pe.Fori(1, TILES) as t:
                    transposes(t, 128)
                transposes(TILES, SAMPLE_T)
                pe.wait_ge(s_hT, TILES + 1)
                with pe.Fori(0, P_CHUNKS // 2) as b:
                    for u in range(UN):
                        tile = u % 9
                        T = 128 if tile < TILES else SAMPLE_T
                        if tile == 0:
                            pe.wait_ge(s_w[u // 9], (b + 1) * 16)
                        pe.wait_ge(s_ev[u % 2], b * 9 + u // 2 + 1)
                        pe.sem_inc(s_step[pe], 1)
                        for dt in range(DT):
                            mm = nc.tensor.matmul(p_mm[u % RING][:T, :PW], hT[:, dt, tile * 128:tile * 128 + T],
                                                  w[u // 9][:, dt, :], start=dt == 0, stop=dt == DT - 1)
                        mm.then_inc(s_mm, 1)

            def evacuate(eng, parity, copy):
                eng.sem_inc(s_ev[parity], 3)
                with eng.Fori(0, P_CHUNKS // 2) as b:
                    for u in range(parity, UN, 2):
                        T = 128 if u % 9 < TILES else SAMPLE_T
                        eng.wait_ge(s_mm, b * UN + u + 1)
                        eng.wait_ge(s_put[u % RING], 16 * (b * 3 + u // RING + 1))
                        copy(out[:T, u % RING, :], p_mm[u % RING][:T, :PW]).then_inc(s_ev[parity], 1)

            @block.scalar
            def _(act):
                def stats(tile, T):
                    act.wait_ge(s_x, 16 * (tile + 1))
                    nc.scalar.activation(squares[:T, :], x_tile[0][:T, :], ACT.Square,
                                         accum_out=stat[:T, 0:1]).then_inc(s_sq, 1)
                    act.wait_ge(s_sq, tile + 1)
                    nc.scalar.activation(stat[:T, 1:2], stat[:T, 0:1], ACT.Sqrt, bias=c.eps[:T, :],
                                         scale=1.0 / D).then_inc(s_std, 1)
                    act.wait_ge(s_tr, tile + 1)
                    nc.scalar.copy(hT[:, :, bass.ds(tile * 128, T)],
                                   p_tr[:, :].rearrange("p (a b) -> p a b", b=128)[:, :, :T]).then_inc(s_hT, 1)

                for k in range(0, RING, 2):
                    act.sem_inc(s_put[k], 16)
                with act.Fori(0, TILES) as t:
                    stats(t, 128)
                stats(TILES, SAMPLE_T)
                evacuate(act, 0, nc.scalar.copy)

            @block.vector
            def _(dve):
                dve.wait_ge(s_g, 16)

                def norm(tile, T):
                    dve.wait_ge(s_std, tile + 1)
                    nc.vector.reciprocal(stat[:T, 2:3], stat[:T, 1:2]).then_inc(s_rstd, 1)
                    if not (isinstance(tile, int) and tile == 0):
                        dve.wait_ge(s_tr, tile)
                    dve.wait_ge(s_rstd, tile + 1)
                    nc.vector.scalar_tensor_tensor(out=h_tile[:T, :], in0=x_tile[0][:T, :], scalar=stat[:T, 2:3],
                                                   in1=g_bc[:T, :], op0=ALU.mult, op1=ALU.mult).then_inc(s_h, 1)

                for k in range(1, RING, 2):
                    dve.sem_inc(s_put[k], 16)
                norm(0, 128)
                with dve.Fori(1, TILES) as t:
                    norm(t, 128)
                norm(TILES, SAMPLE_T)
                evacuate(dve, 1, nc.vector.tensor_copy)
        m.retire()


def memory_projection(nc, c, mem, g_in, w_kv, g_k, mem_k, mem_v):
    with ExitStack() as ctx:
        m = Scope(nc, ctx, "mem")
        g_bc = m.sb("g_bc", [128, D])
        gk_bc = m.sb("gk_bc", [128, MD])
        w = m.sb("w", [128, DT, D])
        x = m.sb("x", [128, MT, D])
        h = m.sb("h", [128, MT, D])
        hT = m.sb("hT", [128, DT, NMEM])
        squares = m.sb("squares", [128, D])
        stat = m.sb("stat", [128, MT, 4])
        ksq = m.sb("ksq", [128, MT, BW])
        kst = m.sb("kst", [128, MT, 3 * MH])
        kn = m.sb("kn", [128, MT, BW])
        v = m.sb("v", [128, MT, BW])
        p_tr = m.pb("p_tr", [128, D])
        p_kv = m.pb("p_kv", [128, MT, 2, BW])
        s_g, s_w, s_x, s_sq, s_std, s_h, s_tr, s_hT = (m.sem(n) for n in (
            "s_g", "s_w", "s_x", "s_sq", "s_std", "s_h", "s_tr", "s_hT"))
        s_kv, s_ksq, s_kss, s_kstd, s_kn, s_v, s_put, s_d = (m.sem(n) for n in (
            "s_kv", "s_ksq", "s_kss", "s_kstd", "s_kn", "s_v", "s_put", "s_d"))

        with nc.Block() as block:
            @block.sync
            def _(sp):
                sp.dma_start(x[:, :, :], mem.rearrange("(a p) d -> p a d", p=128)).then_inc(s_x, 16)
                sp.dma_start(g_bc[:, :], g_in[0:1, :].broadcast_to([128, D])).then_inc(s_g, 16)
                sp.dma_start(gk_bc[:, :], g_k[0:1, :].broadcast_to([128, MD])).then_inc(s_g, 16)
                sp.dma_start(w[:, :, :], w_kv.rearrange("(a p) n -> p a n", p=128)).then_inc(s_w, 16)
                sp.wait_ge(s_kn, MT)
                sp.dma_start(mem_k.rearrange("(a p) n -> p a n", p=128), kn[:, :, :]).then_inc(s_put, 16)
                sp.wait_ge(s_v, MT)
                sp.dma_start(mem_v.rearrange("(a p) n -> p a n", p=128), v[:, :, :]).then_inc(s_put, 16)
                sp.wait_ge(s_put, 32)

            @block.tensor
            def _(pe):
                for a in range(MT):
                    pe.wait_ge(s_h, a + 1)
                    if a:
                        pe.wait_ge(s_hT, a)
                    for dt in range(DT):
                        mm = nc.tensor.transpose(p_tr[:, dt * 128:(dt + 1) * 128], h[:, a, dt * 128:(dt + 1) * 128],
                                                 c.ident[:, :])
                    mm.then_inc(s_tr, 1)
                pe.wait_ge(s_w, 16)
                for a in range(MT):
                    pe.wait_ge(s_hT, a + 1)
                    for n in range(2):
                        for dt in range(DT):
                            mm = nc.tensor.matmul(p_kv[:, a, n, :], hT[:, dt, a * 128:(a + 1) * 128],
                                                  w[:, dt, n * BW:(n + 1) * BW], start=dt == 0, stop=dt == DT - 1)
                    mm.then_inc(s_kv, 1)

            @block.scalar
            def _(act):
                act.wait_ge(s_x, 16)
                for a in range(MT):
                    if a:
                        act.wait_ge(s_sq, a)
                    nc.scalar.activation(squares[:, :], x[:, a, :], ACT.Square,
                                         accum_out=stat[:, a, 0:1]).then_inc(s_sq, 1)
                for a in range(MT):
                    act.wait_ge(s_sq, a + 1)
                    nc.scalar.activation(stat[:, a, 1:2], stat[:, a, 0:1], ACT.Sqrt, bias=c.eps[:, :],
                                         scale=1.0 / D).then_inc(s_std, 1)
                for a in range(MT):
                    act.wait_ge(s_tr, a + 1)
                    nc.scalar.copy(hT[:, :, a * 128:(a + 1) * 128],
                                   p_tr[:, :].rearrange("p (a b) -> p a b", b=128)).then_inc(s_hT, 1)
                for a in range(MT):
                    act.wait_ge(s_kv, a + 1)
                    nc.scalar.activation(ksq[:, a, :], p_kv[:, a, 0, :], ACT.Square).then_inc(s_ksq, 1)
                    nc.scalar.copy(v[:, a, :], p_kv[:, a, 1, :]).then_inc(s_v, 1)
                    act.wait_ge(s_kss, a + 1)
                    nc.scalar.activation(kst[:, a, MH:2 * MH], kst[:, a, 0:MH], ACT.Sqrt, bias=c.eps[:, :],
                                         scale=1.0 / MD).then_inc(s_kstd, 1)

            @block.vector
            def _(dve):
                n = [0]

                def link(ins):
                    n[0] += 1
                    ins.then_inc(s_d, 1)
                    dve.wait_ge(s_d, n[0])

                dve.wait_ge(s_g, 32)
                for a in range(MT):
                    dve.wait_ge(s_std, a + 1)
                    link(nc.vector.reciprocal(stat[:, a, 2:3], stat[:, a, 1:2]))
                    nc.vector.scalar_tensor_tensor(out=h[:, a, :], in0=x[:, a, :], scalar=stat[:, a, 2:3],
                                                   in1=g_bc[:, :], op0=ALU.mult, op1=ALU.mult).then_inc(s_h, 1)
                for a in range(MT):
                    dve.wait_ge(s_ksq, a + 1)
                    nc.vector.tensor_reduce(out=kst[:, a, 0:MH], in_=ksq[:, a, :].rearrange("p (h d) -> p h d", h=MH),
                                            axis=AX.X, op=ALU.add).then_inc(s_kss, 1)
                    dve.wait_ge(s_kstd, a + 1)
                    link(nc.vector.reciprocal(kst[:, a, 2 * MH:3 * MH], kst[:, a, MH:2 * MH]))
                    k3 = kn[:, a, :].rearrange("p (h d) -> p h d", h=MH)
                    link(nc.vector.tensor_tensor(
                        out=k3, in0=p_kv[:, a, 0, :].rearrange("p (h d) -> p h d", h=MH),
                        in1=kst[:, a, 2 * MH:3 * MH].unsqueeze(2).broadcast_to([128, MH, MD]), op=ALU.mult))
                    nc.vector.tensor_tensor(out=k3, in0=k3, in1=gk_bc[:, :].unsqueeze(1).broadcast_to([128, MH, MD]),
                                            op=ALU.mult).then_inc(s_kn, 1)
        m.retire()


def mixers(nc, c, proj, small, caches, mem_k, mem_v, outs, oT_spill):
    w_a2, b_a, g_out, b_f, g_q, g_k, g_mq = small
    ck, cv, clf, state0, cmk, cmv = caches
    k_p, v_p, lf_p, st_p, k_s, v_s, lf_s, st_s = outs
    SPAN = 512
    PER = SPAN // 128
    AD = FD + 2

    with ExitStack() as ctx:
        m = Scope(nc, ctx, "mix")
        wa2 = m.sb("wa2", [GRANK, GH * GDK])
        ba_bc = m.sb("ba_bc", [128, GH * GDK])
        go_bc = m.sb("go_bc", [128, GDV])
        bf_bc = m.sb("bf_bc", [128, FH])
        gq_bc = m.sb("gq_bc", [128, FD])
        gk_bc = m.sb("gk_bc", [128, FD])
        gm_bc = m.sb("gm_bc", [128, MD])
        P = m.sb("P", [128, P_COLS])
        sq = m.sb("sq", [128, 1024])
        sqm = m.sb("sqm", [128, BW])
        tmp = m.sb("tmp", [128, BW])
        st = m.sb("st", [128, 64])
        q_aug = m.sb("q_aug", [128, FH, AD])
        k_aug = m.sb("k_aug", [128, FH, AD])
        mq = m.sb("mq", [128, BW])
        z = m.sb("z", [128, 264])
        za = m.sb("za", [128, 264])
        ze = m.sb("ze", [128, 264])
        zl = m.sb("zl", [128, 264])
        ls = m.sb("ls", [128, 264])
        la = m.sb("la", [128, 256])
        gaT = m.sb("gaT", [GRANK, 128])
        carry = m.sb("carry", [128, FH])
        cs = m.sb("cs", [128, FH])
        eb = m.sb("eb", [128, 3, 256])
        ebl = m.sb("ebl", [GDK, 2 * GH])
        qkd = m.sb("qkd", [128, 2 * GH, GDK])
        ko = m.sb("ko", [128, GH, GDK])
        qkdT = m.sb("qkdT", [GDK, 2 * GH, 128])
        attT = m.sb("attT", [128, GH, 128])
        S = [m.sb(f"S{k}", [GDK, GH, GDV]) for k in range(2)]
        sig = m.sb("sig", [128, BW])
        qT = m.sb("qT", [AD, FH, 128])
        kT = m.sb("kT", [AD, FH, SEQ])
        V = m.sb("V", [128, TILES, BW])
        mkT = m.sb("mkT", [128, MH, NMEM])
        mv = m.sb("mv", [128, MT, BW])
        mk = m.sb("mk", [128, MT, BW])
        mqT = m.sb("mqT", [128, MH, 128])
        pm = m.sb("pm", [128, MH, NMEM])
        pmT = m.sb("pmT", [128, MH * MT, 128])
        mstat = m.sb("mstat", [128, 4 * MH])
        hidden = m.sb("hidden", [128, 896])
        fmax = m.sb("fmax", [128, FH])
        lsum = m.sb("lsum", [128, FH])
        rl = m.sb("rl", [128, FH])
        prob = [m.sb(f"prob{k}", [128, SEQ]) for k in range(2)]
        PT = [m.sb(f"PT{k}", [128, TILES, 128]) for k in range(2)]
        o_all = m.sb("o_all", [128, BRANCHES * BW])
        oT = [m.sb(f"oT{k}", [128, 4, 128]) for k in range(3)]

        p_tr = m.pb("p_tr", [128, 1024])
        p_s = [m.pb(f"p_s{k}", [128, SPAN]) for k in range(2)]
        p_of = m.pb("p_of", [128, BW])
        p_g = m.pb("p_g", [128, BW])
        p_x = m.pb("p_x", [128, BW])
        p_y = m.pb("p_y", [128, BW])

        names = ("par", "P", "sq", "ss", "std", "kn", "mq", "gaT_mm", "gaT", "za", "z", "ln", "la", "cum",
                 "aug", "eb", "qd", "trq", "qT", "trk", "kT", "trg", "gT", "trm", "mqT", "att_mm", "att", "dS",
                 "S1", "S2", "og_mm", "gsq", "gss", "gstd", "og", "sig", "ogl", "ms_mm", "mmax", "pm", "trpm",
                 "pmT", "om_mm", "omem", "z0", "ofox", "tro", "oT", "kout", "lfout", "V", "vout",
                 "mem", "mkT_mm", "mkT", "S0", "sout", "ck", "carry",
                 "d", "a", "e", "dg", "dg2", "astep", "spstep", "dstep", "pestep", "gq")
        s = {n: m.sem(f"s_{n}") for n in names}
        s_oput = [m.sem(f"s_oput{k}") for k in range(3)]
        s_qk, s_score, s_max, s_exp, s_trP, s_pv = (m.sem(n) for n in (
            "s_qk", "s_score", "s_max", "s_exp", "s_trP", "s_pv"))
        s_trh = [m.sem(f"s_trh{k}") for k in range(2)]
        s_PT = [m.sem(f"s_PT{k}") for k in range(2)]

        def at0(t):
            return isinstance(t, int) and t == 0

        def key_step(t):
            return t if not (isinstance(t, int) and t == TILES) else TILES + PAST_TILES

        def spans(t, T, prior):
            if T == SAMPLE_T:
                return [(0, SPAN), (SPAN, T)], [128] * PAST_TILES + [T]
            n = 1 if (t if isinstance(t, int) else t.max_val) < PER else 2
            return [(k * SPAN, SPAN) for k in range(n)], [128] * (n * PER)

        def in_second(t):
            return 8 * (t - PER)

        def h3(ap, h):
            return ap.rearrange("p (h d) -> p h d", h=h)

        with nc.Block() as block:
            @block.sync
            def _(sp):
                def load_P(t, T):
                    if not at0(t):
                        sp.wait_ge(s["ogl"], t)
                    sp.dma_start(P[:T, :], proj[rows(t, T), :]).then_inc(s["P"], 16)

                load_P(0, 128)
                for dst, src, n in ((wa2[:, :], w_a2[0], None), (ba_bc[:, :], b_a, 256), (go_bc[:, :], g_out, GDV),
                                    (bf_bc[:, :], b_f, FH), (gq_bc[:, :], g_q, FD), (gk_bc[:, :], g_k, FD),
                                    (gm_bc[:, :], g_mq, MD)):
                    sp.dma_start(dst, src if n is None else src[0:1, :].broadcast_to([128, n])).then_inc(s["par"], 16)

                def load_mem(k_src, v_src, again):
                    if again:
                        sp.wait_ge(s["om_mm"], TILES)
                    sp.dma_start(mk[:, :, :], k_src.rearrange("(a p) n -> p a n", p=128)).then_inc(s["mem"], 16)
                    sp.dma_start(mv[:, :, :], v_src.rearrange("(a p) n -> p a n", p=128)).then_inc(s["mem"], 16)

                def store_tile(t, T, k_dst, lf_dst, r):
                    sp.wait_ge(s["kn"], t + 1)
                    sp.dma_start(h3(k_dst[r, :], FH), k_aug[:T, :, 0:FD]).then_inc(s["kout"], 16)
                    sp.wait_ge(s["la"], t + 1)
                    sp.dma_start(lf_dst[r, :], ls[:T, 256:264]).then_inc(s["lfout"], 16)

                def store_o(t, T):
                    for k in range(3):
                        sp.wait_ge(s["oT"], 3 * t + k + 1)
                        sp.sem_inc(s["spstep"], 1)
                        sp.dma_start(oT_spill[k, :, :, bass.ds(t * 128, T)] if not isinstance(t, int) else
                                     oT_spill[k, :, :, t * 128:t * 128 + T], oT[k][:, :, :T]).then_inc(s_oput[k], 16)

                load_mem(mem_k, mem_v, False)
                sp.dma_start(V[:, :, :], proj[0:SEQ, FV:FV + BW].rearrange("(a p) n -> p a n", p=128))\
                    .then_inc(s["V"], 16)
                sp.wait_ge(s["V"], 16)
                sp.dma_start(v_p.rearrange("(a p) n -> p a n", p=128), V[:, :, :]).then_inc(s["vout"], 16)
                store_tile(0, 128, k_p, lf_p, rows(0, 128))
                load_P(1, 128)
                store_o(0, 128)
                with sp.Fori(1, TILES - 1) as t:
                    store_tile(t, 128, k_p, lf_p, rows(t, 128))
                    load_P(t + 1, 128)
                    store_o(t, 128)
                t = TILES - 1
                store_tile(t, 128, k_p, lf_p, rows(t, 128))
                load_P(TILES, SAMPLE_T)
                load_mem(cmk, cmv, True)
                store_o(t, 128)
                sp.wait_ge(s["S2"], TILES)
                sp.dma_start(st_p.rearrange("h d e -> d h e"), S[0][:, :, :]).then_inc(s["sout"], 16)
                sp.wait_ge(s["sout"], 16)
                sp.dma_start(S[0][:, :, :], state0.rearrange("h d e -> d h e")).then_inc(s["S0"], 16)
                sp.wait_ge(s["vout"], 16)
                sp.wait_ge(s_pv, FH * TILES + 2)
                sp.dma_start(V[:, 0:PAST_TILES, :], cv.rearrange("(a p) n -> p a n", p=128)).then_inc(s["V"], 16)
                sp.dma_start(V[:SAMPLE_T, PAST_TILES, :], proj[SEQ:TOKENS, FV:FV + BW]).then_inc(s["V"], 16)
                for u in range(PAST_TILES):
                    sp.wait_ge(s["trk"], TILES + u)
                    sp.wait_ge(s["cum"], TILES + u)
                    if u == 0:
                        sp.wait_ge(s["kout"], 16 * TILES)
                        sp.wait_ge(s["lfout"], 16 * TILES)
                    sp.dma_start(k_aug[:, :, 0:FD], h3(ck[rows(u, 128), :], FH)).then_inc(s["ck"], 16)
                    sp.dma_start(ls[:, 256:264], clf[rows(u, 128), :]).then_inc(s["ck"], 16)
                sp.wait_ge(s["V"], 48)
                sp.dma_start(v_s, V[:SAMPLE_T, PAST_TILES, :]).then_inc(s["vout"], 16)
                store_tile(TILES, SAMPLE_T, k_s, lf_s, slice(0, SAMPLE_T))
                sp.wait_ge(s["S1"], TILES + 1)
                sp.dma_start(st_s.rearrange("h d e -> d h e"), S[1][:, :, :]).then_inc(s["sout"], 16)
                store_o(TILES, SAMPLE_T)
                for k in range(3):
                    sp.wait_ge(s_oput[k], 16 * (TILES + 2))
                sp.wait_ge(s["sout"], 32)
                sp.wait_ge(s["kout"], 16 * (TILES + 1))
                sp.wait_ge(s["lfout"], 16 * (TILES + 1))
                sp.wait_ge(s["vout"], 32)

            @block.gpsimd
            def _(pool):
                pool.memset(q_aug[:, :, FD:FD + 1], 1.0).then_inc(s["z0"], 1)
                pool.memset(k_aug[:, :, FD + 1:FD + 2], 1.0).then_inc(s["z0"], 1)
                pool.memset(attT[:, :, :], 0.0).then_inc(s["z0"], 1)
                pool.memset(carry[:, :], 0.0).then_inc(s["z0"], 1)
                pool.memset(S[0][:, :, :], 0.0).then_inc(s["z0"], 1)
                pool.memset(kT[:, :, :], 0.0).then_inc(s["z0"], 1)
                pool.memset(hidden[:, :], 0.0).then_inc(s["z0"], 1)
                pool.wait_ge(s["z0"], 7)
                pool.affine_select(out=hidden[:, :], in_=hidden[:, :], compare_op=ALU.is_ge, fill=MASKED,
                                   base=SPAN - 128, pattern=[[-1, 896]], channel_multiplier=1).then_inc(s["z0"], 1)

            @block.tensor
            def _(pe):
                def alone():
                    pe.sem_inc(s["pestep"], 1)

                def forget_sums(u, T, with_gla):
                    pe.matmul(p_y[:T, 0:FH], c.upto[:T, :T], ls[:T, 256:264], start=True, stop=True)
                    mm = nc.tensor.matmul(p_y[:, FH:2 * FH], c.ones[:T, :], ls[:T, 256:264], start=True, stop=True)
                    if with_gla:
                        nc.tensor.matmul(p_x[:T, 0:256], c.upto_chunk[:T, :T], la[:T, :], start=True, stop=True)
                        nc.tensor.matmul(p_x[:T, 256:512], c.after_chunk[:T, :T], la[:T, :], start=True, stop=True)
                        for h in range(GH):
                            mm = nc.tensor.matmul(p_y[:GDK, 16 + 2 * h:18 + 2 * h], la[:T, h * GDK:(h + 1) * GDK],
                                                  c.chunk_of[:T, :], start=True, stop=True)
                    mm.then_inc(s["cum"], 1)

                def keys_transposed(u, T):
                    for h in range(FH):
                        mm = nc.tensor.transpose(p_tr[:AD, h * 128:h * 128 + T], k_aug[:T, h, :], c.ident[:T, :T])
                    mm.then_inc(s["trk"], 1)

                def memory_keys(n):
                    pe.wait_ge(s["mem"], 32 * n + 32)
                    if n:
                        pe.wait_ge(s["oT"], 3 * TILES)
                    for h in range(MH):
                        for a in range(MT):
                            mm = nc.tensor.transpose(p_tr[:, (h * MT + a) * 128:(h * MT + a + 1) * 128],
                                                     mk[:, a, h * MD:(h + 1) * MD], c.ident[:, :])
                    mm.then_inc(s["mkT_mm"], 1)
                    pe.wait_ge(s["mkT"], n + 1)

                def scores(t, h, T, where):
                    pe.wait_ge(s_score, FH * t + h + 1)
                    alone()
                    for k, (k0, n) in enumerate(where):
                        mm = nc.tensor.matmul(p_s[(len(where) - 1 - k) % 2][:T, :n], qT[:, h, :T],
                                              kT[:, h, k0:k0 + n], start=True, stop=True)
                    mm.then_inc(s_qk, 1)

                def transposed(t, h, T, keys):
                    pe.wait_ge(s_exp, FH * t + h + 1)
                    for half in range(len(keys) // PER + (len(keys) % PER > 0)):
                        base = FH * t if half == 0 else in_second(t)
                        pe.wait_ge(s_PT[half], base + h + 1)
                        alone()
                        for k in range(half * PER, min(len(keys), (half + 1) * PER)):
                            mm = nc.tensor.transpose(p_tr[:keys[k], k * 128:k * 128 + T],
                                                     prob[h % 2][:T, k * 128:k * 128 + keys[k]], c.ident[:T, :T])
                        mm.then_inc(s_trh[half], 1)

                def probabilities_read(t, h, keys):
                    pe.sem_inc(s["pestep"], 1)
                    pe.wait_ge(s_trh[0], FH * t + h + 1)
                    if len(keys) > PER:
                        pe.wait_ge(s_trh[1], in_second(t) + h + 1)
                    pe.sem_inc(s_trP, 1)

                def values(t, h, T, keys):
                    pe.wait_ge(s_PT[0], FH * t + h + 2)
                    if len(keys) > PER:
                        pe.wait_ge(s_PT[1], in_second(t) + h + 2)
                    alone()
                    for k, n in enumerate(keys):
                        mm = nc.tensor.matmul(p_of[:T, h * FD:(h + 1) * FD], PT[h % 2][:n, k, :T],
                                              V[:n, k, h * FD:(h + 1) * FD], start=k == 0, stop=k == len(keys) - 1)
                    mm.then_inc(s_pv, 1)

                def front(t, T):
                    def decay_inputs():
                        pe.wait_ge(s["P"], 16 * (t + 1))
                        alone()
                        nc.tensor.transpose(p_y[:GRANK, :T], P[:T, GA:GA + GRANK], c.ident[:T, :T])\
                            .then_inc(s["gaT_mm"], 1)

                    def decays():
                        pe.wait_ge(s["gaT"], t + 1)
                        alone()
                        nc.tensor.matmul(p_x[:T, 0:256], gaT[:, :T], wa2[:, :], start=True, stop=True)\
                            .then_inc(s["za"], 1)

                    def sums():
                        pe.wait_ge(s["la"], t + 1)
                        alone()
                        forget_sums(key_step(t), T, True)

                    return {0: decay_inputs, 1: decays, 5: sums}

                def tile(t, T, prior, gla_chunks, ahead):
                    u = key_step(t)
                    pe.wait_ge(s["aug"], u + 1)
                    alone()
                    for h in range(FH):
                        mm = nc.tensor.transpose(p_tr[:AD, h * 128:h * 128 + T], q_aug[:T, h, :], c.ident[:T, :T])
                    mm.then_inc(s["trq"], 1)
                    pe.wait_ge(s["qT"], t + 1)
                    alone()
                    keys_transposed(u, T)
                    pe.wait_ge(s["kT"], u + 1)
                    pe.wait_ge(s["qd"], t + 1)
                    alone()
                    for h in range(2 * GH):
                        mm = nc.tensor.transpose(p_tr[:GDK, h * 128:h * 128 + T], qkd[:T, h, :], c.ident[:T, :T])
                    mm.then_inc(s["trg"], 1)
                    pe.wait_ge(s["gT"], t + 1)
                    pe.wait_ge(s["mq"], t + 1)
                    alone()
                    for h in range(MH):
                        mm = nc.tensor.transpose(p_tr[:, h * 128:h * 128 + T], mq[:T, h * MD:(h + 1) * MD],
                                                 c.ident[:T, :T])
                    mm.then_inc(s["trm"], 1)
                    for h in range(GH):
                        mm = nc.tensor.matmul(p_g[:T, h * 128:h * 128 + T], qkdT[:, GH + h, :T], qkdT[:, h, :T],
                                              start=True, stop=True)
                    mm.then_inc(s["att_mm"], 1)
                    for ch in range(gla_chunks):
                        r = slice(ch * CHUNK, (ch + 1) * CHUNK)
                        for h in range(GH):
                            mm = nc.tensor.matmul((p_x, p_y)[ch][:GDK, h * GDV:(h + 1) * GDV], ko[r, h, :],
                                                  P[r, GV + h * GDV:GV + (h + 1) * GDV], start=True, stop=True)
                        mm.then_inc(s["dS"], 1)
                    pe.wait_ge(s["mqT"], t + 1)
                    alone()
                    for h in range(MH):
                        mm = nc.tensor.matmul(p_tr[:T, h * NMEM:(h + 1) * NMEM], mqT[:, h, :T], mkT[:, h, :],
                                              start=True, stop=True)
                    mm.then_inc(s["ms_mm"], 1)
                    pe.wait_ge(s["att"], t + 1)
                    if gla_chunks == 2:
                        pe.wait_ge(s["S1"], t + 1)
                    alone()
                    for h in range(GH):
                        o = p_g[:, h * GDV:(h + 1) * GDV]
                        nc.tensor.matmul(o[:T, :], attT[:T, h, :T], P[:T, GV + h * GDV:GV + (h + 1) * GDV],
                                         start=True, stop=False, skip_group_check=True)
                        for ch in range(gla_chunks):
                            r = slice(ch * CHUNK, (ch + 1) * CHUNK)
                            mm = nc.tensor.matmul(o[r, :], qkdT[:, h, r], S[ch][:, h, :], start=False, stop=True,
                                                  skip_group_check=True)
                    mm.then_inc(s["og_mm"], 1)
                    pe.wait_ge(s["pm"], t + 1)
                    alone()
                    for h in range(MH):
                        for a in range(MT):
                            b = h * MT + a
                            mm = nc.tensor.transpose(p_tr[:, b * 128:b * 128 + T], pm[:T, h, a * 128:(a + 1) * 128],
                                                     c.ident[:T, :T])
                    mm.then_inc(s["trpm"], 1)
                    pe.wait_ge(s["pmT"], t + 1)
                    pe.wait_ge(s["og"], t + 1)
                    alone()
                    for h in range(MH):
                        for a in range(MT):
                            mm = nc.tensor.matmul(p_g[:T, h * MD:(h + 1) * MD], pmT[:, h * MT + a, :T],
                                                  mv[:, a, h * MD:(h + 1) * MD], start=a == 0, stop=a == MT - 1)
                    mm.then_inc(s["om_mm"], 1)
                    where, keys = spans(t, T, prior)
                    if at0(t):
                        pe.wait_ge(s["V"], 16)
                    scores(t, 0, T, where)
                    scores(t, 1, T, where)
                    if not at0(t):
                        pe.wait_ge(s["ofox"], t)
                        alone()
                    for h in range(FH):
                        transposed(t, h, T, keys)
                        if h + 2 < FH:
                            scores(t, h + 2, T, where)
                        probabilities_read(t, h, keys)
                        if h:
                            values(t, h - 1, T, keys)
                        if h in ahead:
                            ahead[h]()
                    values(t, FH - 1, T, keys)
                    pe.wait_ge(s["ogl"], t + 1)
                    pe.wait_ge(s["omem"], t + 1)
                    pe.wait_ge(s["ofox"], t + 1)
                    alone()
                    for k in range(3):
                        if k == 2:
                            pe.wait_ge(s["oT"], 3 * t + 1)
                            alone()
                        for b in range(4):
                            col = (k * 4 + b) * 128
                            mm = nc.tensor.transpose(p_tr[:, (k % 2) * 512 + b * 128:(k % 2) * 512 + b * 128 + T],
                                                     o_all[:T, col:col + 128], c.ident[:T, :T])
                        mm.then_inc(s["tro"], 1)
                    pe.wait_ge(s["oT"], 3 * t + 3)
                    alone()

                pe.wait_ge(s["par"], 7 * 16)
                pe.wait_ge(s["z0"], 8)
                memory_keys(0)
                for stage in front(0, 128).values():
                    stage()
                tile(0, 128, 0, 2, front(1, 128))
                with pe.Fori(1, PER) as t:
                    tile(t, 128, t, 2, front(t + 1, 128))
                with pe.Fori(PER, TILES - 1) as t:
                    tile(t, 128, t, 2, front(t + 1, 128))
                tile(TILES - 1, 128, TILES - 1, 2, {})
                memory_keys(1)
                for u in range(PAST_TILES):
                    pe.wait_ge(s["ck"], 32 * (u + 1))
                    if u:
                        pe.wait_ge(s["aug"], TILES + u)
                    forget_sums(TILES + u, 128, False)
                    pe.wait_ge(s["aug"], TILES + u + 1)
                    if u:
                        pe.wait_ge(s["kT"], TILES + u)
                    keys_transposed(TILES + u, 128)
                pe.wait_ge(s["kT"], TILES + PAST_TILES)
                pe.wait_ge(s["V"], 48)
                pe.wait_ge(s["S0"], 16)
                for stage in front(TILES, SAMPLE_T).values():
                    stage()
                tile(TILES, SAMPLE_T, PAST_TILES, 1, {})

            @block.scalar
            def _(act):
                def front(t, T):
                    def squares():
                        act.wait_ge(s["P"], 16 * (t + 1))
                        act.sem_inc(s["astep"], 1)
                        act.sem_clear(s["a"])
                        nc.scalar.activation(sq[:T, :], P[:T, FQ:FQ + 2 * BW], ACT.Square).then_inc(s["sq"], 1)
                        nc.scalar.activation(sqm[:T, :], P[:T, MQ:MQ + BW], ACT.Square).then_inc(s["sq"], 1)
                        act.wait_ge(s["gaT_mm"], t + 1)
                        nc.scalar.copy(gaT[:, :T], p_y[:GRANK, :T]).then_inc(s["gaT"], 1)

                    def roots():
                        act.wait_ge(s["ss"], t + 1)
                        nc.scalar.activation(st[:T, 20:36], st[:T, 0:16], ACT.Sqrt, bias=c.eps[:T, :], scale=1.0 / FD)
                        nc.scalar.activation(st[:T, 36:40], st[:T, 16:20], ACT.Sqrt, bias=c.eps[:T, :],
                                             scale=1.0 / MD).then_inc(s["std"], 1)

                    def log_sigmoids():
                        act.wait_ge(s["z"], t + 1)
                        nc.scalar.activation(za[:T, :], z[:T, :], ACT.Abs).then_inc(s["a"], 1)
                        act.wait_ge(s["a"], 1)
                        nc.scalar.activation(sig[:T, :], P[:T, GG:GG + BW], ACT.Exp, scale=-1.0).then_inc(s["sig"], 1)
                        nc.scalar.activation(ze[:T, :], za[:T, :], ACT.Exp, scale=-1.0).then_inc(s["a"], 1)
                        act.wait_ge(s["a"], 2)
                        nc.scalar.activation(zl[:T, :], ze[:T, :], ACT.Ln, bias=c.one[:T, :]).then_inc(s["ln"], 1)

                    def decay_factors():
                        act.wait_ge(s["cum"], key_step(t) + 1)
                        nc.scalar.activation(eb[:T, 0, :], p_x[:T, 0:256], ACT.Exp)
                        nc.scalar.activation(eb[:T, 1, :], p_x[:T, 0:256], ACT.Exp, scale=-1.0)
                        nc.scalar.activation(eb[:T, 2, :], p_x[:T, 256:512], ACT.Exp)
                        act.wait_ge(s["aug"], key_step(t) + 1)
                        nc.scalar.activation(ebl[:, :], p_y[:GDK, 16:24], ACT.Exp).then_inc(s["eb"], 1)

                    return {0: squares, 2: roots, 3: log_sigmoids, 7: decay_factors}

                def tile(t, T, prior, gla_chunks, ahead):
                    u = key_step(t)
                    act.wait_ge(s["trq"], t + 1)
                    nc.scalar.copy(qT[:, :, :T], p_tr[:AD, :].rearrange("p (h t) -> p h t", h=FH)[:, :, :T])\
                        .then_inc(s["qT"], 1)
                    act.wait_ge(s["trg"], t + 1)
                    nc.scalar.copy(qkdT[:, :, :T], p_tr[:GDK, :].rearrange("p (h t) -> p h t", h=2 * GH)[:, :, :T])\
                        .then_inc(s["gT"], 1)
                    act.wait_ge(s["trm"], t + 1)
                    nc.scalar.copy(mqT[:, :, :T], p_tr[:, 0:512].rearrange("p (h t) -> p h t", h=MH)[:, :, :T])\
                        .then_inc(s["mqT"], 1)
                    act.wait_ge(s["mmax"], t + 1)
                    for h in range(MH):
                        last = nc.scalar.activation(pm[:T, h, :], p_tr[:T, h * NMEM:(h + 1) * NMEM], ACT.Exp,
                                                    bias=mstat[:T, h:h + 1], accum_out=mstat[:T, MH + h:MH + h + 1])
                    last.then_inc(s["pm"], 1)
                    act.wait_ge(s["og_mm"], t + 1)
                    nc.scalar.activation(sqm[:T, :], p_g[:T, :], ACT.Square).then_inc(s["gsq"], 1)
                    act.wait_ge(s["gss"], t + 1)
                    nc.scalar.activation(st[:T, 44:48], st[:T, 40:44], ACT.Sqrt, bias=c.eps[:T, :], scale=1.0 / GDV)\
                        .then_inc(s["gstd"], 1)
                    act.wait_ge(s["trpm"], t + 1)
                    nc.scalar.copy(pmT[:, :, :T], p_tr[:, :].rearrange("p (h t) -> p h t", h=MH * MT)[:, :, :T])\
                        .then_inc(s["pmT"], 1)

                    where, keys = spans(t, T, prior)
                    width = where[-1][0] + where[-1][1]

                    def exponentials(h):
                        act.wait_ge(s_max, FH * t + h + 1)
                        nc.scalar.activation(prob[h % 2][:T, :width], prob[h % 2][:T, :width], ACT.Exp,
                                             bias=fmax[:T, h:h + 1], accum_out=lsum[:T, h:h + 1]).then_inc(s_exp, 1)

                    exponentials(0)
                    for h in range(FH):
                        if h + 1 < FH:
                            exponentials(h + 1)
                        act.wait_ge(s_pv, FH * t + h + 1)
                        for half in range(len(where)):
                            ks = keys[half * PER:(half + 1) * PER]
                            act.wait_ge(s_trh[half], (FH * t if half == 0 else in_second(t)) + h + 1)
                            nc.scalar.copy(PT[h % 2][:ks[0], half * PER:half * PER + len(ks), :T],
                                           p_tr[:ks[0], half * 512:half * 512 + len(ks) * 128]
                                           .rearrange("p (k t) -> p k t", k=len(ks))[:, :, :T])\
                                .then_inc(s_PT[half], 1)
                        if h in ahead:
                            ahead[h]()
                    for k in range(3):
                        act.wait_ge(s["tro"], 3 * t + k + 1)
                        act.wait_ge(s_oput[k], 16 * (t + 1))
                        nc.scalar.copy(oT[k][:, :, :T],
                                       p_tr[:, (k % 2) * 512:(k % 2) * 512 + 512]
                                       .rearrange("p (h t) -> p h t", h=4)[:, :, :T]).then_inc(s["oT"], 1)

                def memory_keys(n):
                    act.wait_ge(s["mkT_mm"], n + 1)
                    nc.scalar.copy(mkT[:, :, :].rearrange("p h k -> p (h k)"), p_tr[:, :]).then_inc(s["mkT"], 1)

                for half in range(2):
                    act.sem_inc(s_PT[half], 1)
                for k in range(3):
                    act.sem_inc(s_oput[k], 16)
                memory_keys(0)
                for stage in front(0, 128).values():
                    stage()
                tile(0, 128, 0, 2, front(1, 128))
                with act.Fori(1, PER) as t:
                    tile(t, 128, t, 2, front(t + 1, 128))
                with act.Fori(PER, TILES - 1) as t:
                    tile(t, 128, t, 2, front(t + 1, 128))
                tile(TILES - 1, 128, TILES - 1, 2, {})
                memory_keys(1)
                for stage in front(TILES, SAMPLE_T).values():
                    stage()
                tile(TILES, SAMPLE_T, PAST_TILES, 1, {})

            @block.vector
            def _(dve):
                def sums_added(u, T, link):
                    link(nc.vector.tensor_tensor(out=cs[:T, :], in0=p_y[:T, 0:FH], in1=carry[:T, :], op=ALU.add))
                    nc.vector.tensor_copy(q_aug[:T, :, FD + 1], cs[:T, :])
                    nc.vector.tensor_scalar(out=k_aug[:T, :, FD], in0=cs[:T, :], scalar1=-1.0, scalar2=None,
                                            op0=ALU.mult)
                    link(nc.vector.tensor_tensor(out=carry[:, :], in0=p_y[:, FH:2 * FH], in1=carry[:, :],
                                                 op=ALU.add))

                def linker(name):
                    n = [0]

                    def link(ins):
                        n[0] += 1
                        ins.then_inc(s[name], 1)
                        dve.wait_ge(s[name], n[0])

                    return link

                def front(t, T):
                    link = linker("e")

                    def bc(col, h, d):
                        return st[:T, col:col + h].unsqueeze(2).broadcast_to([T, h, d])

                    def scaled(out, src, col, gain, heads, d):
                        link(nc.vector.tensor_tensor(out=h3(tmp[:T, :], heads), in0=h3(src, heads),
                                                     in1=bc(col, heads, d), op=ALU.mult))
                        return nc.vector.tensor_tensor(out=out, in0=h3(tmp[:T, :], heads),
                                                       in1=gain[:T, :].unsqueeze(1).broadcast_to([T, heads, d]),
                                                       op=ALU.mult)

                    def sums_of_squares():
                        dve.wait_ge(s["sq"], 2 * (t + 1))
                        dve.sem_inc(s["dstep"], 1)
                        dve.sem_clear(s["e"])
                        nc.vector.tensor_reduce(out=st[:T, 0:16], in_=h3(sq[:T, :], 2 * FH), axis=AX.X, op=ALU.add)
                        nc.vector.tensor_reduce(out=st[:T, 16:20], in_=h3(sqm[:T, :], MH), axis=AX.X, op=ALU.add)\
                            .then_inc(s["ss"], 1)
                        nc.vector.tensor_tensor(out=z[:T, 256:264], in0=P[:T, FF:FF + FH], in1=bf_bc[:T, :],
                                                op=ALU.add)

                    def gates():
                        dve.wait_ge(s["za"], t + 1)
                        nc.vector.tensor_tensor(out=z[:T, 0:256], in0=p_x[:T, 0:256], in1=ba_bc[:T, :], op=ALU.add)\
                            .then_inc(s["z"], 1)

                    def keys():
                        dve.wait_ge(s["std"], t + 1)
                        link(nc.vector.reciprocal(st[:T, 20:40], st[:T, 20:40]))
                        if not at0(t):
                            dve.wait_ge(s["trk"], key_step(t))
                            dve.wait_ge(s["kout"], 16 * t)
                        scaled(k_aug[:T, :, 0:FD], P[:T, FK:FK + BW], 28, gk_bc, FH, FD).then_inc(s["kn"], 1)
                        dve.wait_ge(s["kn"], t + 1)

                    def log_sigmoids():
                        dve.wait_ge(s["ln"], t + 1)
                        if not at0(t):
                            dve.wait_ge(s["lfout"], 16 * t)
                            dve.sem_inc(s["dstep"], 1)
                        link(nc.vector.scalar_tensor_tensor(out=ls[:T, :], in0=z[:T, :], scalar=0.0, in1=zl[:T, :],
                                                            op0=ALU.min, op1=ALU.subtract))
                        nc.vector.tensor_scalar(out=la[:T, :], in0=ls[:T, 0:256], scalar1=1.0 / GLA_TAU,
                                                scalar2=None, op0=ALU.mult).then_inc(s["la"], 1)
                        link(scaled(q_aug[:T, :, 0:FD], P[:T, FQ:FQ + BW], 20, gq_bc, FH, FD))

                    def memory_queries():
                        scaled(h3(mq[:T, :], MH), P[:T, MQ:MQ + BW], 36, gm_bc, MH, MD).then_inc(s["mq"], 1)
                        dve.wait_ge(s["sig"], t + 1)
                        dve.sem_inc(s["dstep"], 1)
                        link(nc.vector.tensor_scalar(out=sig[:T, :], in0=sig[:T, :], scalar1=1.0, scalar2=None,
                                                     op0=ALU.add))

                    def output_gates():
                        link(nc.vector.reciprocal(sig[:T, :], sig[:T, :]))
                        link(nc.vector.tensor_tensor(out=sig[:T, :], in0=sig[:T, :], in1=P[:T, GG:GG + BW],
                                                     op=ALU.mult))

                    def sums():
                        dve.wait_ge(s["cum"], key_step(t) + 1)
                        sums_added(key_step(t), T, link)
                        dve.sem_inc(s["aug"], 1)

                    return {1: sums_of_squares, 2: gates, 3: keys, 4: log_sigmoids, 5: memory_queries,
                            6: output_gates, 7: sums}

                def tile(t, T, prior, gla_chunks, ahead):
                    u = key_step(t)
                    link = linker("d")

                    def bc(col, h, d):
                        return st[:T, col:col + h].unsqueeze(2).broadcast_to([T, h, d])

                    dve.sem_clear(s["d"])
                    dve.wait_ge(s["eb"], t + 1)
                    nc.vector.scalar_tensor_tensor(out=qkd[:T, 0:GH, :].rearrange("p h d -> p (h d)"),
                                                   in0=P[:T, GQ:GQ + 256], scalar=GDK ** -0.5, in1=eb[:T, 0, :],
                                                   op0=ALU.mult, op1=ALU.mult)
                    nc.vector.tensor_tensor(out=qkd[:T, GH:2 * GH, :].rearrange("p h d -> p (h d)"),
                                            in0=P[:T, GK:GK + 256], in1=eb[:T, 1, :], op=ALU.mult)
                    nc.vector.tensor_tensor(out=ko[:T, :, :].rearrange("p h d -> p (h d)"),
                                            in0=P[:T, GK:GK + 256], in1=eb[:T, 2, :], op=ALU.mult)\
                        .then_inc(s["qd"], 1)
                    dve.wait_ge(s["trk"], u + 1)
                    nc.vector.tensor_copy(kT[:, :, bass.ds(prior * 128, T)],
                                          p_tr[:AD, :].rearrange("p (h t) -> p h t", h=FH)[:, :, :T])\
                        .then_inc(s["kT"], 1)
                    dve.wait_ge(s["att_mm"], t + 1)
                    dve.sem_inc(s["dstep"], 1)
                    for h in range(GH):
                        last = nc.vector.copy_predicated(attT[:T, h, :T], c.upto_chunk[:T, :T].bitcast(I32),
                                                         p_g[:T, h * 128:h * 128 + T])
                    last.then_inc(s["att"], 1)
                    if gla_chunks == 2:
                        dve.wait_ge(s["dS"], 2 * t + 1)
                    else:
                        dve.wait_ge(s["dS"], 2 * TILES + 1)
                        dve.wait_ge(s["S0"], 16)
                    if not at0(t):
                        dve.wait_ge(s["og_mm"], t)
                    for h in range(GH):
                        last = nc.vector.scalar_tensor_tensor(
                            out=S[1][:, h, :], in0=S[0][:, h, :], scalar=ebl[:, 2 * h:2 * h + 1],
                            in1=p_x[:GDK, h * GDV:(h + 1) * GDV], op0=ALU.mult, op1=ALU.add)
                    last.then_inc(s["S1"], 1)
                    dve.wait_ge(s["ms_mm"], t + 1)
                    nc.vector.tensor_reduce(out=mstat[:T, 0:MH], in_=h3(p_tr[:T, :], MH), axis=AX.X, op=ALU.max,
                                            negate=True).then_inc(s["mmax"], 1)
                    dve.wait_ge(s["gsq"], t + 1)
                    nc.vector.tensor_reduce(out=st[:T, 40:44], in_=h3(sqm[:T, :], GH), axis=AX.X, op=ALU.add)\
                        .then_inc(s["gss"], 1)
                    if gla_chunks == 2:
                        dve.wait_ge(s["dS"], 2 * t + 2)
                        dve.wait_ge(s["S1"], t + 1)
                        dve.wait_ge(s["og_mm"], t + 1)
                        for h in range(GH):
                            last = nc.vector.scalar_tensor_tensor(
                                out=S[0][:, h, :], in0=S[1][:, h, :], scalar=ebl[:, 2 * h + 1:2 * h + 2],
                                in1=p_y[:GDK, h * GDV:(h + 1) * GDV], op0=ALU.mult, op1=ALU.add)
                        last.then_inc(s["S2"], 1)
                        dve.wait_ge(s["S2"], t + 1)
                    dve.wait_ge(s["gstd"], t + 1)
                    link(nc.vector.reciprocal(st[:T, 48:52], st[:T, 44:48]))
                    nc.vector.tensor_tensor(out=h3(tmp[:T, :], GH), in0=h3(p_g[:T, :], GH), in1=bc(48, GH, GDV),
                                            op=ALU.mult).then_inc(s["og"], 1)
                    dve.wait_ge(s["og"], t + 1)
                    link(nc.vector.tensor_tensor(out=h3(tmp[:T, :], GH), in0=h3(tmp[:T, :], GH),
                                                 in1=go_bc[:T, :].unsqueeze(1).broadcast_to([T, GH, GDV]),
                                                 op=ALU.mult))
                    if not at0(t):
                        dve.wait_ge(s["oT"], 3 * t)
                    nc.vector.tensor_tensor(out=o_all[:T, 0:BW], in0=tmp[:T, :], in1=sig[:T, :], op=ALU.mult)\
                        .then_inc(s["ogl"], 1)
                    dve.wait_ge(s["pm"], t + 1)
                    link(nc.vector.reciprocal(mstat[:T, 2 * MH:3 * MH], mstat[:T, MH:2 * MH]))
                    dve.wait_ge(s["om_mm"], t + 1)
                    nc.vector.tensor_tensor(out=h3(o_all[:T, 2 * BW:3 * BW], MH), in0=h3(p_g[:T, :], MH),
                                            in1=mstat[:T, 2 * MH:3 * MH].unsqueeze(2).broadcast_to([T, MH, MD]),
                                            op=ALU.mult).then_inc(s["omem"], 1)
                    where, keys = spans(t, T, prior)
                    width = where[-1][0] + where[-1][1]
                    for h in range(FH):
                        dve.wait_ge(s_qk, FH * t + h + 1)
                        dve.wait_ge(s_trP, FH * t + h + 1)
                        dve.sem_inc(s["dstep"], 1)
                        k0, width_last = where[-1]
                        x0 = SPAN - 128 if T == SAMPLE_T else (len(where) * PER - 1) * 128 - t * 128
                        nc.vector.tensor_tensor(out=prob[h % 2][:T, k0:k0 + width_last],
                                                in0=p_s[0][:T, :width_last],
                                                in1=hidden[:T, bass.ds(x0, width_last)], op=ALU.add)\
                            .then_inc(s["dg"], 1)
                        if len(where) == 2:
                            nc.vector.tensor_copy(prob[h % 2][:T, 0:SPAN], p_s[1][:T, :]).then_inc(s["dg2"], 1)
                            dve.wait_ge(s["dg2"], in_second(t) + h + 1)
                        dve.wait_ge(s["dg"], FH * t + h + 1)
                        dve.sem_inc(s_score, 1)
                        nc.vector.tensor_reduce(out=fmax[:T, h:h + 1], in_=prob[h % 2][:T, :width], axis=AX.X,
                                                op=ALU.max, negate=True).then_inc(s_max, 1)
                        if h - 1 in ahead:
                            ahead[h - 1]()
                    if FH - 1 in ahead:
                        ahead[FH - 1]()
                    dve.wait_ge(s_exp, FH * (t + 1))
                    link(nc.vector.reciprocal(rl[:T, :], lsum[:T, :]))
                    dve.wait_ge(s_pv, FH * (t + 1) + 2)
                    nc.vector.tensor_tensor(out=h3(o_all[:T, BW:2 * BW], FH), in0=h3(p_of[:T, :], FH),
                                            in1=rl[:T, :].unsqueeze(2).broadcast_to([T, FH, FD]), op=ALU.mult)\
                        .then_inc(s["ofox"], 1)

                dve.sem_inc(s_score, 1)
                dve.sem_inc(s_trP, 2)
                dve.sem_inc(s_pv, 2)
                dve.wait_ge(s["par"], 7 * 16)
                dve.wait_ge(s["z0"], 8)
                nc.vector.tensor_scalar(out=gq_bc[:, :], in0=gq_bc[:, :], scalar1=FD ** -0.5, scalar2=None,
                                        op0=ALU.mult).then_inc(s["gq"], 1)
                nc.vector.tensor_scalar(out=gm_bc[:, :], in0=gm_bc[:, :], scalar1=MD ** -0.5, scalar2=None,
                                        op0=ALU.mult).then_inc(s["gq"], 1)
                dve.wait_ge(s["gq"], 2)
                for stage in front(0, 128).values():
                    stage()
                tile(0, 128, 0, 2, front(1, 128))
                with dve.Fori(1, PER) as t:
                    tile(t, 128, t, 2, front(t + 1, 128))
                with dve.Fori(PER, TILES - 1) as t:
                    tile(t, 128, t, 2, front(t + 1, 128))
                tile(TILES - 1, 128, TILES - 1, 2, {})
                nc.vector.memset(carry[:, :], 0.0).then_inc(s["carry"], 1)
                dve.wait_ge(s["carry"], 1)
                dve.sem_clear(s["d"])
                link = linker("d")
                for u in range(PAST_TILES):
                    dve.wait_ge(s["cum"], TILES + u + 1)
                    dve.wait_ge(s["ck"], 32 * (u + 1))
                    sums_added(TILES + u, 128, link)
                    dve.sem_inc(s["aug"], 1)
                    dve.wait_ge(s["trk"], TILES + u + 1)
                    nc.vector.tensor_copy(kT[:, :, u * 128:(u + 1) * 128],
                                          p_tr[:AD, :].rearrange("p (h t) -> p h t", h=FH)).then_inc(s["kT"], 1)
                for stage in front(TILES, SAMPLE_T).values():
                    stage()
                tile(TILES, SAMPLE_T, PAST_TILES, 1, {})
        m.retire()


def gated_mix(nc, c, hT_spill, oT_spill, w_gate, w_br, mixT):
    SPANS = [(0, 364), (364, 364), (728, 360)]
    assert sum(n for _, n in SPANS) == TOKENS
    UN = 2 * BRANCHES * len(SPANS)
    GW, BRW = DT * 128, 4 * 128
    with ExitStack() as ctx:
        m = Scope(nc, ctx, "gate")
        hT = m.sb("hT", [128, DT, TOKENS])
        oT = m.sb("oT", [128, BRANCHES * 4, TOKENS])
        wg = [m.sb(f"wg{k}", [128, BRANCHES, DT, 128]) for k in range(2)]
        wb = [m.sb(f"wb{k}", [128, BRANCHES, 4, 128]) for k in range(2)]
        sg = [m.sb(f"sg{k}", [128, 364]) for k in range(3)]
        part = [m.sb(f"part{k}", [128, 364]) for k in range(3)]
        acc = [m.sb(f"acc{k}", [128, 364]) for k in range(3)]
        p_g = [m.pb(f"p_g{k}", [128, 512]) for k in range(3)]
        p_b = [m.pb(f"p_b{k}", [128, 512]) for k in range(3)]
        s_mm, s_sg, s_pr, s_part, s_step = (m.sem(n) for n in ("s_mm", "s_sg", "s_pr", "s_part", "s_step"))
        s_h = [m.sem(f"s_h{k}") for k in range(len(SPANS))]
        s_o = [m.sem(f"s_o{k}") for k in range(BRANCHES)]
        s_w = [m.sem(f"s_w{k}") for k in range(2)]

        def units():
            for v in range(UN):
                yield v, v // 9, (v // 3) % 3, v % 3

        with nc.Block() as block:
            @block.sync
            def _(sp):
                def load(k, dd):
                    if isinstance(dd, int):
                        g, b = w_gate[dd], w_br[dd]
                    else:
                        g, b = w_gate[bass.ds(dd, 1)].squeeze(0), w_br[bass.ds(dd, 1)].squeeze(0)
                    sp.dma_start(wg[k][:, :, :, :].rearrange("p n k m -> p (n k m)"), g).then_inc(s_w[k], 16)
                    sp.dma_start(wb[k][:, :, :, :].rearrange("p n k m -> p (n k m)"), b).then_inc(s_w[k], 16)

                h_all = hT_spill.rearrange("p (a b) -> p a b", a=DT)
                load(0, 0)
                for tc, (t0, N) in enumerate(SPANS):
                    sp.dma_start(hT[:, :, t0:t0 + N], h_all[:, :, t0:t0 + N]).then_inc(s_h[tc], 16)
                    if tc == 0:
                        sp.dma_start(oT[:, 0:4, :], oT_spill[0]).then_inc(s_o[0], 16)
                for k in range(1, BRANCHES):
                    sp.dma_start(oT[:, 4 * k:4 * k + 4, :], oT_spill[k]).then_inc(s_o[k], 16)
                load(1, 1)
                with sp.Fori(1, DT // 2) as b:
                    for k in range(2):
                        sp.wait_ge(s_mm, b * UN - UN + 9 * (k + 1))
                        load(k, b * 2 + k)

            @block.tensor
            def _(pe):
                with pe.Fori(0, DT // 2) as b:
                    for v, e, n, tc in units():
                        t0, N = SPANS[tc]
                        if n == 0 and tc == 0:
                            pe.wait_ge(s_w[e], 32 * (b + 1))
                        if e == 0 and n == 0:
                            pe.wait_ge(s_h[tc], 16)
                        pe.wait_ge(s_sg, b * UN + v + 1)
                        pe.wait_ge(s_pr, b * UN + v + 1)
                        pe.sem_inc(s_step, 1)
                        for k in range(DT):
                            nc.tensor.matmul(p_g[tc][:, :N], wg[e][:, n, k, :], hT[:, k, t0:t0 + N],
                                             start=k == 0, stop=k == DT - 1)
                        if e == 0 and tc == 0:
                            pe.wait_ge(s_o[n], 16)
                        for k in range(4):
                            mm = nc.tensor.matmul(p_b[tc][:, :N], wb[e][:, n, k, :], oT[:, 4 * n + k, t0:t0 + N],
                                                  start=k == 0, stop=k == 3)
                        mm.then_inc(s_mm, 1)

            @block.scalar
            def _(act):
                act.sem_inc(s_sg, 3)
                with act.Fori(0, DT // 2) as b:
                    for v, e, n, tc in units():
                        N = SPANS[tc][1]
                        act.wait_ge(s_mm, b * UN + v + 1)
                        act.wait_ge(s_pr, b * UN + v + 1)
                        nc.scalar.activation(sg[tc][:, :N], p_g[tc][:, :N], ACT.Sigmoid).then_inc(s_sg, 1)

            @block.vector
            def _(dve):
                dve.sem_inc(s_pr, 3)
                with dve.Fori(0, DT // 2) as b:
                    for v, e, n, tc in units():
                        t0, N = SPANS[tc]
                        dve.wait_ge(s_sg, b * UN + v + 4)
                        to = acc if n == 0 else part
                        nc.vector.tensor_tensor(out=to[tc][:, :N], in0=sg[tc][:, :N], in1=p_b[tc][:, :N],
                                                op=ALU.mult).then_inc(s_pr, 1)
                        dve.wait_ge(s_pr, b * UN + v + 4)
                        if n:
                            out = acc[tc][:, :N]
                            if n == BRANCHES - 1:
                                out = mixT[:, bass.ds(b * 2 + e, 1), t0:t0 + N].squeeze(1)
                            nc.vector.tensor_tensor(out=out, in0=acc[tc][:, :N], in1=part[tc][:, :N], op=ALU.add)\
                                .then_inc(s_part, 1)
                            dve.wait_ge(s_part, (b * 2 + e) * 6 + (n - 1) * 3 + tc + 1)
        m.retire()


def output_projection(nc, c, x_all, w_out, mixT, x1):
    with ExitStack() as ctx:
        m = Scope(nc, ctx, "out")
        w = m.sb("w", [128, DT, D])
        mt = [m.sb(f"mt{k}", [128, DT, 128]) for k in range(2)]
        x = [m.sb(f"x{k}", [128, D]) for k in range(2)]
        y = [m.sb(f"y{k}", [128, D]) for k in range(2)]
        p_o = [m.pb(f"p_o{k}", [128, D]) for k in range(2)]
        s_mt, s_mm, s_y, s_yfree, s_step = (m.sem(n) for n in ("s_mt", "s_mm", "s_y", "s_yfree", "s_step"))
        s_w = [m.sem(f"s_w{k}") for k in range(2)]
        s_x = [m.sem(f"s_x{k}") for k in range(2)]
        s_put = [m.sem(f"s_put{k}") for k in range(2)]

        with nc.Block() as block:
            @block.sync
            def _(sp):
                def load(k, t, T):
                    sp.dma_start(x[k][:T, :], x_all[rows(t, T), :]).then_inc(s_x[k], 16)

                def store(k, t, T):
                    sp.wait_ge(s_y, t + 1)
                    sp.dma_start(x1[rows(t, T), :], y[k][:T, :]).then_inc(s_put[k], 16)

                for n in range(2):
                    cols = slice(n * 512, (n + 1) * 512)
                    sp.dma_start(w[:, :, cols], w_out[:, cols].rearrange("(a p) n -> p a n", p=128))\
                        .then_inc(s_w[n], 16)
                    load(n, n, 128)
                with sp.Fori(0, TILES // 2 - 1) as b:
                    for k in range(2):
                        store(k, b * 2 + k, 128)
                        load(k, b * 2 + k + 2, 128)
                store(0, TILES - 2, 128)
                load(0, TILES, SAMPLE_T)
                store(1, TILES - 1, 128)
                store(0, TILES, SAMPLE_T)
                sp.wait_ge(s_put[0], 16 * (TILES // 2 + 1) + 16)
                sp.wait_ge(s_put[1], 16 * (TILES // 2) + 16)

            @block.scalar
            def _(act):
                for k in range(2):
                    act.sem_inc(s_put[k], 16)
                act.sem_inc(s_mm, 2)

                def take(k, t, T):
                    act.wait_ge(s_mm, t + 1)
                    nc.scalar.copy(mt[k][:, :, :T], mixT[:, :, bass.ds(t * 128, T)]).then_inc(s_mt, 1)

                with act.Fori(0, TILES // 2) as b:
                    for k in range(2):
                        take(k, b * 2 + k, 128)
                take(0, TILES, SAMPLE_T)

            @block.tensor
            def _(pe):
                def product(k, t, T):
                    pe.wait_ge(s_mt, t + 1)
                    pe.wait_ge(s_yfree, t + 1)
                    pe.sem_inc(s_step, 1)
                    for n in range(2):
                        pe.wait_ge(s_w[n], 16)
                        for dt in range(DT):
                            mm = nc.tensor.matmul(p_o[k][:T, n * 512:(n + 1) * 512], mt[k][:, dt, :T],
                                                  w[:, dt, n * 512:(n + 1) * 512], start=dt == 0, stop=dt == DT - 1)
                    mm.then_inc(s_mm, 1)

                with pe.Fori(0, TILES // 2) as b:
                    for k in range(2):
                        product(k, b * 2 + k, 128)
                product(0, TILES, SAMPLE_T)

            @block.vector
            def _(dve):
                dve.sem_inc(s_yfree, 2)

                def add(k, t, T):
                    dve.wait_ge(s_mm, t + 3)
                    dve.wait_ge(s_x[k], (t - k) * 8 + 16)
                    dve.wait_ge(s_put[k], (t - k) * 8 + 16)
                    nc.vector.tensor_tensor(out=y[k][:T, :], in0=p_o[k][:T, :], in1=x[k][:T, :], op=ALU.add)\
                        .then_inc(s_y, 1)
                    dve.wait_ge(s_y, t + 1)
                    dve.sem_inc(s_yfree, 1)

                with dve.Fori(0, TILES // 2) as b:
                    for k in range(2):
                        add(k, b * 2 + k, 128)
                add(0, TILES, SAMPLE_T)
        m.retire()


def peer(nc, c, x1, g_ffn, w_qT, sub_kT, uv, y):
    HEADS, TOPK, NK = 8, 16, 128
    SLOTS = 16
    RING = 8
    GROUP = 2
    NG = SLOTS // GROUP
    NEG = -3.0e38
    WQ_BUFS = 4
    HALF = SLOTS // 2
    NGH = HALF // GROUP

    def groups(tile, r, q):
        if isinstance(tile, int) and tile == TILES:
            return r * NGH + (TILES * HEADS * NG + q)
        return (tile * HEADS + r) * NG + q

    ctx = ExitStack()
    with ctx:
        m = Scope(nc, ctx, "peer")
        sb, pb, sem = m.sb, m.pb, m.sem
        ident, iota16, eps_col = c.ident, c.iota16, c.eps

        gf_bc = sb("gf_bc", [128, D])
        skT = sb("skT", [128, 16, NK])
        wq_buf = [sb(f"wq_buf{j}", [128, D]) for j in range(WQ_BUFS)]
        route_w = sb("route_w", [128, DT, 16 * NK])
        x_tile = sb("x_tile", [128, D])
        x_res = sb("x_res", [128, D])
        h_next = sb("h_next", [128, D])
        h_cur = sb("h_cur", [128, D])
        hT = sb("hT", [128, DT, 128])
        junk_a = sb("junk_a", [128, D])
        stat = sb("stat", [128, 4])
        sc = sb("sc", [128, 256])
        sc_rep = sb("sc_rep", [128, 256])
        v16 = sb("v16", [128, 2, TOPK])
        i16 = sb("i16", [128, 2, TOPK], U32)
        i16f = sb("i16f", [128, 2, TOPK])
        cand = sb("cand", [128, TOPK * TOPK])
        cand_rep = sb("cand_rep", [128, TOPK * TOPK])
        top = sb("top", [128, TOPK])
        pos = sb("pos", [128, TOPK], U32)
        posab = sb("posab", [128, 2, TOPK], U32)
        posabf = sb("posabf", [128, 2, TOPK])
        onehot = sb("onehot", [128, 2, TOPK, TOPK])
        isel = sb("isel", [128, 2, TOPK])
        smx = sb("smx", [128, 4])
        ex = sb("ex", [128, TOPK])
        idx_all = sb("idx_all", [128, HEADS * TOPK], U32)
        g_all = sb("g_all", [128, HEADS * TOPK])
        idx_now = sb("idx_now", [128, SLOTS], U32)
        g_now = sb("g_now", [128, SLOTS])
        dots = sb("dots", [128, SLOTS])
        gel = sb("gel", [128, SLOTS])
        wgt = sb("wgt", [128, SLOTS])
        diag = sb("diag", [128, RING, 128])
        fold = sb("fold", [128, SAMPLE_T])
        ring = sb("ring", [128, RING, 2 * D])
        ysb = sb("ysb", [128, D])

        p_y = pb("p_y", [128, D])
        p_s = pb("p_s", [128, 512])
        p_t = pb("p_t", [128, D])

        s_gf = sem("s_gf")
        s_sk = sem("s_sk")
        s_wq = [sem(f"s_wq{j}") for j in range(WQ_BUFS)]
        s_rw_mm = [sem(f"s_rw_mm{k}") for k in range(2)]
        s_rw = [sem(f"s_rw{k}") for k in range(2)]
        s_x = sem("s_x")
        s_xres = sem("s_xres")
        s_sq = sem("s_sq")
        s_std = sem("s_std")
        s_h = sem("s_h")
        s_rstd = sem("s_rstd")
        s_hcur = sem("s_hcur")
        s_fold = sem("s_fold")
        s_tr = sem("s_tr")
        s_hT = sem("s_hT")
        s_res = sem("s_res")
        s_scores = sem("s_scores")
        s_sc = sem("s_sc")
        s_sfree = sem("s_sfree")
        s_top = sem("s_top")
        s_ex = sem("s_ex")
        s_idx = sem("s_idx")
        s_idxcp = sem("s_idxcp")
        s_gcp = sem("s_gcp")
        s_slot = [sem(f"s_slot{j}") for j in range(RING)]
        s_dot = sem("s_dot")
        s_diag = sem("s_diag")
        s_vdone = sem("s_vdone")
        s_yev = sem("s_yev")
        s_out = sem("s_out")
        s_dch = sem("s_dch")
        s_ach = sem("s_ach")
        s_step = {e: sem(f"s_step_{k}") for k, e in (("dve", nc.vector), ("pe", nc.tensor), ("pool", nc.gpsimd))}

        block = ctx.enter_context(nc.Block())

        def apart(eng):
            eng.sem_inc(s_step[eng], 1)

        @block.sync
        def _(sp):
            def load_x(tile, T):
                if not (isinstance(tile, int) and tile == 0):
                    sp.wait_ge(s_h, tile)
                sp.dma_start(x_tile[:T, :], x1[rows(tile, T), :]).then_inc(s_x, 16)

            def load_res(tile, T):
                if not (isinstance(tile, int) and tile == 0):
                    sp.wait_ge(s_res, tile)
                sp.dma_start(x_res[:T, :], x1[rows(tile, T), :]).then_inc(s_xres, 16)

            def store_y(tile, T):
                sp.wait_ge(s_yev, tile + 2)
                sp.dma_start(y[rows(tile, T), :], ysb[:T, :]).then_inc(s_out, 16)

            load_x(0, 128)
            sp.dma_start(gf_bc[:, :], g_ffn[0:1, :].broadcast_to([128, D])).then_inc(s_gf, 16)
            sp.dma_start(skT[:, :, :], sub_kT.rearrange("h c k -> c h k")).then_inc(s_sk, 16)
            for j in range(WQ_BUFS):
                sp.dma_start(wq_buf[j][:, :], w_qT[j * 128:(j + 1) * 128, :]).then_inc(s_wq[j], 16)
            with sp.Fori(1, 2 * HEADS // WQ_BUFS) as round_:
                for j in range(WQ_BUFS):
                    sp.wait_ge(s_rw_mm[j % 2], (WQ_BUFS // 2) * (round_ - 1) + j // 2 + 1)
                    sp.dma_start(wq_buf[j][:, :], w_qT[bass.ds((round_ * WQ_BUFS + j) * 128, 128), :])\
                        .then_inc(s_wq[j], 16)
            load_res(0, 128)
            load_x(1, 128)
            load_res(1, 128)
            with sp.Fori(0, TILES - 2) as i:
                load_x(i + 2, 128)
                store_y(i, 128)
                load_res(i + 2, 128)
            load_x(TILES, SAMPLE_T)
            store_y(TILES - 2, 128)
            load_res(TILES, SAMPLE_T)
            store_y(TILES - 1, 128)
            store_y(TILES, SAMPLE_T)
            sp.wait_ge(s_out, 16 * (TILES + 2))

        @block.gpsimd
        def _(pool):
            def gather_head(tile, r, T):
                n = tile * HEADS + r
                pool.wait_ge(s_idx, n + 1)
                for half in range(2):
                    c = half * RING
                    pool.tensor_copy(idx_now[:T, c:c + RING],
                                     idx_all[:T, bass.ds(r * TOPK + c, RING)]).then_inc(s_idxcp, 1)
                    pool.wait_ge(s_idxcp, 2 * n + half + 1)
                    for j in range(RING):
                        if j % GROUP == 0:
                            k = n * NG + half * (RING // GROUP) + j // GROUP - RING // GROUP + 1
                            first = isinstance(n, int) and k <= 0
                            if not first:
                                pool.wait_ge(s_vdone, k)
                                apart(pool)
                        nc.gpsimd.indirect_dma_start(
                            out=ring[:T, j, :], out_offset=None, in_=uv[:, :],
                            in_offset=bass.IndirectOffsetOnAxis(ap=idx_now[:T, c + j:c + j + 1], axis=0)
                        ).then_inc(s_slot[j], 16)

            def gather_sample_head(r, c):
                n = TILES * HEADS + r
                pool.wait_ge(s_idx, n + 1)
                for half in range(2):
                    pool.tensor_copy(idx_now[half * SAMPLE_T:(half + 1) * SAMPLE_T, c:c + HALF],
                                     idx_all[:SAMPLE_T, bass.ds(r * TOPK + half * HALF, HALF)]).then_inc(s_idxcp, 1)
                pool.wait_ge(s_idxcp, 2 * n + 2)
                for j in range(HALF):
                    if j % GROUP == 0:
                        pool.wait_ge(s_vdone, groups(TILES, r, j // GROUP - RING // GROUP + 1))
                        apart(pool)
                    nc.gpsimd.indirect_dma_start(
                        out=ring[:, j, :], out_offset=None, in_=uv[:, :],
                        in_offset=bass.IndirectOffsetOnAxis(ap=idx_now[:, c + j:c + j + 1], axis=0)
                    ).then_inc(s_slot[j], 16)

            gather_head(0, 0, 128)
            with pool.Fori(1, HEADS) as r:
                gather_head(0, r, 128)
            with pool.Fori(1, TILES) as i:
                with pool.Fori(0, HEADS) as r:
                    gather_head(i, r, 128)
            with pool.Fori(0, HEADS // 2) as pair:
                for odd in range(2):
                    gather_sample_head(pair * 2 + odd, odd * HALF)

        @block.tensor
        def _(pe):
            def make_route_weights():
                pe.wait_ge(s_sk, 16)
                with pe.Fori(0, 2 * HEADS // WQ_BUFS) as round_:
                    for j in range(WQ_BUFS):
                        pe.wait_ge(s_wq[j], (round_ + 1) * 16)
                        pe.wait_ge(s_rw[j % 2], (WQ_BUFS // 2) * round_ + j // 2 + 1)
                        for dt in range(DT):
                            mm = nc.tensor.matmul((p_t, p_y)[j % 2][:, dt * 128:(dt + 1) * 128],
                                                  wq_buf[j][:, dt * 128:(dt + 1) * 128],
                                                  skT[:, bass.ds(round_ * WQ_BUFS + j, 1), :].squeeze(1),
                                                  start=True, stop=True)
                        mm.then_inc(s_rw_mm[j % 2], 1)
                for k in range(2):
                    pe.wait_ge(s_rw[k], HEADS + 1)

            def prep(tile, T):
                pe.wait_ge(s_h, tile + 1)
                if not (isinstance(tile, int) and tile == 0):
                    pe.wait_ge(s_hT, tile)
                    apart(pe)
                for dt in range(DT):
                    mm = nc.tensor.transpose(p_t[:, dt * 128:dt * 128 + T], h_next[:T, dt * 128:(dt + 1) * 128],
                                             ident[:T, :T])
                mm.then_inc(s_tr, 1)
                pe.wait_ge(s_hT, tile + 1)
                apart(pe)

            def scores(n, r, T):
                pe.wait_ge(s_sc, n + 1)
                apart(pe)
                for dt in range(DT):
                    mm = nc.tensor.matmul(p_s[:T, 0:256], hT[:, dt, :T], route_w[:, dt, bass.ds(r * 256, 256)],
                                          start=dt == 0, stop=dt == DT - 1)
                mm.then_inc(s_scores, 1)

            def residual(tile, T):
                pe.wait_ge(s_yev, tile + 1)
                pe.wait_ge(s_xres, 16 * (tile + 1))
                apart(pe)
                for c in range(2):
                    mm = nc.tensor.matmul(p_y[:T, c * 512:(c + 1) * 512], ident[:T, :T],
                                          x_res[:T, c * 512:(c + 1) * 512], start=True, stop=True)
                mm.then_inc(s_res, 1)

            def values(tile, r, T, q):
                P = 128 if T == SAMPLE_T else T
                pe.wait_ge(s_diag, groups(tile, r, q) + 1)
                apart(pe)
                for k in range(GROUP):
                    j = (q * GROUP + k) % RING
                    for c in range(2):
                        mm = nc.tensor.matmul(p_y[:T, c * 512:(c + 1) * 512], diag[:P, j, :T],
                                              ring[:P, j, D + c * 512:D + (c + 1) * 512],
                                              start=False, stop=True, skip_group_check=True)
                mm.then_inc(s_vdone, 1)

            def values_and_scores(tile, r, T, next_head, T_next):
                scores(tile * HEADS + r + 1, next_head, T_next)
                for q in range(NGH if T == SAMPLE_T else NG):
                    values(tile, r, T, q)

            def heads(tile, T, T_next):
                with pe.Fori(0, HEADS - 1) as r:
                    values_and_scores(tile, r, T, r + 1, T)
                prep(tile + 1, T_next)
                values_and_scores(tile, HEADS - 1, T, 0, T_next)
                residual(tile + 1, T_next)

            prep(0, 128)
            make_route_weights()
            scores(0, 0, 128)
            residual(0, 128)
            heads(0, 128, 128)
            with pe.Fori(1, TILES - 1) as i:
                heads(i, 128, 128)
            heads(TILES - 1, 128, SAMPLE_T)
            with pe.Fori(0, HEADS - 1) as r:
                values_and_scores(TILES, r, SAMPLE_T, r + 1, SAMPLE_T)
            for q in range(NGH):
                values(TILES, HEADS - 1, SAMPLE_T, q)

        @block.scalar
        def _(act):
            act.sem_inc(s_rw[0], 1)
            act.sem_inc(s_sc, 1)
            act.sem_inc(s_out, 16)
            def stats(tile, T):
                act.wait_ge(s_x, 16 * (tile + 1))
                nc.scalar.activation(junk_a[:T, :], x_tile[:T, :], ACT.Square,
                                     accum_out=stat[:T, 0:1]).then_inc(s_sq, 1)
                act.wait_ge(s_sq, tile + 1)
                nc.scalar.activation(stat[:T, 1:2], stat[:T, 0:1], ACT.Sqrt, bias=eps_col[:T, :],
                                     scale=1.0 / D).then_inc(s_std, 1)

            def take_hT(tile, T):
                act.wait_ge(s_tr, tile + 1)
                nc.scalar.copy(hT[:, :, :T],
                               p_t[:, :].rearrange("p (a b) -> p a b", b=128)[:, :, :T]).then_inc(s_hT, 1)

            def route(n, T):
                act.wait_ge(s_scores, n + 1)
                act.wait_ge(s_sfree, n + 1)
                nc.scalar.copy(sc[:T, :], p_s[:T, 0:256]).then_inc(s_sc, 1)

            def soften(n, T):
                act.wait_ge(s_top, n + 1)
                nc.scalar.activation(ex[:T, :], top[:T, :], ACT.Exp, bias=smx[:T, 0:1],
                                     accum_out=smx[:T, 1:2]).then_inc(s_ex, 1)

            def weigh(tile, r, T, q):
                n = groups(tile, r, q)
                c = q * GROUP
                P, unit = (128, fold) if T == SAMPLE_T else (T, ident)
                act.wait_ge(s_dot, n + 1)
                nc.scalar.activation(gel[:P, c:c + GROUP], dots[:P, c:c + GROUP], ACT.Gelu).then_inc(s_ach, 1)
                act.wait_ge(s_ach, n * 2 + 1)
                for k in range(GROUP):
                    last = nc.scalar.mul(wgt[:P, c + k:c + k + 1], gel[:P, c + k:c + k + 1],
                                         g_now[:P, c + k:c + k + 1])
                last.then_inc(s_ach, 1)
                act.wait_ge(s_ach, n * 2 + 2)
                for k in range(GROUP):
                    last = nc.scalar.mul(diag[:P, (c + k) % RING, :T], unit[:P, :T], wgt[:P, c + k:c + k + 1])
                last.then_inc(s_diag, 1)

            def take_g(tile, r, T):
                n = tile * HEADS + r
                act.wait_ge(s_idx, n + 1)
                if T == SAMPLE_T:
                    for half in range(2):
                        last = nc.scalar.copy(g_now[half * SAMPLE_T:(half + 1) * SAMPLE_T, 0:HALF],
                                              g_all[:T, bass.ds(r * TOPK + half * HALF, HALF)])
                else:
                    last = nc.scalar.copy(g_now[:T, :], g_all[:T, bass.ds(r * TOPK, TOPK)])
                last.then_inc(s_gcp, 1)
                act.wait_ge(s_gcp, n + 1)

            def finish(tile, T):
                act.wait_ge(s_vdone, groups(tile, HEADS - 1, (NGH if T == SAMPLE_T else NG)))
                act.wait_ge(s_out, 16 * tile + 16)
                nc.scalar.copy(ysb[:T, :], p_y[:T, :]).then_inc(s_yev, 1)

            def weigh_and_route(tile, r, T, T_next):
                n_next = tile * HEADS + r + 1
                route(n_next, T_next)
                take_g(tile, r, T)
                weigh(tile, r, T, 0)
                weigh(tile, r, T, 1)
                soften(n_next, T_next)
                for q in range(2, NGH if T == SAMPLE_T else NG):
                    weigh(tile, r, T, q)

            def heads(tile, T, T_next):
                with act.Fori(0, HEADS - 1) as r:
                    weigh_and_route(tile, r, T, T)
                stats(tile + 1, T_next)
                take_hT(tile + 1, T_next)
                weigh_and_route(tile, HEADS - 1, T, T_next)
                finish(tile, T)

            act.wait_ge(s_fold, 1)
            stats(0, 128)
            take_hT(0, 128)
            with act.Fori(0, HEADS) as h:
                act.wait_ge(s_rw_mm[0], h + 1)
                nc.scalar.copy(route_w[:, :, bass.ds(h * 2 * NK, NK)],
                               p_t[:, :].rearrange("p (a b) -> p a b", b=NK)).then_inc(s_rw[0], 1)
            route(0, 128)
            soften(0, 128)
            heads(0, 128, 128)
            with act.Fori(1, TILES - 1) as i:
                heads(i, 128, 128)
            heads(TILES - 1, 128, SAMPLE_T)
            with act.Fori(0, HEADS - 1) as r:
                weigh_and_route(TILES, r, SAMPLE_T, SAMPLE_T)
            take_g(TILES, HEADS - 1, SAMPLE_T)
            for q in range(NGH):
                weigh(TILES, HEADS - 1, SAMPLE_T, q)
            finish(TILES, SAMPLE_T)

        @block.vector
        def _(dve):
            dve.sem_inc(s_sfree, 1)
            dve.sem_inc(s_yev, 1)
            dve.sem_inc(s_rw[1], 1)
            dve.wait_ge(s_gf, 16)

            def prep(tile, T):
                dve.wait_ge(s_std, tile + 1)
                if not (isinstance(tile, int) and tile == 0):
                    dve.wait_ge(s_tr, tile)
                nc.vector.reciprocal(stat[:T, 2:3], stat[:T, 1:2]).then_inc(s_rstd, 1)
                dve.wait_ge(s_rstd, tile + 1)
                nc.vector.scalar_tensor_tensor(out=h_next[:T, :], in0=x_tile[:T, :], scalar=stat[:T, 2:3],
                                               in1=gf_bc[:T, :], op0=ALU.mult, op1=ALU.mult).then_inc(s_h, 1)

            def linked(ins, k):
                ins.then_inc(s_dch, 1)
                dve.wait_ge(s_dch, k)

            def best_of_side(n, T, p):
                if p == 0:
                    dve.wait_ge(s_sc, n + 2)
                    apart(dve)
                    dve.sem_clear(s_dch)
                s, rep = sc[:T, p * NK:(p + 1) * NK], sc_rep[:T, p * NK:(p + 1) * NK]
                lo, hi = v16[:T, p, 0:8], v16[:T, p, 8:16]
                linked(nc.vector.max(lo, s), 4 * p + 1)
                nc.vector.max_index(i16[:T, p, 0:8], lo, s)
                linked(nc.vector.match_replace(rep, lo, s, NEG), 4 * p + 2)
                linked(nc.vector.max(hi, rep), 4 * p + 3)
                linked(nc.vector.max_index(i16[:T, p, 8:16], hi, rep), 4 * p + 4)

            def best_sums_first(n, T):
                nc.vector.tensor_copy(i16f[:T, :, :], i16[:T, :, :])
                nc.vector.tensor_tensor(
                    out=cand[:T, :].rearrange("p (a b) -> p a b", b=TOPK),
                    in0=v16[:T, 0, :].unsqueeze(2).broadcast_to([T, TOPK, TOPK]),
                    in1=v16[:T, 1, :].unsqueeze(1).broadcast_to([T, TOPK, TOPK]), op=ALU.add).then_inc(s_sfree, 1)
                dve.wait_ge(s_sfree, n + 2)
                apart(dve)
                linked(nc.vector.max(top[:T, 0:8], cand[:T, :]), 9)
                nc.vector.tensor_scalar(out=smx[:T, 0:1], in0=top[:T, 0:1], scalar1=-1.0, scalar2=None, op0=ALU.mult)
                nc.vector.max_index(pos[:T, 0:8], top[:T, 0:8], cand[:T, :])
                linked(nc.vector.match_replace(cand_rep[:T, :], top[:T, 0:8], cand[:T, :], NEG), 10)

            def best_sums_second(n, T):
                nc.vector.max(top[:T, 8:16], cand_rep[:T, :]).then_inc(s_top, 1)
                dve.wait_ge(s_top, n + 1)
                apart(dve)
                linked(nc.vector.max_index(pos[:T, 8:16], top[:T, 8:16], cand_rep[:T, :]), 11)
                nc.vector.tensor_single_scalar(posab[:T, 0, :], pos[:T, :], 4, ALU.logical_shift_right)
                linked(nc.vector.tensor_single_scalar(posab[:T, 1, :], pos[:T, :], 15, ALU.bitwise_and), 12)
                linked(nc.vector.tensor_copy(posabf[:T, :, :], posab[:T, :, :]), 13)

            def expert_numbers(T):
                oh = onehot[:T, :, :, :].rearrange("p s k a -> p (s k) a")
                linked(nc.vector.tensor_tensor(
                    out=oh, in0=iota16[:T, :].unsqueeze(1).broadcast_to([T, 32, 16]),
                    in1=posabf[:T, :, :].rearrange("p s k -> p (s k)").unsqueeze(2).broadcast_to([T, 32, 16]),
                    op=ALU.is_equal), 14)
                linked(nc.vector.tensor_tensor(
                    out=onehot[:T, :, :, :], in0=onehot[:T, :, :, :],
                    in1=i16f[:T, :, :].unsqueeze(2).broadcast_to([T, 2, TOPK, TOPK]), op=ALU.mult), 15)
                linked(nc.vector.tensor_reduce(out=isel[:T, :, :].rearrange("p s k -> p (s k)"), in_=oh,
                                               axis=AX.X, op=ALU.add), 16)

            def softmax_weights(n, r, T):
                if not (isinstance(n, int) and n == 0):
                    dve.wait_ge(s_idxcp, 2 * n)
                    dve.wait_ge(s_gcp, n)
                nc.vector.scalar_tensor_tensor(out=idx_all[:T, bass.ds(r * TOPK, TOPK)], in0=isel[:T, 0, :],
                                               scalar=float(NK), in1=isel[:T, 1, :], op0=ALU.mult, op1=ALU.add)
                dve.wait_ge(s_ex, n + 1)
                linked(nc.vector.reciprocal(smx[:T, 2:3], smx[:T, 1:2]), 17)
                nc.vector.tensor_scalar(out=g_all[:T, bass.ds(r * TOPK, TOPK)], in0=ex[:T, :],
                                        scalar1=smx[:T, 2:3], scalar2=None, op0=ALU.mult).then_inc(s_idx, 1)

            def dot(tile, r, T, q):
                P = 128 if T == SAMPLE_T else T
                for k in range(GROUP):
                    c = q * GROUP + k
                    if T == SAMPLE_T:
                        dve.wait_ge(s_slot[c], r * 16 + (32 * TILES * HEADS + 16))
                    else:
                        dve.wait_ge(s_slot[c % RING], 32 * (tile * HEADS + r) + 16 * (c // RING + 1))
                    last = nc.vector.tensor_tensor_reduce(
                        out=ring[:P, c % RING, 0:D], in0=ring[:P, c % RING, 0:D], in1=h_cur[:P, :], scale=1.0,
                        scalar=0.0, op0=ALU.mult, op1=ALU.add, accum_out=dots[:P, c:c + 1])
                last.then_inc(s_dot, 1)

            def dot_and_pick(tile, r, T, next_head, T_next):
                n_next = tile * HEADS + r + 1
                dot(tile, r, T, 0)
                best_of_side(n_next, T_next, 0)
                best_of_side(n_next, T_next, 1)
                dot(tile, r, T, 1)
                best_sums_first(n_next, T_next)
                best_sums_second(n_next, T_next)
                dot(tile, r, T, 2)
                expert_numbers(T_next)
                softmax_weights(n_next, next_head, T_next)
                for q in range(3, NGH if T == SAMPLE_T else NG):
                    dot(tile, r, T, q)

            def keep_h(tile, T):
                if not (isinstance(tile, int) and tile == 0):
                    dve.wait_ge(s_dot, tile * HEADS * NG)
                dve.wait_ge(s_h, tile + 1)
                if T == SAMPLE_T:
                    nc.vector.tensor_copy(h_cur[T:2 * T, :], h_next[:T, :])
                nc.vector.tensor_copy(h_cur[:T, :], h_next[:T, :]).then_inc(s_hcur, 1)
                dve.wait_ge(s_hcur, tile + 1)

            def heads(tile, T, T_next):
                with dve.Fori(0, HEADS - 1) as r:
                    dot_and_pick(tile, r, T, r + 1, T)
                prep(tile + 1, T_next)
                dot_and_pick(tile, HEADS - 1, T, 0, T_next)
                keep_h(tile + 1, T_next)

            nc.vector.tensor_tensor(out=fold[:, :], in0=ident[:, 0:SAMPLE_T], in1=ident[:, SAMPLE_T:2 * SAMPLE_T],
                                    op=ALU.add).then_inc(s_fold, 1)
            prep(0, 128)
            with dve.Fori(0, HEADS) as h:
                dve.wait_ge(s_rw_mm[1], h + 1)
                nc.vector.tensor_copy(route_w[:, :, bass.ds(h * 2 * NK + NK, NK)],
                                      p_y[:, :].rearrange("p (a b) -> p a b", b=NK)).then_inc(s_rw[1], 1)
            best_of_side(0, 128, 0)
            best_of_side(0, 128, 1)
            best_sums_first(0, 128)
            best_sums_second(0, 128)
            expert_numbers(128)
            softmax_weights(0, 0, 128)
            keep_h(0, 128)
            heads(0, 128, 128)
            with dve.Fori(1, TILES - 1) as i:
                heads(i, 128, 128)
            heads(TILES - 1, 128, SAMPLE_T)
            with dve.Fori(0, HEADS - 1) as r:
                dot_and_pick(TILES, r, SAMPLE_T, r + 1, SAMPLE_T)
            for q in range(NGH):
                dot(TILES, HEADS - 1, SAMPLE_T, q)


def program(nc, t, out):
    with ExitStack() as ctx:
        c = Scope(nc, ctx, "c")
        c.ident, c.ones, c.upto, c.upto_chunk, c.after_chunk = (
            c.sb(n, [128, 128]) for n in ("ident", "ones", "upto", "upto_chunk", "after_chunk"))
        c.chunk_of = c.sb("chunk_of", [128, 2])
        c.eps, c.one = c.sb("eps", [128, 1]), c.sb("one", [128, 1])
        c.iota16 = c.sb("iota16", [128, 16])
        proj = nc.dram_tensor("proj", (TOKENS, P_COLS), F32, kind="Internal").ap()
        hT_spill = nc.dram_tensor("hT_spill", (128, DT * TOKENS), F32, kind="Internal").ap()
        oT_spill = nc.dram_tensor("oT_spill", (BRANCHES, 128, 4, TOKENS), F32, kind="Internal").ap()
        x1 = nc.dram_tensor("x1", (TOKENS, D), F32, kind="Internal").ap()

        constants(nc, c)
        input_projection(nc, c, t["x_all"], t["g_attn"], t["w_in1"], proj, hT_spill)
        memory_projection(nc, c, t["mem"], t["mem_g_in"], t["w_kv"], t["mem_g_k"], out["mem_k"], out["mem_v"])
        mixers(nc, c, proj,
               [t[k] for k in ("gla_w_a2", "gla_b_a", "gla_g_out", "fox_b_f", "fox_g_q", "fox_g_k", "mem_g_q")],
               [t[k] for k in ("fox_k", "fox_v", "fox_logf", "state_gla", "cache_mem_k", "cache_mem_v")],
               out["mem_k"], out["mem_v"],
               [out[k] for k in ("k_p", "v_p", "lf_p", "st_p", "k_s", "v_s", "lf_s", "st_s")], oT_spill)
        with ExitStack() as inner:
            mixT = inner.enter_context(nc.sbuf_tensor("mixT", [128, DT, TOKENS], F32))
            gated_mix(nc, c, hT_spill, oT_spill, t["w_gate"], t["w_br"], mixT)
            output_projection(nc, c, t["x_all"], t["w_out"], mixT, x1)
        peer(nc, c, x1, t["g_ffn"], t["w_qT"], t["sub_kT"], t["uv"], out["y"])


def kernel(x_prompt, x_sample, mem_prompt, cache_fox_k, cache_fox_v, cache_fox_logf, state_gla,
           cache_mem_k, cache_mem_v, g_attn, w_in, gla_w_a2, gla_b_a, gla_g_out, fox_b_f, fox_g_q, fox_g_k,
           mem_g_q, mem_g_in, mem_w_kv, mem_g_k, w_branch, w_out, g_ffn, peer_w_q, peer_sub_keys, peer_u, peer_v):
    import numpy as np
    import concourse.bacc as bacc
    from concourse.bass_utils import run_bass_kernel_spmd

    a = np.asarray
    w = a(w_in)[0]
    laid = {
        "x_all": np.concatenate([a(x_prompt)[0], a(x_sample)[0]], axis=0),
        "mem": a(mem_prompt)[0],
        "fox_k": a(cache_fox_k)[0, 0].reshape(PAST, BW),
        "fox_v": a(cache_fox_v)[0, 0].reshape(PAST, BW),
        "fox_logf": a(cache_fox_logf)[0, 0],
        "state_gla": a(state_gla)[0, 0],
        "cache_mem_k": a(cache_mem_k)[0, 0].reshape(NMEM, BW),
        "cache_mem_v": a(cache_mem_v)[0, 0].reshape(NMEM, BW),
        "g_attn": a(g_attn), "gla_w_a2": a(gla_w_a2), "gla_b_a": a(gla_b_a), "gla_g_out": a(gla_g_out),
        "fox_b_f": a(fox_b_f), "fox_g_q": a(fox_g_q), "fox_g_k": a(fox_g_k), "mem_g_q": a(mem_g_q),
        "mem_g_in": a(mem_g_in), "w_kv": a(mem_w_kv)[0], "mem_g_k": a(mem_g_k),
        "w_in1": w[:, :P_COLS].reshape(DT, 128, P_CHUNKS, PW).transpose(2, 1, 0, 3).reshape(P_CHUNKS, 128, DT * PW),
        "w_gate": w[:, P_COLS:].reshape(DT, 128, BRANCHES, DT, 128).transpose(3, 1, 2, 0, 4)
                   .reshape(DT, 128, BRANCHES * DT * 128),
        "w_br": a(w_branch)[0].reshape(BRANCHES, 4, 128, DT, 128).transpose(3, 2, 0, 1, 4)
                 .reshape(DT, 128, BRANCHES * 4 * 128),
        "w_out": a(w_out)[0], "g_ffn": a(g_ffn),
        "w_qT": a(peer_w_q)[0].T,
        "sub_kT": a(peer_sub_keys)[0].reshape(16, 128, 128).transpose(0, 2, 1),
        "uv": np.concatenate([a(peer_u)[0], a(peer_v)[0]], axis=1),
    }
    shapes = {"y": (TOKENS, D), "k_p": (SEQ, BW), "v_p": (SEQ, BW), "lf_p": (SEQ, FH), "st_p": (GH, GDK, GDV),
              "mem_k": (NMEM, BW), "mem_v": (NMEM, BW), "k_s": (SAMPLE_T, BW), "v_s": (SAMPLE_T, BW),
              "lf_s": (SAMPLE_T, FH), "st_s": (GH, GDK, GDV)}
    nc = bacc.Bacc("TRN2", target_bir_lowering=False, num_devices=1)
    laid = {k: np.ascontiguousarray(v) for k, v in laid.items()}
    t = {k: nc.dram_tensor(f"in_{k}", v.shape, F32, kind="ExternalInput").ap() for k, v in laid.items()}
    out = {k: nc.dram_tensor(f"out_{k}", v, F32, kind="ExternalOutput").ap() for k, v in shapes.items()}
    program(nc, t, out)
    r = run_bass_kernel_spmd(nc, [{f"in_{k}": v for k, v in laid.items()}], core_ids=[0]).results[0]
    o = {k: a(r[f"out_{k}"]) for k in shapes}
    return (o["y"][:SEQ].reshape(1, SEQ, D), o["y"][SEQ:].reshape(1, SAMPLE_T, D),
            o["k_p"].reshape(1, 1, SEQ, FH, FD), o["v_p"].reshape(1, 1, SEQ, FH, FD), o["lf_p"].reshape(1, 1, SEQ, FH),
            o["st_p"].reshape(1, 1, GH, GDK, GDV), o["mem_k"].reshape(1, 1, NMEM, MH, MD),
            o["mem_v"].reshape(1, 1, NMEM, MH, MD), o["k_s"].reshape(1, 1, SAMPLE_T, FH, FD),
            o["v_s"].reshape(1, 1, SAMPLE_T, FH, FD), o["lf_s"].reshape(1, 1, SAMPLE_T, FH),
            o["st_s"].reshape(1, 1, GH, GDK, GDV))
```
